# Optimizing a Trainium2 kernel written in Bass

```python
import math
import jax, jax.numpy as jnp
from jax import lax
import numpy as np

D_MODEL = 1024
BATCH = 1
SEQ = 1024
DEPTH = 2
DEC_BATCH = 8
DEC_SEQ = 8
PAST_LEN = 2048
PAGE_SIZE = 128

N_EVEN = (DEPTH + 1) // 2
N_ODD = DEPTH // 2
HALF_W = D_MODEL // 2
H_A = 4
DV_A = HALF_W // H_A
DK_A = DV_A // 2
RET_CHUNK = 128
RET_THETA = 10000.0
G_B = 4
DG_B = HALF_W // G_B
MLP_CHUNK = 128
H_C = 4
DK_C = 128
DV_C = HALF_W // H_C
HGRN_CHUNK = 64
HD_D = 64
HQ_D = HALF_W // HD_D
HKV_D = 2
WINDOW = 128
ROPE_THETA = 500000.0
ROT_DIM_D = HD_D // 4
N_MEM = 256
H_X = 4
HD_X = 128
D_FF = ((8 * D_MODEL // 3 + 255) // 256) * 256
CONV_W = 3
EPS = 1e-6

EVEN_SIZES = (H_A * DK_A, H_A * DK_A, H_A * DV_A, H_A * DV_A, G_B * DG_B, G_B * DG_B)
ODD_SIZES = (H_C * DK_C, H_C * DK_C, H_C * DV_C, H_C * DV_C, HQ_D * HD_D, HKV_D * HD_D, HKV_D * HD_D)
EVEN_OUT = H_A * DV_A + G_B * DG_B
ODD_OUT = H_C * DV_C + HQ_D * HD_D

kernel_name = 'hybrid_retention_gmlp_hgrn2_swa_step'

F32 = jnp.float32

def _split(t, sizes):
    idx, acc = [], 0
    for s in sizes[:-1]:
        acc += s
        idx.append(acc)
    return jnp.split(t, idx, axis=-1)

def _rms_norm(x, g):
    xf = x.astype(F32)
    y = xf * lax.rsqrt(jnp.mean(xf * xf, axis=-1, keepdims=True) + EPS)
    return (y * g).astype(x.dtype)

def _layer_norm(x, g):
    xf = x.astype(F32)
    mu = jnp.mean(xf, axis=-1, keepdims=True)
    xc = xf - mu
    y = xc * lax.rsqrt(jnp.mean(xc * xc, axis=-1, keepdims=True) + EPS)
    return (y * g).astype(x.dtype)

def _rope(x, pos, rot_dim, theta):
    half = rot_dim // 2
    inv = theta ** (-jnp.arange(half, dtype=F32) / half)
    ang = pos.astype(F32)[:, None] * inv[None, :]
    cos = jnp.cos(ang)[:, None, :]
    sin = jnp.sin(ang)[:, None, :]
    xf = x.astype(F32)
    x1 = xf[..., :half]
    x2 = xf[..., half:rot_dim]
    out = jnp.concatenate([x1 * cos - x2 * sin, x2 * cos + x1 * sin, xf[..., rot_dim:]], axis=-1)
    return out.astype(x.dtype)

def _retention(q, k, v, s0):
    B, L, H, _ = q.shape
    DV = v.shape[-1]
    c = math.gcd(L, RET_CHUNK)
    n = L // c
    lg = jnp.log1p(-jnp.exp2(-5.0 - jnp.arange(H, dtype=F32)))
    idx = jnp.arange(c, dtype=F32)
    rel = idx[:, None] - idx[None, :]
    dmask = jnp.where(rel >= 0, jnp.exp(rel[None] * lg[:, None, None]), 0.0)
    q_dec = jnp.exp((idx + 1.0)[None, :] * lg[:, None])[..., None]
    k_dec = jnp.exp((c - 1.0 - idx)[None, :] * lg[:, None])[..., None]
    c_dec = jnp.exp(c * lg)[:, None, None]

    def chunks(t):
        return t.astype(F32).reshape(B, n, c, H, t.shape[-1]).transpose(1, 0, 3, 2, 4)

    def step(S, inp):
        qc, kc, vc = inp
        a = jnp.einsum('bhnd,bhmd->bhnm', qc, kc) * dmask
        o = jnp.einsum('bhnm,bhmv->bhnv', a, vc) + jnp.einsum('bhnd,bhdv->bhnv', qc * q_dec, S)
        S = c_dec * S + jnp.einsum('bhmd,bhmv->bhdv', kc * k_dec, vc)
        return S, o

    S, o = lax.scan(step, s0.astype(F32), (chunks(q), chunks(k), chunks(v)))
    return o.transpose(1, 0, 3, 2, 4).reshape(B, L, H, DV), S

def _hgrn2(q, k, log_f, v, s0):
    B, L, H, _ = q.shape
    DV = v.shape[-1]
    c = math.gcd(L, HGRN_CHUNK)
    n = L // c
    tri = jnp.tril(jnp.ones((c, c), dtype=bool))[:, :, None]

    def chunks(t):
        return t.astype(F32).reshape(B, n, c, H, t.shape[-1]).transpose(1, 0, 3, 2, 4)

    def step(S, inp):
        qc, kc, gc, vc = inp
        b = jnp.cumsum(gc, axis=2)
        diff = jnp.where(tri, b[:, :, :, None, :] - b[:, :, None, :, :], -jnp.inf)
        a = jnp.einsum('bhnmd,bhnd->bhnm', jnp.exp(diff) * kc[:, :, None, :, :], qc)
        o = jnp.einsum('bhnm,bhmv->bhnv', a, vc) + jnp.einsum('bhnd,bhdv->bhnv', qc * jnp.exp(b), S)
        bl = b[:, :, -1:, :]
        S = jnp.exp(bl[:, :, 0, :, None]) * S + jnp.einsum('bhmd,bhmv->bhdv', kc * jnp.exp(bl - b), vc)
        return S, o

    S, o = lax.scan(step, s0.astype(F32), (chunks(q), chunks(k), chunks(log_f), chunks(v)))
    return o.transpose(1, 0, 3, 2, 4).reshape(B, L, H, DV), S

def _chunk_gate(u, v, w_s, b_s):
    B, L, G, DG = v.shape
    c = min(MLP_CHUNK, L)
    n = L // c
    w = jnp.tril(w_s[:, :c, :c])
    mixed = jnp.einsum('gts,bnsgd->bntgd', w, v.reshape(B, n, c, G, DG)) + b_s[:, :c].T[None, None, :, :, None]
    return u * mixed.reshape(B, L, G, DG)

def _sink_probs(s, mask, sink):
    s = jnp.where(mask, s, -jnp.inf)
    m = jnp.maximum(jnp.max(s, axis=-1, keepdims=True), sink)
    p = jnp.exp(s - m)
    return p / (jnp.sum(p, axis=-1, keepdims=True) + jnp.exp(sink - m))

def _swa_prompt(q, k, v, sinks):
    B, L = q.shape[:2]
    nb = L // WINDOW
    rep = HQ_D // HKV_D
    qb = q.astype(F32).reshape(B, nb, WINDOW, HKV_D, rep, HD_D)
    kb = k.astype(F32).reshape(B, nb, WINDOW, HKV_D, HD_D)
    vb = v.astype(F32).reshape(B, nb, WINDOW, HKV_D, HD_D)
    pad = jnp.zeros_like(kb[:, :1])
    kk = jnp.concatenate([jnp.concatenate([pad, kb[:, :-1]], axis=1), kb], axis=2)
    vv = jnp.concatenate([jnp.concatenate([pad, vb[:, :-1]], axis=1), vb], axis=2)
    s = jnp.einsum('bnqgrd,bnkgd->bngrqk', qb, kk) * (HD_D ** -0.5)
    qi = jnp.arange(WINDOW)[:, None]
    ki = jnp.arange(2 * WINDOW)[None, :] - WINDOW
    band = (ki <= qi) & (qi - ki < WINDOW)
    mask = band[None] & ((jnp.arange(nb)[:, None, None] > 0) | (ki >= 0)[None])
    p = _sink_probs(s, mask[None, :, None, None], sinks.astype(F32).reshape(HKV_D, rep)[None, None, :, :, None, None])
    o = jnp.einsum('bngrqk,bnkgd->bnqgrd', p, vv)
    return o.reshape(B, L, HQ_D * HD_D), k[:, L - WINDOW:], v[:, L - WINDOW:]

def _swa_sample(q, k, v, kbuf, vbuf, sinks):
    B, L = q.shape[:2]
    rep = HQ_D // HKV_D
    kk = jnp.concatenate([kbuf.astype(k.dtype), k], axis=1)
    vv = jnp.concatenate([vbuf.astype(v.dtype), v], axis=1)
    s = jnp.einsum('bqgrd,bkgd->bgrqk', q.astype(F32).reshape(B, L, HKV_D, rep, HD_D), kk.astype(F32)) * (HD_D ** -0.5)
    qi = jnp.arange(L)[:, None]
    ki = jnp.arange(WINDOW + L)[None, :] - WINDOW
    mask = (ki <= qi) & (qi - ki < WINDOW)
    p = _sink_probs(s, mask, sinks.astype(F32).reshape(HKV_D, rep)[None, :, :, None, None])
    o = jnp.einsum('bgrqk,bkgd->bqgrd', p, vv.astype(F32))
    return o.reshape(B, L, HQ_D * HD_D), kk[:, L:], vv[:, L:]

def _even_mixer(h, pos, s0, w_in, w_out, ret_gn_g, mlp_norm_g, w_s, b_s):
    B, L, _ = h.shape
    qa, ka, va, ga, ub, vb = _split(h @ w_in, EVEN_SIZES)
    qa = _rope(qa.reshape(B, L, H_A, DK_A), pos, DK_A, RET_THETA)
    ka = _rope(ka.reshape(B, L, H_A, DK_A), pos, DK_A, RET_THETA) * (DK_A ** -0.5)
    o_a, s_new = _retention(qa, ka, va.reshape(B, L, H_A, DV_A), s0)
    o_a = (jax.nn.silu(ga) * _layer_norm(o_a, ret_gn_g).reshape(B, L, H_A * DV_A).astype(h.dtype))
    u = jax.nn.gelu(ub, approximate=False).reshape(B, L, G_B, DG_B)
    v_rows = _layer_norm(jax.nn.gelu(vb, approximate=False).reshape(B, L, G_B, DG_B), mlp_norm_g)
    o_b = _chunk_gate(u, v_rows, w_s, b_s).reshape(B, L, G_B * DG_B).astype(h.dtype)
    y = jnp.concatenate([o_a, o_b], axis=-1) @ w_out
    return y, s_new, v_rows

def _odd_mixer(h, pos, s0, kbuf, vbuf, lb, w_in, w_out, onorm_g, qn_g, kn_g, sinks):
    B, L, _ = h.shape
    qc, fc, ic, gc, qd, kd, vd = _split(h @ w_in, ODD_SIZES)
    f = lb + (1.0 - lb) * jax.nn.sigmoid(fc.astype(F32))
    f = f.reshape(B, L, H_C, DK_C)
    q_c = jax.nn.silu(qc).reshape(B, L, H_C, DK_C)
    o_c, s_new = _hgrn2(q_c, 1.0 - f, jnp.log(f), ic.reshape(B, L, H_C, DV_C), s0)
    o_c = (_rms_norm(o_c, onorm_g).reshape(B, L, H_C * DV_C).astype(h.dtype) * jax.nn.silu(gc))
    q_d = _rope(_rms_norm(qd.reshape(B, L, HQ_D, HD_D), qn_g), pos, ROT_DIM_D, ROPE_THETA)
    k_d = _rope(_rms_norm(kd.reshape(B, L, HKV_D, HD_D), kn_g), pos, ROT_DIM_D, ROPE_THETA)
    v_d = vd.reshape(B, L, HKV_D, HD_D)
    if kbuf is None:
        o_d, k_new, v_new = _swa_prompt(q_d, k_d, v_d, sinks)
    else:
        o_d, k_new, v_new = _swa_sample(q_d, k_d, v_d, kbuf, vbuf, sinks)
    y = jnp.concatenate([o_c, o_d.astype(h.dtype)], axis=-1) @ w_out
    return y, s_new, k_new, v_new

def _mem_kv(mem, w_kv, kn_g):
    B = mem.shape[0]
    k, v = jnp.split(mem @ w_kv, 2, axis=-1)
    return _rms_norm(k.reshape(B, N_MEM, H_X, HD_X), kn_g), v.reshape(B, N_MEM, H_X, HD_X)

def _mem_attend(h, mk, mv, w_q, qn_g, w_o):
    B, L, _ = h.shape
    q = _rms_norm((h @ w_q).reshape(B, L, H_X, HD_X), qn_g)
    s = jnp.einsum('blhd,bmhd->bhlm', q.astype(F32), mk.astype(F32)) * (HD_X ** -0.5)
    p = jax.nn.softmax(s, axis=-1)
    o = jnp.einsum('bhlm,bmhd->blhd', p, mv.astype(F32)).astype(h.dtype)
    return o.reshape(B, L, H_X * HD_X) @ w_o

def _conv_ffn(h, c0, w_gate, w_up, conv_w, conv_b, w_down):
    L = h.shape[1]
    g = h @ w_gate
    u = h @ w_up
    gg = jnp.concatenate([c0.astype(g.dtype), g], axis=1)
    c = conv_b + sum(gg[:, j:j + L] * conv_w[j] for j in range(CONV_W))
    y = (jax.nn.gelu(c, approximate=False) * u).astype(h.dtype) @ w_down
    return y, gg[:, L:]

def _run_group(x, pos, mem, st, W):
    prompt = st is None
    B = x.shape[0]
    lbs = jnp.cumsum(jax.nn.softmax(W['hgrn_lb_logits'].astype(F32), axis=0), axis=0)
    out = {'ret': [], 'chunk_v': [], 'hgrn': [], 'swa_k': [], 'swa_v': [], 'mem_k': [], 'mem_v': [], 'conv': []}
    for l in range(DEPTH):
        j = l // 2
        h = _rms_norm(x, W['norm_mix_g'][l])
        if l % 2 == 0:
            s0 = jnp.zeros((B, H_A, DK_A, DV_A), F32) if prompt else st['ret'][j]
            y, s_new, v_rows = _even_mixer(h, pos, s0, W['ev_w_in'][j], W['ev_w_out'][j], W['ret_gn_g'][j],
                                           W['mlp_norm_g'][j], W['mlp_w_s'][j], W['mlp_b_s'][j])
            out['ret'].append(s_new)
            out['chunk_v'].append(v_rows)
        else:
            s0 = jnp.zeros((B, H_C, DK_C, DV_C), F32) if prompt else st['hgrn'][j]
            kbuf = None if prompt else st['swa_k'][j]
            vbuf = None if prompt else st['swa_v'][j]
            y, s_new, k_new, v_new = _odd_mixer(h, pos, s0, kbuf, vbuf, lbs[l] - lbs[0], W['od_w_in'][j],
                                                W['od_w_out'][j], W['hgrn_onorm_g'][j], W['swa_qnorm_g'][j],
                                                W['swa_knorm_g'][j], W['swa_sinks'][j])
            out['hgrn'].append(s_new)
            out['swa_k'].append(k_new)
            out['swa_v'].append(v_new)
        x = x + y
        h = _rms_norm(x, W['norm_mem_g'][l])
        if prompt:
            mk, mv = _mem_kv(mem, W['mem_w_kv'][l], W['mem_knorm_g'][l])
            out['mem_k'].append(mk)
            out['mem_v'].append(mv)
        else:
            mk, mv = st['mem_k'][l], st['mem_v'][l]
        x = x + _mem_attend(h, mk, mv, W['mem_w_q'][l], W['mem_qnorm_g'][l], W['mem_w_o'][l])
        h = _rms_norm(x, W['norm_ffn_g'][l])
        c0 = jnp.zeros((B, CONV_W - 1, D_FF), x.dtype) if prompt else st['conv'][l]
        y, c_new = _conv_ffn(h, c0, W['ffn_w_gate'][l], W['ffn_w_up'][l], W['ffn_conv_w'][l],
                             W['ffn_conv_b'][l], W['ffn_w_down'][l])
        out['conv'].append(c_new)
        x = x + y
    return x, {name: jnp.stack(rows) for name, rows in out.items() if rows}

def setup_inputs(seed: int = 0) -> dict:
    key = jax.random.key(seed)
    keys = iter(jax.random.split(key, 64))

    def nrm(shape, scale):
        return scale * jax.random.normal(next(keys), shape, F32)

    def gain(shape):
        return 1.0 + 0.05 * jax.random.normal(next(keys), shape, F32)

    ev_in = sum(EVEN_SIZES)
    od_in = sum(ODD_SIZES)
    return {
        'x_prompt': nrm((BATCH, SEQ, D_MODEL), 1.0),
        'x_sample': nrm((DEC_BATCH, DEC_SEQ, D_MODEL), 1.0),
        'state_ret': nrm((N_EVEN, DEC_BATCH, H_A, DK_A, DV_A), 1.0),
        'state_hgrn': nrm((N_ODD, DEC_BATCH, H_C, DK_C, DV_C), 1.0),
        'cache_swa_k': nrm((N_ODD, DEC_BATCH, WINDOW, HKV_D, HD_D), 1.0),
        'cache_swa_v': nrm((N_ODD, DEC_BATCH, WINDOW, HKV_D, HD_D), 1.0),
        'cache_mem_k': nrm((DEPTH, DEC_BATCH, N_MEM, H_X, HD_X), 1.0),
        'cache_mem_v': nrm((DEPTH, DEC_BATCH, N_MEM, H_X, HD_X), 1.0),
        'state_ffn_conv': nrm((DEPTH, DEC_BATCH, CONV_W - 1, D_FF), 1.0),
        'mem_prompt': nrm((BATCH, N_MEM, D_MODEL), 1.0),
        'norm_mix_g': gain((DEPTH, D_MODEL)),
        'norm_mem_g': gain((DEPTH, D_MODEL)),
        'norm_ffn_g': gain((DEPTH, D_MODEL)),
        'ev_w_in': nrm((N_EVEN, D_MODEL, ev_in), D_MODEL ** -0.5),
        'ev_w_out': nrm((N_EVEN, EVEN_OUT, D_MODEL), 0.5 * EVEN_OUT ** -0.5),
        'ret_gn_g': gain((N_EVEN, H_A, DV_A)),
        'mlp_norm_g': gain((N_EVEN, G_B, DG_B)),
        'mlp_w_s': nrm((N_EVEN, G_B, MLP_CHUNK, MLP_CHUNK), 0.5 * MLP_CHUNK ** -0.5),
        'mlp_b_s': gain((N_EVEN, G_B, MLP_CHUNK)),
        'od_w_in': nrm((N_ODD, D_MODEL, od_in), D_MODEL ** -0.5),
        'od_w_out': nrm((N_ODD, ODD_OUT, D_MODEL), 0.5 * ODD_OUT ** -0.5),
        'hgrn_lb_logits': nrm((DEPTH, H_C * DK_C), 0.5),
        'hgrn_onorm_g': gain((N_ODD, H_C, DV_C)),
        'swa_qnorm_g': gain((N_ODD, HD_D)),
        'swa_knorm_g': gain((N_ODD, HD_D)),
        'swa_sinks': nrm((N_ODD, HQ_D), 0.5),
        'mem_w_q': nrm((DEPTH, D_MODEL, H_X * HD_X), D_MODEL ** -0.5),
        'mem_w_kv': nrm((DEPTH, D_MODEL, 2 * H_X * HD_X), D_MODEL ** -0.5),
        'mem_qnorm_g': gain((DEPTH, HD_X)),
        'mem_knorm_g': gain((DEPTH, HD_X)),
        'mem_w_o': nrm((DEPTH, H_X * HD_X, D_MODEL), 0.5 * (H_X * HD_X) ** -0.5),
        'ffn_w_gate': nrm((DEPTH, D_MODEL, D_FF), D_MODEL ** -0.5),
        'ffn_w_up': nrm((DEPTH, D_MODEL, D_FF), D_MODEL ** -0.5),
        'ffn_conv_w': nrm((DEPTH, CONV_W, D_FF), CONV_W ** -0.5),
        'ffn_conv_b': nrm((DEPTH, D_FF), 0.02),
        'ffn_w_down': nrm((DEPTH, D_FF, D_MODEL), 0.5 * D_FF ** -0.5),
    }

def reference(x_prompt, x_sample, state_ret, state_hgrn, cache_swa_k, cache_swa_v, cache_mem_k, cache_mem_v,
              state_ffn_conv, mem_prompt, norm_mix_g, norm_mem_g, norm_ffn_g, ev_w_in, ev_w_out, ret_gn_g,
              mlp_norm_g, mlp_w_s, mlp_b_s, od_w_in, od_w_out, hgrn_lb_logits, hgrn_onorm_g, swa_qnorm_g,
              swa_knorm_g, swa_sinks, mem_w_q, mem_w_kv, mem_qnorm_g, mem_knorm_g, mem_w_o, ffn_w_gate,
              ffn_w_up, ffn_conv_w, ffn_conv_b, ffn_w_down):
    W = dict(norm_mix_g=norm_mix_g, norm_mem_g=norm_mem_g, norm_ffn_g=norm_ffn_g, ev_w_in=ev_w_in,
             ev_w_out=ev_w_out, ret_gn_g=ret_gn_g, mlp_norm_g=mlp_norm_g, mlp_w_s=mlp_w_s, mlp_b_s=mlp_b_s,
             od_w_in=od_w_in, od_w_out=od_w_out, hgrn_lb_logits=hgrn_lb_logits, hgrn_onorm_g=hgrn_onorm_g,
             swa_qnorm_g=swa_qnorm_g, swa_knorm_g=swa_knorm_g, swa_sinks=swa_sinks, mem_w_q=mem_w_q,
             mem_w_kv=mem_w_kv, mem_qnorm_g=mem_qnorm_g, mem_knorm_g=mem_knorm_g, mem_w_o=mem_w_o,
             ffn_w_gate=ffn_w_gate, ffn_w_up=ffn_w_up, ffn_conv_w=ffn_conv_w, ffn_conv_b=ffn_conv_b,
             ffn_w_down=ffn_w_down)
    pos_prompt = jnp.arange(SEQ, dtype=jnp.int32)
    pos_sample = PAST_LEN + jnp.arange(DEC_SEQ, dtype=jnp.int32)
    y_prompt, ns_p = _run_group(x_prompt, pos_prompt, mem_prompt, None, W)
    st = dict(ret=state_ret, hgrn=state_hgrn, swa_k=cache_swa_k, swa_v=cache_swa_v,
              mem_k=cache_mem_k, mem_v=cache_mem_v, conv=state_ffn_conv)
    y_sample, ns_s = _run_group(x_sample, pos_sample, None, st, W)
    ret_state_prompt = ns_p['ret']
    hgrn_state_prompt = ns_p['hgrn']
    swa_k_prompt = ns_p['swa_k']
    swa_v_prompt = ns_p['swa_v']
    mem_k_prompt = ns_p['mem_k']
    mem_v_prompt = ns_p['mem_v']
    ffn_conv_prompt = ns_p['conv']
    ret_state_sample = ns_s['ret']
    chunk_v_sample = ns_s['chunk_v']
    hgrn_state_sample = ns_s['hgrn']
    swa_k_sample = ns_s['swa_k']
    swa_v_sample = ns_s['swa_v']
    ffn_conv_sample = ns_s['conv']
    return (y_prompt, y_sample, ret_state_prompt, hgrn_state_prompt, swa_k_prompt, swa_v_prompt,
            mem_k_prompt, mem_v_prompt, ffn_conv_prompt, ret_state_sample, chunk_v_sample,
            hgrn_state_sample, swa_k_sample, swa_v_sample, ffn_conv_sample)


_drawn_inputs = setup_inputs


def setup_inputs(seed=0):
    import zlib

    import numpy as np

    out = dict(_drawn_inputs(seed))
    spreads = {}
    factors = {'norm_mem_g': 8.0,
     'ret_gn_g': 5.079,
     'mlp_b_s': 4.911,
     'hgrn_onorm_g': 5.619,
     'swa_qnorm_g': 25.326,
     'swa_sinks': 64.0,
     'mem_qnorm_g': 8.0,
     'ffn_conv_b': 6.625}
    for name, (base, spread) in spreads.items():
        noise = np.random.default_rng([zlib.crc32(name.encode()), seed]).standard_normal(out[name].shape)
        drawn = base * np.exp(spread * noise) if base else spread * noise
        out[name] = __import__('jax').numpy.asarray(drawn.astype(out[name].dtype))
    for name, factor in factors.items():
        out[name] = (out[name] * factor).astype(out[name].dtype)
    return out
```

```python
from contextlib import ExitStack

import numpy as np
import concourse.bass as bass
from concourse import mybir

F32 = mybir.dt.float32
ALU = mybir.AluOpType
ACT = mybir.ActivationFunctionType
AX = mybir.AxisListType

P = 128
D = 1024
KT = D // P
SEQ, NB, NS = 1024, 8, 8
S = NB * NS
T = SEQ + S
NBLK = SEQ // P
HEADS = 4
DK_A = 64
FF = 2816
FT = FF // P
MEM = 256
WIN = 128
EPS = 1e-6
CH = 256
SPANS = ((0, 384), (384, 384), (768, 320))
TOK = [(j * P, P) for j in range(NBLK)] + [(SEQ, S)]
LEVELS = 7
FIRST = 16


class Count:

    def __init__(self, sem):
        self.sem, self.base = sem, 0

    def at(self, n):
        return n + self.base

    def adds(self, n):
        self.base += n


class Chain:

    def __init__(self, sem):
        self.sem, self.n, self.term = sem, 0, None

    def now(self):
        return self.n if self.term is None else self.term + self.n

    def next(self):
        self.n += 1
        return self.now()

    def enter(self, i, per):
        self.term, self.start, self.per = i * per, self.n, per

    def leave(self, rounds):
        assert self.n - self.start == self.per, (self.n - self.start, self.per)
        self.n, self.term = self.start + rounds * self.per, None


class Shared:
    pass


def build(nc, io):
    with ExitStack() as ctx:
        _build(nc, io, ctx)


def _build(nc, io, ctx):
    def sb(name, shape):
        return ctx.enter_context(nc.sbuf_tensor(name, shape, F32))

    def sem(name):
        return ctx.enter_context(nc.semaphore(name))

    counts = {}

    def count(name):
        if name not in counts:
            counts[name] = Count(sem(name))
        return counts[name]

    X = sb("residual", [P, KT, T])
    H = sb("normed", [P, KT, T])
    OT = sb("mixed", [P, KT, T])
    R = sb("work", [P, 13, T])
    WS = [sb(f"weights{s}", [P, 2048]) for s in range(2)]
    COS, SIN = sb("cos", [P, T]), sb("sin", [P, T])
    MASK = sb("masks", [P, 1408])
    IDENT, ROT = sb("ident", [P, P]), sb("rot", [P, P])
    ONES, ONES128, ONES64 = (sb(n, [P, P]) for n in ("ones1024", "ones128", "ones64"))
    GAIN = sb("gains", [P, 3 * KT])
    COL = sb("columns", [P, 96])
    SM = sb("small", [P, 320])
    EPSC = sb("eps", [P, 1])
    SPARE = sb("spare", [P, 2, T])
    PS = ctx.enter_context(nc.psum_tensor("psum", [P, 8, 512], F32))
    Rf = R[:, :, :].rearrange("p a b -> p (a b)")
    Hf = H[:, :, :].rearrange("p a b -> p (a b)")
    OTf = OT[:, :, :].rearrange("p a b -> p (a b)")
    PSf = PS[:, :, :].rearrange("p a b -> p (a b)")

    def view(flat, at, *dims):
        n = 1
        for d in dims:
            n *= d
        v = flat[:, at:at + n]
        if len(dims) == 2:
            v = v.rearrange("p (a b) -> p a b", b=dims[1])
        if len(dims) == 3:
            v = v.rearrange("p (a b c) -> p a b c", b=dims[1], c=dims[2])
        return v

    act_own, dve_own, pool_own = Chain(sem("act_own")), Chain(sem("dve_own")), Chain(sem("pool_own"))
    w_loaded = [count(f"w_loaded{s}") for s in range(2)]
    tile_full, tile_free = count("tile_full"), count("tile_free")
    loaded, stored = count("loaded"), count("stored")
    stores = [0]

    def store(eng, dst, src):
        eng.dma_start(dst, src).then_inc(stored.sem, 16)
        stores[0] += 16

    def load(pairs, zero=()):
        cleared = count("cleared")
        with nc.Block() as block:
            @block.gpsimd
            def _(pool):
                for z in zero:
                    nc.gpsimd.memset(z, 0.0).then_inc(cleared.sem, 1)

            @block.sync
            def _(sp):
                if zero:
                    sp.wait_ge(cleared.sem, cleared.at(len(zero)))
                for dst, src in pairs:
                    sp.dma_start(dst, src).then_inc(loaded.sem, 16)
                sp.wait_ge(loaded.sem, loaded.at(16 * len(pairs)))
        loaded.adds(16 * len(pairs))
        cleared.adds(len(zero))

    def w_slot(s, kt, cols):
        return WS[s][:, 0:kt * cols].rearrange("p (k n) -> p k n", n=cols)

    def project(w, src, kt, chunks, evac, on="scalar", cols=CH, spans=SPANS, own=0):
        tpc = cols // P
        wr = w.rearrange("(k p) n -> p k n", p=P)
        pairs = chunks // 2

        def rounds(eng, body, chain=None):
            if pairs > 1:
                with eng.Fori(0, pairs) as i:
                    if chain:
                        chain.enter(i, own * 2 * tpc)
                    for s in range(2):
                        body(i * 2 + s, s, i)
                if chain:
                    chain.leave(pairs)
            elif pairs:
                for s in range(2):
                    body(s, s, 0)
            if chunks % 2:
                body(chunks - 1, 0, pairs)

        with nc.Block() as block:
            @block.sync
            def _(sp):
                def body(c, s, i):
                    sp.wait_ge(tile_full.sem, tile_full.at((c - 1) * tpc))
                    sp.dma_start(w_slot(s, kt, cols), wr[:, :, bass.ds(c * cols, cols)]).then_inc(w_loaded[s].sem, 16)
                rounds(sp, body)

            @block.tensor
            def _(pe):
                def body(c, s, i):
                    pe.wait_ge(w_loaded[s].sem, w_loaded[s].at(i * 16 + 16))
                    ws = w_slot(s, kt, cols)
                    for t in range(tpc):
                        pe.wait_ge(tile_free.sem, tile_free.at(c * tpc + (t - 1)))
                        par = t % 2 if tpc == 2 else s
                        for n, (a, m) in enumerate(spans):
                            for k in range(kt):
                                last = pe.matmul(PS[:, 3 * par + n, 0:m], ws[:, k, t * P:(t + 1) * P],
                                                 src[:, k, a:a + m], start=(k == 0), stop=(k == kt - 1))
                        last.then_inc(tile_full.sem, 1)
                rounds(pe, body)

            def out(eng):
                def body(c, s, i):
                    for t in range(tpc):
                        par = t % 2 if tpc == 2 else s
                        eng.wait_ge(tile_full.sem, tile_full.at(c * tpc + t + 1))
                        evac(eng, c * tpc + t, 3 * par).then_inc(tile_free.sem, 1)
                rounds(eng, body, (act_own if on == "scalar" else dve_own))
            (block.scalar if on == "scalar" else block.vector)(lambda eng: out(eng))
        tile_full.adds(chunks * tpc)
        tile_free.adds(chunks * tpc)
        w_loaded[0].adds(16 * ((chunks + 1) // 2))
        w_loaded[1].adds(16 * (chunks // 2))

    def pieces(bank, spans=SPANS):
        if len(spans) == 1:
            return [(PS[:, bank, 0:spans[0][1]], 0, spans[0][1], 1)]
        return [(PS[:, bank:bank + 2, 0:384], 0, 768, 2), (PS[:, bank + 2, 0:320], 768, 320, 1)]

    def cut(buf, tile, a, m, rows):
        v = buf[:, bass.ds(tile, 1), a:a + m].rearrange("p a b -> p (a b)")
        return v.rearrange("p (r b) -> p r b", r=rows) if rows > 1 else v

    def to_tiles(buf, first, func, scale=1.0, spans=SPANS):
        def evac(eng, tile, bank):
            for ps, a, m, rows in pieces(bank, spans):
                last = eng.activation(cut(buf, tile + first, a, m, rows), ps, func, scale=scale)
            return last
        return evac

    def to_residual(eng, tile, bank):
        for ps, a, m, rows in pieces(bank):
            x = cut(X, tile, a, m, rows)
            last = eng.tensor_tensor(x, ps, x, ALU.add)
        return last

    def project_tokens(w, src, kt, chunks, evac, on="scalar", cols=CH, toks=TOK):
        wr = w.rearrange("(k p) n -> p k n", p=P)
        nt = len(toks)
        with nc.Block() as block:
            @block.sync
            def _(sp):
                for c in range(chunks):
                    sp.wait_ge(tile_full.sem, tile_full.at((c - 1) * nt))
                    sp.dma_start(w_slot(c % 2, kt, cols), wr[:, :, c * cols:(c + 1) * cols]).then_inc(w_loaded[c % 2].sem, 16)

            @block.tensor
            def _(pe):
                for c in range(chunks):
                    pe.wait_ge(w_loaded[c % 2].sem, w_loaded[c % 2].at(c // 2 * 16 + 16))
                    ws = w_slot(c % 2, kt, cols)
                    for n, (a, m) in enumerate(toks):
                        j = c * nt + n
                        pe.wait_ge(tile_free.sem, tile_free.at(j - 1))
                        for k in range(kt):
                            last = pe.matmul(PS[0:m, j % 2, 0:cols], src[:, k, a:a + m], ws[:, k, :],
                                             start=(k == 0), stop=(k == kt - 1))
                        last.then_inc(tile_full.sem, 1)

            def out(eng):
                for c in range(chunks):
                    for n, (a, m) in enumerate(toks):
                        j = c * nt + n
                        eng.wait_ge(tile_full.sem, tile_full.at(j + 1))
                        evac(eng, c, n, m, PS[0:m, j % 2, 0:cols]).then_inc(tile_free.sem, 1)
            (block.scalar if on == "scalar" else block.vector)(lambda eng: out(eng))
        tile_full.adds(chunks * nt)
        tile_free.adds(chunks * nt)
        w_loaded[0].adds(16 * ((chunks + 1) // 2))
        w_loaded[1].adds(16 * (chunks // 2))

    def to_rows(buf, func):
        def evac(eng, c, n, m, ps):
            return eng.activation(buf[0:m, n, c * CH:(c + 1) * CH], ps, func)
        return evac

    def rms_norm(which):
        squared, freed, rooted = count("squared"), count("square_used"), count("rooted")
        SQ, RS, RI = OT[:, 6:8, :], OT[:, 5, :], OT[:, 4, :]
        with nc.Block() as block:
            @block.scalar
            def _(act):
                for k in range(KT):
                    if k >= 2:
                        act.wait_ge(freed.sem, freed.at(k - 1))
                    act.activation(SQ[:, k % 2, :], X[:, k, :], ACT.Square).then_inc(squared.sem, 1)
                act.wait_ge(freed.sem, freed.at(KT))
                for ps, a, m, rows in pieces(0):
                    act.activation(cut(OT, 5, a, m, rows), ps, ACT.Sqrt, bias=EPSC[:, 0:1]).then_inc(rooted.sem, 1)

            @block.tensor
            def _(pe):
                for k in range(KT):
                    pe.wait_ge(squared.sem, squared.at(k + 1))
                    for n, (a, m) in enumerate(SPANS):
                        last = pe.matmul(PS[:, n, 0:m], ONES[:, :], SQ[:, k % 2, a:a + m], start=(k == 0), stop=(k == KT - 1))
                    last.then_inc(freed.sem, 1)

            @block.vector
            def _(dve):
                dve.wait_ge(rooted.sem, rooted.at(2))
                dve.reciprocal(RI, RS).then_inc(dve_own.sem, 1)
                dve.wait_ge(dve_own.sem, dve_own.next())
                for k in range(KT):
                    dve.scalar_tensor_tensor(H[:, k, :], X[:, k, :], GAIN[:, which * KT + k:which * KT + k + 1], RI, ALU.mult, ALU.mult)
        for c, n in ((squared, KT), (freed, KT), (rooted, 2)):
            c.adds(n)

    def tile_norm(srcs, dsts, ones, gains, scratch, width=T, center=False, times=None):
        spans = SPANS if width == T else ((0, width),)
        squared, summed, rooted = count("tile_squared"), count("tile_summed"), count("tile_rooted")
        meaned, centered, scaled = count("tile_meaned"), count("tile_centered"), count("tile_scaled")
        n_t, n_p = len(srcs), len(pieces(0, spans))

        def shaped(v, a, m, rows):
            v = v[:, a:a + m]
            return v.rearrange("p (r b) -> p r b", r=rows) if rows > 1 else v
        with nc.Block() as block:
            @block.tensor
            def _(pe):
                for t in range(n_t):
                    if t >= 1:
                        pe.wait_ge(rooted.sem, rooted.at(n_p * t))
                    if center:
                        for n, (a, m) in enumerate(spans):
                            last = pe.matmul(PS[:, 3 + n, 0:m], ones, srcs[t][:, a:a + m], start=True, stop=True)
                        last.then_inc(meaned.sem, 1)
                    pe.wait_ge(squared.sem, squared.at(t + 1))
                    for n, (a, m) in enumerate(spans):
                        last = pe.matmul(PS[:, n, 0:m], ones, scratch[t % 2][:, a:a + m], start=True, stop=True)
                    last.then_inc(summed.sem, 1)

            @block.scalar
            def _(act):
                for t in range(n_t):
                    if center:
                        act.wait_ge(centered.sem, centered.at(t + 1))
                    if t >= 2:
                        act.wait_ge(summed.sem, summed.at(t - 1))
                    act.activation(scratch[t % 2], srcs[t], ACT.Square).then_inc(squared.sem, 1)
                    act.wait_ge(summed.sem, summed.at(t + 1))
                    if t >= 2:
                        act.wait_ge(scaled.sem, scaled.at(t - 1))
                    for ps, a, m, rows in pieces(0, spans):
                        act.activation(shaped(scratch[2 + t % 2], a, m, rows), ps, ACT.Sqrt, bias=EPSC[:, 0:1]).then_inc(rooted.sem, 1)

            @block.vector
            def _(dve):
                for t in range(n_t):
                    if center:
                        dve.wait_ge(meaned.sem, meaned.at(t + 1))
                        for ps, a, m, rows in pieces(3, spans):
                            v = shaped(srcs[t], a, m, rows)
                            last = dve.tensor_tensor(v, v, ps, ALU.subtract)
                        last.then_inc(centered.sem, 1)
                        dve.wait_ge(centered.sem, centered.at(t + 1))
                    dve.wait_ge(rooted.sem, rooted.at(n_p * (t + 1)))
                    inv = scratch[2 + t % 2]
                    dve.reciprocal(inv, inv).then_inc(dve_own.sem, 1)
                    dve.wait_ge(dve_own.sem, dve_own.next())
                    last = dve.scalar_tensor_tensor(srcs[t] if times else dsts[t], srcs[t], gains[t], inv, ALU.mult, ALU.mult)
                    if times:
                        last.then_inc(dve_own.sem, 1)
                        dve.wait_ge(dve_own.sem, dve_own.next())
                        last = dve.tensor_tensor(dsts[t], srcs[t], times[t], ALU.mult)
                    last.then_inc(scaled.sem, 1)
        for c, n in ((squared, n_t), (summed, n_t), (rooted, n_t * n_p), (scaled, n_t)):
            c.adds(n)
        if center:
            meaned.adds(n_t)
            centered.adds(n_t)

    def rotate(tiles, scratch):
        rotated, taken = count("rotated"), count("rotated_taken")
        with nc.Block() as block:
            @block.tensor
            def _(pe):
                for t, x in enumerate(tiles):
                    if t >= 2:
                        pe.wait_ge(taken.sem, taken.at(t - 1))
                    for n, (a, m) in enumerate(SPANS):
                        last = pe.matmul(PS[:, 3 * (t % 2) + n, 0:m], ROT[:, :], x[:, a:a + m], start=True, stop=True)
                    last.then_inc(rotated.sem, 1)

            @block.vector
            def _(dve):
                for t, x in enumerate(tiles):
                    dve.wait_ge(rotated.sem, rotated.at(t + 1))
                    for ps, a, m, rows in pieces(3 * (t % 2)):
                        o, s = scratch[:, a:a + m], SIN[:, a:a + m]
                        if rows > 1:
                            o, s = (v.rearrange("p (r b) -> p r b", r=rows) for v in (o, s))
                        last = dve.tensor_tensor(o, ps, s, ALU.mult)
                    last.then_inc(taken.sem, 1)
                    dve.tensor_tensor(x, x, COS[:, :], ALU.mult).then_inc(dve_own.sem, 1)
                    dve.wait_ge(dve_own.sem, dve_own.next())
                    dve.wait_ge(taken.sem, taken.at(t + 1))
                    dve.tensor_tensor(x, x, scratch, ALU.add).then_inc(dve_own.sem, 1)
                    dve.wait_ge(dve_own.sem, dve_own.next())
        rotated.adds(len(tiles))
        taken.adds(len(tiles))

    def tok(v, j):
        a, m = TOK[j]
        return v[..., a:a + m]

    with nc.Block() as block:
        consts = [(X[:, :, :], io["xT"].rearrange("(k p) t -> p k t", p=P)), (IDENT[:, :], io["ident"])]

        @block.sync
        def _(sp):
            for dst, src in consts:
                sp.dma_start(dst, src).then_inc(loaded.sem, 16)
            sp.wait_ge(loaded.sem, loaded.at(16 * len(consts)))

        @block.gpsimd
        def _(pool):
            for v, x in ((ONES, 1.0 / D), (ONES128, 1.0 / P), (EPSC, EPS), (ONES64, 0.0)):
                nc.gpsimd.memset(v[:, :], x).then_inc(pool_own.sem, 1)
            pool.wait_ge(pool_own.sem, 4)
            nc.gpsimd.memset(ONES64[0:64, 0:64], 1.0 / 64)
            nc.gpsimd.memset(ONES64[64:128, 64:128], 1.0 / 64)
            pool.sem_inc(tile_full.sem, FIRST)
            pool.sem_inc(tile_free.sem, FIRST)
        pool_own.n = 4
        tile_full.adds(FIRST)
        tile_free.adds(FIRST)
    loaded.adds(16 * 2)

    env = Shared()
    env.COL = COL
    env.COS = COS
    env.EPSC = EPSC
    env.GAIN = GAIN
    env.H = H
    env.Hf = Hf
    env.IDENT = IDENT
    env.MASK = MASK
    env.ONES128 = ONES128
    env.ONES64 = ONES64
    env.OT = OT
    env.OTf = OTf
    env.PS = PS
    env.PSf = PSf
    env.R = R
    env.ROT = ROT
    env.Rf = Rf
    env.SIN = SIN
    env.SM = SM
    env.SPARE = SPARE
    env.WS = WS
    env.X = X
    env.act_own = act_own
    env.count = count
    env.cut = cut
    env.dve_own = dve_own
    env.load = load
    env.loaded = loaded
    env.pieces = pieces
    env.project = project
    env.project_tokens = project_tokens
    env.rms_norm = rms_norm
    env.rotate = rotate
    env.store = store
    env.stored = stored
    env.stores = stores
    env.tile_norm = tile_norm
    env.to_residual = to_residual
    env.to_rows = to_rows
    env.to_tiles = to_tiles
    env.view = view
    env.w_loaded = w_loaded
    env.w_slot = w_slot

    def run(stage, *args, **options):
        stage(*args, **options)

    _layer0(nc, io, env, run)
    for l in range(2):
        if l == 1:
            _layer1(nc, io, env, run)
        _memory(nc, io, env, run, l)
        _feed_forward(nc, io, env, run, l)
    with nc.Block() as block:
        @block.sync
        def _(sp):
            store(sp, io["yT"].rearrange("(k p) t -> p k t", p=P), X[:, :, :])
            sp.wait_ge(stored.sem, stored.at(stores[0]))


def _layer0(nc, io, env, run):
    g = env
    X, H, OT, R, Rf, Hf, OTf, PS, PSf, view, count, P_ = g.X, g.H, g.OT, g.R, g.Rf, g.Hf, g.OTf, g.PS, g.PSf, g.view, g.count, P
    MASK, COS, SIN, COL, SM, IDENT = g.MASK, g.COS, g.SIN, g.COL, g.SM, g.IDENT
    act_own, dve_own = g.act_own, g.dve_own
    VA, VB = view(Rf, 4 * T, 9, 512), view(Rf, 4 * T + 4608, 9, 512)
    STATE = view(Rf, 4 * T + 9216, 2, 256)
    DMASK, QDEC, PAIR = view(MASK[:, :], 0, 4, P), view(MASK[:, :], 512, 2, P), view(MASK[:, :], 768, 256)
    DMASK_S, QDEC_S = MASK[0:S, 1024:1280].rearrange("p (h n) -> p h n", n=S), view(MASK[:, :], 1280, 2, NS)
    RC = MASK[:, 1296:1320]
    SAMPLE_STATE = view(Hf, 4 * T, NB, 2, 256)
    w_in = io["ev_w_in"]

    run(g.load, [(g.GAIN[:, :], io["gain0"]), (COS[:, :], io["ret_cos"]), (SIN[:, :], io["ret_sin"]), (g.ROT[:, :], io["ret_rot"]),
                 (MASK[:, 0:1320], io["ret_tables"]), (COL[:, 0:4], io["ret_gn_g"])], zero=(VB[64:128, 8, :],))
    run(g.rms_norm, 0)

    def q_k(eng, tile, bank):
        for ps, a, m, rows in g.pieces(bank):
            last = eng.activation(g.cut(R, tile, a, m, rows), ps, ACT.Copy, scale=DK_A ** -0.5 if tile >= 2 else 1.0)
        return last
    run(g.project, w_in[:, 0:512], H, KT, 2, q_k)
    run(g.project_tokens, w_in[:, 512:1024], H, KT, 2, g.to_rows(VA, ACT.Copy))
    run(g.project, w_in[:, 1024:1536], H, KT, 2, g.to_tiles(OT, 0, ACT.Silu))
    run(g.project, w_in[:, 1536:2048], H, KT, 2, g.to_tiles(OT, 4, ACT.Gelu))
    run(g.project_tokens, w_in[:, 2048:2560], H, KT, 2, g.to_rows(VB, ACT.Gelu))
    run(g.rotate, [R[:, t, :] for t in range(4)], H[:, 7, :])

    def clear_state():
        run(g.load, [(SAMPLE_STATE[64 * hh:64 * hh + 64, :, pr, 128 * hh:128 * hh + 128],
                      io["state_ret"].rearrange("b (t e) k v -> t e k b v", e=2)[pr, hh])
                     for hh in range(2) for pr in range(2)],
            zero=(SAMPLE_STATE[0:64, :, :, 128:256], SAMPLE_STATE[64:128, :, :, 0:128]))
    clear_state()

    work = [COS, SIN]

    def retention():
        a_ready, a_taken, o_ready, o_out = (count(n) for n in ("ret_scores", "ret_taken", "ret_out", "ret_out_taken"))
        kv_ready, s_ready = count("ret_kv"), count("ret_state")

        def bufs(j):
            w = work[j % 2]
            return view(w[:, :], 0, 4, P), view(w[:, :], 512, 4, 64), view(w[:, :], 768, 2, P)
        with nc.Block() as block:
            @block.tensor
            def _(pe):
                for j, (a, m) in enumerate(TOK):
                    AT, KD, QD = bufs(j)
                    if j:
                        pe.wait_ge(a_taken.sem, a_taken.at(j))
                    for h in range(HEADS):
                        pr, r = h // 2, 64 * (h % 2)
                        pe.matmul(PS[0:m, h % 2, pr * P:pr * P + m], R[r:r + 64, 2 + pr, a:a + m], R[r:r + 64, pr, a:a + m], start=True, stop=True)
                    for pr in range(2):
                        last = pe.transpose(PS[0:m, 2, pr * P:(pr + 1) * P], R[:, 2 + pr, a:a + m], IDENT[:, :])
                    last.then_inc(a_ready.sem, 1)
                    pe.wait_ge(a_taken.sem, a_taken.at(j + 1))
                    pe.wait_ge(s_ready.sem, s_ready.at(min(j, NBLK - 1) + 1))
                    if j >= 2:
                        pe.wait_ge(o_out.sem, o_out.at(j - 1))
                    for h in range(HEADS):
                        pr, hh = h // 2, h % 2
                        o = PS[:, 3 + j % 2, h * P:h * P + m]
                        pe.matmul(o, VA[0:m, j, h * P:(h + 1) * P], AT[0:m, h, 0:m], start=True, stop=(j == NBLK))
                        if j < NBLK:
                            last = pe.matmul(o, STATE[:, pr, hh * P:(hh + 1) * P], QD[:, pr, :], start=False, stop=True)
                        else:
                            for b in range(NB):
                                last = pe.matmul(PS[:, 3 + j % 2, h * P + b * NS:h * P + (b + 1) * NS], SAMPLE_STATE[:, b, pr, hh * P:(hh + 1) * P],
                                                 QD[:, pr, b * NS:(b + 1) * NS], start=False, stop=True, skip_group_check=True)
                    last.then_inc(o_ready.sem, 1)
                    if j < NBLK:
                        for pr in range(2):
                            last = pe.matmul(PS[:, 5, pr * 256:(pr + 1) * 256], KD[:, 2 * pr:2 * pr + 2, :].rearrange("p a b -> p (a b)"),
                                             VA[:, j, pr * 256:(pr + 1) * 256], start=True, stop=True)
                        last.then_inc(kv_ready.sem, 1)

            @block.vector
            def _(dve):
                dve.memset(STATE, 0.0).then_inc(s_ready.sem, 1)
                for j, (a, m) in enumerate(TOK):
                    AT, KD, QD = bufs(j)
                    dve.wait_ge(a_ready.sem, a_ready.at(j + 1))
                    if j >= 2:
                        dve.wait_ge(o_ready.sem, o_ready.at(j - 1))
                        dve.wait_ge(kv_ready.sem, kv_ready.at(j - 1))
                    dm = DMASK if j < NBLK else DMASK_S
                    for hh in range(2):
                        dve.tensor_tensor(AT[0:m, hh:4:2, 0:m], PS[0:m, hh, 0:256].rearrange("p (a b) -> p a b", b=P)[:, :, 0:m], dm[0:m, hh:4:2, 0:m], ALU.mult)
                    kc = RC[0:m, 0:4] if j < NBLK else RC[0:m, 4:8]
                    dve.tensor_tensor(KD[0:m, :, :], PS[0:m, 2, 0:256].rearrange("p (a b) -> p a b", b=64), kc.unsqueeze(2).to_broadcast([m, 4, 64]), ALU.mult)
                    if j < NBLK:
                        last = dve.tensor_tensor(QD[:, :, :], R[:, 0:2, a:a + m], QDEC[:, :, :], ALU.mult)
                    else:
                        for pr in range(2):
                            last = dve.tensor_tensor(QD[:, pr, 0:m].rearrange("p (b t) -> p b t", t=NS), R[:, pr, a:a + m].rearrange("p (b t) -> p b t", t=NS),
                                                     QDEC_S[:, pr, :].unsqueeze(1).to_broadcast([P, NB, NS]), ALU.mult)
                    last.then_inc(a_taken.sem, 1)
                    if j < NBLK:
                        dve.wait_ge(kv_ready.sem, kv_ready.at(j + 1))
                        kv = PS[:, 5, :].rearrange("p (a b) -> p a b", b=256)
                        dve.tensor_tensor(kv, kv, PAIR.unsqueeze(1).to_broadcast([P, 2, 256]), ALU.mult).then_inc(dve_own.sem, 1)
                        dve.wait_ge(dve_own.sem, dve_own.next())
                        for pr in range(2):
                            last = dve.scalar_tensor_tensor(STATE[:, pr, :], STATE[:, pr, :], RC[:, 8 + pr:9 + pr], kv[:, pr, :], ALU.mult, ALU.add)
                        last.then_inc(s_ready.sem, 1)
                        dve.wait_ge(s_ready.sem, s_ready.at(j + 2))

            @block.scalar
            def _(act):
                for j, (a, m) in enumerate(TOK):
                    act.wait_ge(o_ready.sem, o_ready.at(j + 1))
                    act.activation(H[:, 0:4, a:a + m], PS[:, 3 + j % 2, :].rearrange("p (h n) -> p h n", n=P)[:, :, 0:m], ACT.Copy).then_inc(o_out.sem, 1)
        for c, n in ((a_ready, 9), (a_taken, 9), (o_ready, 9), (o_out, 9), (kv_ready, 8), (s_ready, 9)):
            c.adds(n)
    run(retention)

    def new_sample_states():
        spread, made, updated = count("spread"), count("states_made"), count("states_updated")
        VBD = view(Rf, 0, 2, NB, 256)
        KD = view(COS[:, :], 512, 2, P)
        with nc.Block() as block:
            @block.vector
            def _(dve):
                for pr in range(2):
                    dve.tensor_tensor(VBD[0:S, pr], VA[0:S, 8, pr * 256:(pr + 1) * 256].unsqueeze(1).to_broadcast([S, NB, 256]),
                                      RC[0:S, 12:20].unsqueeze(2).to_broadcast([S, NB, 256]), ALU.mult).then_inc(spread.sem, 1)
                for pr in range(2):
                    for c in range(4):
                        dve.wait_ge(made.sem, made.at(pr * 4 + c + 1))
                        s = SAMPLE_STATE[:, 2 * c:2 * c + 2, pr, :]
                        dve.scalar_tensor_tensor(s, s, RC[:, 10 + pr:11 + pr], PS[:, pr * 4 + c, :].rearrange("p (a b) -> p a b", b=256),
                                                 ALU.mult, ALU.add).then_inc(updated.sem, 1)

            @block.tensor
            def _(pe):
                for pr in range(2):
                    pe.wait_ge(spread.sem, spread.at(pr + 1))
                    for c in range(4):
                        pe.matmul(PS[:, pr * 4 + c, :], KD[0:S, pr, :], VBD[0:S, pr, 2 * c:2 * c + 2, :].rearrange("p a b -> p (a b)"), start=True, stop=True).then_inc(made.sem, 1)

            @block.sync
            def _(sp):
                out = io["ret_state_prompt"].rearrange("(t e) k v -> t e k v", e=2)
                for hh in range(2):
                    g.store(sp, out[:, hh].rearrange("t k v -> k t v"), STATE[64 * hh:64 * hh + 64, :, hh * P:(hh + 1) * P])
                sp.wait_ge(updated.sem, updated.at(8))
                out = io["ret_state_sample"].rearrange("b (t e) k v -> t e k b v", e=2)
                for pr in range(2):
                    for hh in range(2):
                        g.store(sp, out[pr, hh], SAMPLE_STATE[64 * hh:64 * hh + 64, :, pr, hh * P:(hh + 1) * P])
                sp.wait_ge(g.stored.sem, g.stored.at(g.stores[0]))
        for c, n in ((spread, 2), (made, 8), (updated, 8)):
            c.adds(n)
    run(new_sample_states)
    run(g.tile_norm, [H[:, h, :] for h in range(4)], [OT[:, h, :] for h in range(4)], g.ONES128[:, :], [COL[:, h:h + 1] for h in range(4)],
        [H[:, 4 + i, :] for i in range(4)], center=True, times=[OT[:, h, :] for h in range(4)])

    WT, BT, TRI = view(MASK[:, :], 0, 4, P), view(MASK[:, :], 512, 4, P), view(MASK[:, :], 1024, P)
    WTS = MASK[0:S, 1152:1408].rearrange("p (g t) -> p g t", t=S)
    GB, TRIS, BTS = COS[:, 0:512], COS[0:S, 512:576], view(COS[:, :], 576, 4, NS)
    run(g.load, [(WT, io["mlp_wT"].rearrange("g s t -> s g t")), (BT, io["mlp_b_s"].partition_broadcast(P)), (TRI, io["tri"]),
                 (WTS, io["mlp_wTs"].rearrange("g s t -> s g t")), (GB, io["mlp_norm_g"].partition_broadcast(P)), (TRIS, io["tri_s"]),
                 (BTS, io["mlp_b_s"].partition_broadcast(P)[:, :, 0:NS])])

    def gate_norm():
        centered, squared, var, rooted, rows = (count(n) for n in ("gate_centered", "gate_squared", "gate_var", "gate_rooted", "gate_rows"))
        V3 = VB.rearrange("p n (g d) -> p (n g) d", d=P)
        SQ = view(Hf, 0, 36, P)
        mean, inv = SM[:, 0:36], SM[:, 36:72]
        with nc.Block() as block:
            @block.vector
            def _(dve):
                dve.tensor_reduce(mean, V3, AX.X, ALU.add).then_inc(dve_own.sem, 1)
                dve.wait_ge(dve_own.sem, dve_own.next())
                dve.tensor_scalar(mean, mean, 1.0 / P, None, ALU.mult).then_inc(dve_own.sem, 1)
                dve.wait_ge(dve_own.sem, dve_own.next())
                dve.tensor_tensor(V3, V3, mean.unsqueeze(2).to_broadcast([P, 36, P]), ALU.subtract).then_inc(centered.sem, 1)
                dve.tensor_tensor(WT, WT, TRI.unsqueeze(1).to_broadcast([P, 4, P]), ALU.mult)
                dve.tensor_tensor(WTS, WTS, TRIS.unsqueeze(1).to_broadcast([S, 4, S]), ALU.mult)
                dve.wait_ge(squared.sem, squared.at(1))
                dve.tensor_reduce(inv, SQ, AX.X, ALU.add).then_inc(var.sem, 1)
                dve.wait_ge(rooted.sem, rooted.at(1))
                dve.reciprocal(inv, inv).then_inc(dve_own.sem, 1)
                dve.wait_ge(dve_own.sem, dve_own.next())
                dve.tensor_tensor(V3, V3, inv.unsqueeze(2).to_broadcast([P, 36, P]), ALU.mult).then_inc(dve_own.sem, 1)
                dve.wait_ge(dve_own.sem, dve_own.next())
                dve.tensor_tensor(VB, VB, GB.unsqueeze(1).to_broadcast([P, 9, 512]), ALU.mult).then_inc(rows.sem, 1)

            @block.scalar
            def _(act):
                act.wait_ge(centered.sem, centered.at(1))
                act.activation(SQ, V3, ACT.Square).then_inc(squared.sem, 1)
                act.wait_ge(var.sem, var.at(1))
                act.activation(inv, inv, ACT.Sqrt, scale=1.0 / P, bias=g.EPSC[:, 0:1]).then_inc(rooted.sem, 1)

            @block.sync
            def _(sp):
                sp.wait_ge(rows.sem, rows.at(1))
                g.store(sp, io["chunk_v_sample"], VB[0:S, 8, :])
                sp.wait_ge(g.stored.sem, g.stored.at(g.stores[0]))
        for c in (centered, squared, var, rooted, rows):
            c.adds(1)
    run(gate_norm)

    def gate_mix():
        mixed, taken = count("gate_mixed"), count("gate_taken")
        with nc.Block() as block:
            @block.tensor
            def _(pe):
                for j, (a, m) in enumerate(TOK):
                    if j >= 2:
                        pe.wait_ge(taken.sem, taken.at(j - 1))
                    w = WT if j < NBLK else WTS
                    for q in range(4):
                        last = pe.matmul(PS[:, j % 2, q * P:q * P + m], VB[0:m, j, q * P:(q + 1) * P], w[0:m, q, 0:m], start=True, stop=True)
                    last.then_inc(mixed.sem, 1)

            @block.vector
            def _(dve):
                for j, (a, m) in enumerate(TOK):
                    dve.wait_ge(mixed.sem, mixed.at(j + 1))
                    ps = PS[:, j % 2, :].rearrange("p (g t) -> p g t", t=P)
                    tmp = view(Hf, (j % 2) * 512, 4, P)
                    if j < NBLK:
                        last = dve.tensor_tensor(tmp, ps, BT, ALU.add)
                    else:
                        for q in range(4):
                            last = dve.tensor_tensor(tmp[:, q, 0:S].rearrange("p (b t) -> p b t", t=NS), ps[:, q, 0:S].rearrange("p (b t) -> p b t", t=NS),
                                                     BTS[:, q, :].unsqueeze(1).to_broadcast([P, NB, NS]), ALU.add)
                    last.then_inc(taken.sem, 1)
                    dve.wait_ge(taken.sem, taken.at(j + 1))
                    dve.tensor_tensor(OT[:, 4:8, a:a + m], OT[:, 4:8, a:a + m], tmp[:, :, 0:m], ALU.mult)
        mixed.adds(9)
        taken.adds(9)
    run(gate_mix)
    run(g.project, io["ev_w_out"], OT, KT, 4, g.to_residual, on="vector")


def _attend(nc, g, units, scale, nt):
    count, PS, view, Hf, SM, dve_own = g.count, g.PS, g.view, g.Hf, g.SM, g.dve_own
    scored, peaked, exped, normed, turned, pt_ready, out_ready, out_taken = (count("att_" + n) for n in (
        "scored", "peaked", "exped", "normed", "turned", "pt_ready", "out_ready", "out_taken"))
    n = len(units)
    outs, k = [], 0
    for u in units:
        k += u.last
        outs.append(k)

    def probs(u):
        return view(Hf, (u % 2) * 1024, 4, 256) if units[u].G > 1 else view(Hf, (u % 2) * 1024, 1, 256)

    def turned_probs(u):
        return view(Hf, 2048 + (u % 2) * 1024, 2, 4, P)

    def stat(u, k):
        return SM[:, (u % 2) * 32 + 4 * k:(u % 2) * 32 + 4 * k + 4]

    def ps_scores(u):
        b = 2 * (u % 2)
        return g.PSf[:, b * 512:b * 512 + 1024].rearrange("p (g w) -> p g w", w=256)
    with nc.Block() as block:
        @block.tensor
        def _(pe):
            def scores(u):
                if u >= 2:
                    pe.wait_ge(exped.sem, exped.at(u - 1))
                units[u].scores(pe, ps_scores(u)).then_inc(scored.sem, 1)

            def turn(u):
                pe.wait_ge(normed.sem, normed.at(u + 1))
                if u >= 1:
                    pe.wait_ge(pt_ready.sem, pt_ready.at(u))
                x = units[u]
                for kt, (a, m) in enumerate(x.keys):
                    for q in range(x.G):
                        last = pe.transpose(PS[0:m, 4 + kt, q * P:q * P + x.rows], probs(u)[0:x.rows, q, a:a + m], g.IDENT[0:x.rows, 0:x.rows])
                last.then_inc(turned.sem, 1)

            def outputs(u):
                pe.wait_ge(pt_ready.sem, pt_ready.at(u + 1))
                x = units[u]
                if x.first and outs[u] - x.last >= 2:
                    pe.wait_ge(out_taken.sem, out_taken.at(outs[u] - x.last - 1))
                x.outputs(pe, turned_probs(u), 6 + x.bank).then_inc(out_ready.sem, 1)
            scores(0)
            for u in range(n):
                if u + 1 < n:
                    scores(u + 1)
                turn(u)
                if u:
                    outputs(u - 1)
            outputs(n - 1)

        @block.vector
        def _(dve):
            def peak(u):
                x = units[u]
                r = x.rows
                dve.wait_ge(scored.sem, scored.at(u + 1))
                s = ps_scores(u)[0:r, 0:x.G, 0:x.W]
                if x.mask is not None:
                    if u >= 2:
                        dve.wait_ge(turned.sem, turned.at(u - 1))
                    p = probs(u)[0:r, :, 0:x.W]
                    dve.tensor_tensor(p, s, x.mask, ALU.add).then_inc(dve_own.sem, 1)
                    dve.wait_ge(dve_own.sem, dve_own.next())
                    s = p
                mx, nm, df = stat(u, 0)[0:r, 0:x.G], stat(u, 1)[0:r, 0:x.G], stat(u, 2)[0:r, 0:x.G]
                dve.tensor_reduce(mx, s, AX.X, ALU.max).then_inc(dve_own.sem, 1)
                dve.wait_ge(dve_own.sem, dve_own.next())
                if x.sink is None:
                    last = dve.tensor_scalar(nm, mx, -scale, None, ALU.mult)
                else:
                    dve.scalar_tensor_tensor(nm, mx, -scale, x.sink, ALU.mult, ALU.min).then_inc(dve_own.sem, 1)
                    dve.wait_ge(dve_own.sem, dve_own.next())
                    last = dve.tensor_tensor(df, nm, x.sink, ALU.subtract)
                last.then_inc(peaked.sem, 1)

            def norm(u):
                x = units[u]
                r = x.rows
                dve.wait_ge(exped.sem, exped.at(u + 1))
                es, l, inv = (stat(u, k)[0:r, 0:x.G] for k in (3, 4, 5))
                if x.sink is not None:
                    dve.tensor_tensor(l, l, es, ALU.add).then_inc(dve_own.sem, 1)
                    dve.wait_ge(dve_own.sem, dve_own.next())
                dve.reciprocal(inv, l).then_inc(dve_own.sem, 1)
                dve.wait_ge(dve_own.sem, dve_own.next())
                p = probs(u)[0:r, :, 0:x.W]
                dve.tensor_tensor(p, p, inv.unsqueeze(2).to_broadcast([r, x.G, x.W]), ALU.mult).then_inc(normed.sem, 1)
            peak(0)
            for u in range(n):
                if u + 1 < n:
                    peak(u + 1)
                norm(u)

        @block.scalar
        def _(act):
            def place(u):
                if units[u].last:
                    act.wait_ge(out_ready.sem, out_ready.at(u + 1))
                    units[u].place(act, 6 + units[u].bank).then_inc(out_taken.sem, 1)
            for u in range(n + 2):
                if u < n:
                    x = units[u]
                    r = x.rows
                    act.wait_ge(peaked.sem, peaked.at(u + 1))
                    if u >= 2:
                        act.wait_ge(turned.sem, turned.at(u - 1))
                    for q in range(x.G):
                        src = ps_scores(u)[0:r, q, 0:x.W] if x.mask is None else probs(u)[0:r, q, 0:x.W]
                        last = act.activation(probs(u)[0:r, q, 0:x.W], src, ACT.Exp, bias=stat(u, 1)[0:r, q:q + 1], scale=scale,
                                              accum_out=stat(u, 4)[0:r, q:q + 1])
                    if x.sink is not None:
                        last = act.activation(stat(u, 3)[0:r, 0:x.G], stat(u, 2)[0:r, 0:x.G], ACT.Exp)
                    last.then_inc(exped.sem, 1)
                if 1 <= u <= n:
                    v = u - 1
                    act.wait_ge(turned.sem, turned.at(v + 1))
                    if v >= 2:
                        act.wait_ge(out_ready.sem, out_ready.at(v - 1))
                    x = units[v]
                    for kt, (a, m) in enumerate(x.keys):
                        w = x.G * P if x.G > 1 else x.rows
                        last = act.activation(turned_probs(v)[0:m, kt].rearrange("p a b -> p (a b)")[:, 0:w], PS[0:m, 4 + kt, 0:w], ACT.Copy)
                    last.then_inc(pt_ready.sem, 1)
                if u >= 2:
                    place(u - 2)
    for c in (scored, peaked, exped, normed, turned, pt_ready, out_ready):
        c.adds(n)
    out_taken.adds(outs[-1])


class Unit:
    def __init__(self, rows, G, W, keys, scores, outputs, place, bank, first=True, last=True, mask=None, sink=None):
        self.rows, self.G, self.W, self.keys, self.scores, self.outputs, self.place = rows, G, W, keys, scores, outputs, place
        self.bank, self.first, self.last, self.mask, self.sink = bank, first, last, mask, sink


def _memory(nc, io, env, run, l):
    g = env
    H, OT, R, Rf, Hf, OTf, view, COL = g.H, g.OT, g.R, g.Rf, g.Hf, g.OTf, g.view, g.COL
    MT, MK, MV = view(Rf, 0, KT, MEM), view(Rf, 2048, HEADS, MEM), view(Rf, 3072, 2, 512)
    Q = R[:, 4:8, :]
    QZ = view(Rf, 8 * T, 16, P)
    KC, VC = view(OTf, 4 * T, 4, HEADS, MEM), view(Hf, 4096, 4, 2, 512)
    w_kv = io["mem_w_kv"][l]
    run(g.load, [(MT, io["memT"].rearrange("(k p) m -> p k m", p=P)), (COL[:, 8:9], io["mem_knorm_g"][l]), (COL[:, 9:10], io["mem_qnorm_g"][l])])

    def keys_out(eng, tile, bank):
        return eng.activation(MK[:, bass.ds(tile, 1), :].rearrange("p a b -> p (a b)"), g.PS[:, bank, 0:MEM], ACT.Copy)
    run(g.project, w_kv[:, 0:512], MT, KT, 2, keys_out, spans=((0, MEM),))
    run(g.project_tokens, w_kv[:, 512:1024], MT, KT, 2, g.to_rows(MV, ACT.Copy), toks=TOK[0:2])
    run(g.tile_norm, [MK[:, h, :] for h in range(4)], [MK[:, h, :] for h in range(4)], g.ONES128[:, :], [COL[:, 8:9]] * 4,
        [OT[:, 4 + i, 0:MEM] for i in range(4)], width=MEM)
    run(g.rms_norm, 1)
    run(g.project, io["mem_w_q"][l], H, KT, 2, g.to_tiles(R, 4, ACT.Copy))
    run(g.tile_norm, [Q[:, h, :] for h in range(4)], [Q[:, h, :] for h in range(4)], g.ONES128[:, :], [COL[:, 9:10]] * 4,
        [OT[:, 4 + i, :] for i in range(4)])

    def caches(bt):
        b = slice(4 * bt, 4 * bt + 4)
        return [(KC.rearrange("p b h m -> p (b h) m"), io["cache_mem_kT"][l, b].rearrange("b h d m -> d (b h) m")),
                (VC.rearrange("p b k n -> p (b k) n"), io["cache_mem_v"][l, b].rearrange("b (k p) n -> p (b k) n", p=P))]
    run(g.load, caches(0), zero=(QZ,))

    def prompt_unit(j):
        a = j * P

        def scores(pe, ps):
            for h in range(HEADS):
                last = pe.matmul(ps[:, h, :], Q[:, h, a:a + P], MK[:, h, :], start=True, stop=True)
            return last

        def outputs(pe, pt, bank):
            for h in range(HEADS):
                for kt in range(2):
                    last = pe.matmul(g.PS[:, bank, h * P:(h + 1) * P], MV[:, kt, h * P:(h + 1) * P], pt[:, kt, h, :], start=(kt == 0), stop=(kt == 1))
            return last

        def place(act, bank):
            return act.activation(OT[:, 0:4, a:a + P], g.PS[:, bank, :].rearrange("p (h n) -> p h n", n=P), ACT.Copy)
        return Unit(P, HEADS, MEM, [(0, P), (P, P)], scores, outputs, place, j % 2)

    def sample_unit(bt, bank):
        def scores(pe, ps):
            for i in range(16):
                last = pe.matmul(ps[:, 0, :], QZ[:, i, :], KC[:, i // 4, i % 4, :], start=(i == 0), stop=(i == 15))
            return last

        def outputs(pe, pt, bank):
            for i in range(16):
                for kt in range(2):
                    last = pe.matmul(g.PS[:, bank, i * NS:(i + 1) * NS], VC[:, i // 4, kt, (i % 4) * P:(i % 4 + 1) * P],
                                     pt[:, kt, 0, i * NS:(i + 1) * NS], start=(kt == 0), stop=(kt == 1))
            return last

        def place(act, bank):
            a = SEQ + bt * 32
            return act.activation(OT[:, 0:4, a:a + 32].rearrange("p h (b t) -> p h b t", t=NS),
                                  g.PS[:, bank, 0:P].rearrange("p (b h t) -> p h b t", h=4, t=NS), ACT.Copy)
        return Unit(P, 1, MEM, [(0, P), (P, P)], scores, outputs, place, bank)

    def spread_queries(bt):
        spread = g.count("queries_spread")
        with nc.Block() as block:
            @block.vector
            def _(dve):
                for b in range(4):
                    src = Q[:, :, SEQ + (bt * 4 + b) * NS:SEQ + (bt * 4 + b + 1) * NS]
                    flat = QZ.rearrange("p a b -> p (a b)")
                    at = 4 * b * (P + NS)
                    dst = flat[:, at:at + 4 * (P + NS)].rearrange("p (h x) -> p h x", x=P + NS)[:, :, 0:NS] if b < 3 else None
                    if dst is None:
                        for h in range(4):
                            dve.tensor_copy(QZ[:, 4 * b + h, (4 * b + h) * NS:(4 * b + h + 1) * NS], src[:, h, :])
                    else:
                        dve.tensor_copy(dst, src)
    run(spread_queries, 0)
    run(_attend, nc, g, [prompt_unit(j) for j in range(NBLK)] + [sample_unit(0, 0)], HD_X ** -0.5, 2)
    run(g.load, caches(1))
    run(spread_queries, 1)
    run(_attend, nc, g, [sample_unit(1, 0)], HD_X ** -0.5, 2)

    def keep_memory():
        with nc.Block() as block:
            @block.sync
            def _(sp):
                g.store(sp, io["mem_kT_prompt"][l].rearrange("h d m -> d h m"), MK)
                g.store(sp, io["mem_v_prompt"][l].rearrange("(k p) n -> p k n", p=P), MV)
                sp.wait_ge(g.stored.sem, g.stored.at(g.stores[0]))
    run(keep_memory)
    run(g.project, io["mem_w_o"][l], OT, 4, 4, g.to_residual, on="vector")


HD_X = 128


def _feed_forward(nc, io, env, run, l):
    g = env
    X, H, OT, R, OTf, PS, view, count, dve_own, act_own = g.X, g.H, g.OT, g.R, g.OTf, g.PS, g.view, g.count, g.dve_own, g.act_own
    GW = 2 + SEQ + NB * (2 + NS)
    GATE = [OTf[:, i * GW:(i + 1) * GW] for i in range(2)]
    CONV = [OTf[:, 2 * GW + i * T:2 * GW + (i + 1) * T] for i in range(2)]
    at = 2 * GW + 2 * T
    PAST = view(OTf, at, FT, NB * 2)
    TAPS = view(OTf, at + FT * 16, FT, 4)
    KEEP = view(OTf, at + FT * 20, FT, 18)
    run(g.rms_norm, 2)
    run(g.load, [(PAST, io["conv_past"][l]), (TAPS, io["conv_taps"][l])], zero=tuple(x[:, 0:2] for x in GATE))
    wg, wu = (io[n][l].rearrange("(k p) n -> p k n", p=P) for n in ("ffn_w_gate", "ffn_w_up"))

    def hidden(first, pairs):
        gate_full, up_full, gate_copied, convolved, gelued, made = (count("ff_" + n) for n in (
            "gate_full", "up_full", "gate_copied", "convolved", "gelued", "made"))
        with nc.Block() as block:
            @block.sync
            def _(sp):
                with sp.Fori(0, pairs) as i:
                    for s, (w, full) in enumerate(((wg, gate_full), (wu, up_full))):
                        sp.wait_ge(full.sem, full.at(i * 2))
                        sp.dma_start(g.w_slot(s, KT, CH), w[:, :, bass.ds(i * CH + first * P, CH)]).then_inc(g.w_loaded[s].sem, 16)

            @block.tensor
            def _(pe):
                with pe.Fori(0, pairs) as i:
                    for t in range(2):
                        for s, (full, taken) in enumerate(((gate_full, gate_copied), (up_full, made))):
                            if t == 0:
                                pe.wait_ge(g.w_loaded[s].sem, g.w_loaded[s].at(i * 16 + 16))
                            pe.wait_ge(taken.sem, taken.at(i * 2 + t))
                            ws = g.w_slot(s, KT, CH)
                            for n, (a, m) in enumerate(SPANS):
                                for k in range(KT):
                                    last = pe.matmul(PS[:, 3 * s + n, 0:m], ws[:, k, t * P:(t + 1) * P], H[:, k, a:a + m], start=(k == 0), stop=(k == KT - 1))
                            last.then_inc(full.sem, 1)

            @block.scalar
            def _(act):
                with act.Fori(0, pairs) as i:
                    for t in range(2):
                        G = GATE[t]
                        act.wait_ge(gate_full.sem, gate_full.at(i * 2 + t + 1))
                        act.wait_ge(convolved.sem, convolved.at(i * 2 + (t - 1)))
                        act.activation(G[:, 2:770].rearrange("p (r b) -> p r b", r=2), PS[:, 0:2, 0:384], ACT.Copy)
                        act.activation(G[:, 770:2 + SEQ], PS[:, 2, 0:256], ACT.Copy)
                        act.activation(G[:, 2 + SEQ:GW].rearrange("p (b t) -> p b t", t=2 + NS)[:, :, 2:2 + NS],
                                       PS[:, 2, 256:320].rearrange("p (b t) -> p b t", t=NS), ACT.Copy).then_inc(gate_copied.sem, 1)
                        act.wait_ge(convolved.sem, convolved.at(i * 2 + (t + 1)))
                        act.activation(CONV[t], CONV[t], ACT.Gelu).then_inc(gelued.sem, 1)

            @block.vector
            def _(dve):
                with dve.Fori(0, pairs) as i:
                    dve_own.enter(i, 2 * 3)
                    for t in range(2):
                        G, C = GATE[t], CONV[t]
                        f = i * 2 + (first + t)

                        def tap(k):
                            return TAPS[:, bass.ds(f, 1), k:k + 1].rearrange("p a b -> p (a b)")
                        SG = G[:, 2 + SEQ:GW].rearrange("p (b t) -> p b t", t=2 + NS)
                        SC = C[:, SEQ:T].rearrange("p (b t) -> p b t", t=NS)
                        dve.tensor_copy(SG[:, :, 0:2], PAST[:, bass.ds(f, 1), :].rearrange("p a (b t) -> p (a b) t", t=2)).then_inc(dve_own.sem, 1)
                        dve_own.next()
                        dve.wait_ge(gate_copied.sem, gate_copied.at(i * 2 + (t + 1)))
                        dve.wait_ge(dve_own.sem, dve_own.now())
                        dve.tensor_scalar(C[:, 0:SEQ], G[:, 0:SEQ], tap(0), tap(3), ALU.mult, ALU.add)
                        dve.tensor_scalar(SC, SG[:, :, 0:NS], tap(0), tap(3), ALU.mult, ALU.add).then_inc(dve_own.sem, 1)
                        dve.wait_ge(dve_own.sem, dve_own.next())
                        dve.scalar_tensor_tensor(C[:, 0:SEQ], G[:, 1:1 + SEQ], tap(1), C[:, 0:SEQ], ALU.mult, ALU.add)
                        dve.scalar_tensor_tensor(SC, SG[:, :, 1:1 + NS], tap(1), SC, ALU.mult, ALU.add).then_inc(dve_own.sem, 1)
                        dve.wait_ge(dve_own.sem, dve_own.next())
                        dve.scalar_tensor_tensor(C[:, 0:SEQ], G[:, 2:2 + SEQ], tap(2), C[:, 0:SEQ], ALU.mult, ALU.add)
                        dve.scalar_tensor_tensor(SC, SG[:, :, 2:2 + NS], tap(2), SC, ALU.mult, ALU.add)
                        keep = KEEP[:, bass.ds(f, 1), :].rearrange("p a b -> p (a b)")
                        dve.tensor_copy(keep[:, 0:2], G[:, SEQ:SEQ + 2])
                        dve.tensor_copy(keep[:, 2:18].rearrange("p (b t) -> p b t", t=2), SG[:, :, NS:NS + 2]).then_inc(convolved.sem, 1)
                        dve.wait_ge(gelued.sem, gelued.at(i * 2 + (t + 1)))
                        dve.wait_ge(up_full.sem, up_full.at(i * 2 + (t + 1)))
                        for ps, a, m, rows in g.pieces(3):
                            c = C[:, a:a + m].rearrange("p (r b) -> p r b", r=rows) if rows > 1 else C[:, a:a + m]
                            last = dve.tensor_tensor(g.cut(R, i * 2 + t, a, m, rows), ps, c, ALU.mult)
                        last.then_inc(made.sem, 1)
                dve_own.leave(pairs)
        for c in (gate_full, up_full, gate_copied, convolved, gelued, made):
            c.adds(2 * pairs)
        for s in range(2):
            g.w_loaded[s].adds(16 * pairs)

    def keep_gate():
        with nc.Block() as block:
            @block.sync
            def _(sp):
                g.store(sp, io["ffn_conv"][l], KEEP)
                sp.wait_ge(g.stored.sem, g.stored.at(g.stores[0]))
    if l == 0:
        prime_feed_forward(nc, g)
    for first, tiles in ((0, 12), (12, 10)):
        run(hidden, first, tiles // 2)
        run(g.project, io["ffn_w_down"][l, first * P:(first + tiles) * P, :], R, tiles, 8, g.to_residual, on="vector", cols=P)
    run(keep_gate)


def prime_feed_forward(nc, g):
    looked_back = [g.count("ff_" + n) for n in ("gate_full", "up_full", "gate_copied", "convolved", "made")]
    with nc.Block() as block:
        @block.vector
        def _(dve):
            for c in looked_back:
                dve.sem_inc(c.sem, FIRST)
    for c in looked_back:
        c.adds(FIRST)


def _layer1(nc, io, env, run):
    g = env
    X, H, OT, R, Rf, Hf, OTf, PS, PSf, view, count = g.X, g.H, g.OT, g.R, g.Rf, g.Hf, g.OTf, g.PS, g.PSf, g.view, g.count
    MASK, COS, SIN, COL, SM, IDENT, SPARE = g.MASK, g.COS, g.SIN, g.COL, g.SM, g.IDENT, g.SPARE
    act_own, dve_own = g.act_own, g.dve_own
    IC = view(Rf, 8 * T, 9, 512)
    LMASK = view(MASK[:, :], 0, LEVELS + 1, P)
    RESET = SPARE[:, 0, :]
    w_in = io["od_w_in"]
    WSf = [w[:, :] for w in g.WS]
    run(g.load, [(g.GAIN[:, :], io["gain1"]), (MASK[:, 0:1024], io["hgrn_masks"]), (RESET, io["hgrn_reset"]),
                 (COL[:, 12:16], io["hgrn_onorm_g"]), (COL[:, 16:24], io["hgrn_lb_logits"])])

    def lower_bound():
        peaked, exped = count("lb_peaked"), count("lb_exped")
        a, b, m = COL[:, 16:20], COL[:, 20:24], COL[:, 24:28]
        with nc.Block() as block:
            @block.vector
            def _(dve):
                dve.tensor_tensor(m, a, b, ALU.max).then_inc(dve_own.sem, 1)
                dve.wait_ge(dve_own.sem, dve_own.next())
                dve.tensor_tensor(a, a, m, ALU.subtract)
                dve.tensor_tensor(b, b, m, ALU.subtract).then_inc(peaked.sem, 1)
                dve.wait_ge(exped.sem, exped.at(1))
                dve.tensor_tensor(m, a, b, ALU.add).then_inc(dve_own.sem, 1)
                dve.wait_ge(dve_own.sem, dve_own.next())
                dve.reciprocal(m, m).then_inc(dve_own.sem, 1)
                dve.wait_ge(dve_own.sem, dve_own.next())
                dve.tensor_tensor(b, b, m, ALU.mult).then_inc(dve_own.sem, 1)
                dve.wait_ge(dve_own.sem, dve_own.next())
                dve.tensor_scalar(a, b, -1.0, 1.0, ALU.mult, ALU.add)

            @block.scalar
            def _(act):
                act.wait_ge(peaked.sem, peaked.at(1))
                act.activation(COL[:, 16:24], COL[:, 16:24], ACT.Exp).then_inc(exped.sem, 1)
        peaked.adds(1)
        exped.adds(1)
    run(lower_bound)
    run(g.rms_norm, 0)
    run(g.project, w_in[:, 0:512], H, KT, 2, g.to_tiles(R, 0, ACT.Silu))
    run(g.project, w_in[:, 512:1024], H, KT, 2, g.to_tiles(R, 4, ACT.Sigmoid))
    run(g.project_tokens, w_in[:, 1024:1536], H, KT, 2, g.to_rows(IC, ACT.Copy))

    def hgrn(h):
        q, k = R[:, h, :], R[:, 4 + h, :]
        B, LG = OT[:, 4, :], OT[:, 5, :]
        A = WSf[0][:, 0:T]
        KTS = WSf[0][:, T:T + P]
        CHAIN, S0 = view(WSf[1], 0, NBLK, P), view(WSf[1], 1024, NB, P)
        KTK = view(COS[:, :], 0, NBLK, P)
        VBD = view(SIN[:, :], 0, NB, P)
        E = [OT[:, 5, :], OT[:, 7, :]]
        QE = [OT[:, 6, :], SPARE[:, 1, :]]
        logged, forgot, summed = (count("hg_" + n) for n in ("logged", "forgot", "summed"))
        offset, decayed, paired, scored, masked = (count("hg_" + n) for n in ("offset", "decayed", "paired", "scored", "masked"))
        lo = COL[:, 16 + h:17 + h]
        bound = COL[:, 20 + h:21 + h]

        def blocks(v, lv, flat=False):
            s2 = 2 ** lv
            n = T if s2 <= NS else SEQ
            return v[:, 0:n].rearrange("p (b t) -> p b t", t=s2), n

        def intra():
            with nc.Block() as block:
                @block.vector
                def _(dve):
                    dve.tensor_scalar(k, k, lo, bound, ALU.mult, ALU.add).then_inc(dve_own.sem, 1)
                    dve.wait_ge(dve_own.sem, dve_own.next())
                    dve.tensor_scalar(LG, k, 2.0 ** -64, None, ALU.max).then_inc(forgot.sem, 1)
                    dve.tensor_scalar(k, k, -1.0, 1.0, ALU.mult, ALU.add).then_inc(dve_own.sem, 1)
                    dve.wait_ge(dve_own.sem, dve_own.next())
                    dve.wait_ge(logged.sem, logged.at(1))
                    dve.tensor_tensor_scan(B, RESET, LG, 0.0, ALU.mult, ALU.add).then_inc(summed.sem, 1)
                    dve.wait_ge(summed.sem, summed.at(1))

                    def offsets(lv):
                        if lv > 2:
                            dve.wait_ge(scored.sem, scored.at(lv - 1))
                        bb, n = blocks(B, lv)
                        e, _ = blocks(E[lv % 2], lv)
                        mid = bb[:, :, 2 ** (lv - 1) - 1:2 ** (lv - 1)]
                        dve.tensor_tensor(e, bb, mid.to_broadcast(list(bb.shape)), ALU.subtract).then_inc(offset.sem, 1)

                    def pair(lv):
                        n = blocks(B, lv)[1]
                        dve.wait_ge(decayed.sem, decayed.at(lv))
                        e, x = E[lv % 2][:, 0:n], QE[lv % 2][:, 0:n]
                        dve.tensor_tensor(x, e, q[:, 0:n], ALU.mult)
                        dve.tensor_tensor(e, e, k[:, 0:n], ALU.mult).then_inc(paired.sem, 1)

                    def gather(lv):
                        dve.wait_ge(scored.sem, scored.at(lv + 1))
                        n = SEQ if lv and 2 ** lv > NS else T
                        b = 3 * (lv % 2)
                        ps = PSf[:, b * 512:b * 512 + SEQ].rearrange("p (j n) -> p j n", n=P)
                        ps_s = PS[0:S, b + 2, 0:S]
                        a3 = A[:, 0:SEQ].rearrange("p (j n) -> p j n", n=P)
                        m = LMASK[:, lv, :].unsqueeze(1).to_broadcast([P, NBLK, P])
                        out, out_s = (a3, A[0:S, SEQ:T]) if lv == 0 else (ps, ps_s)
                        last = dve.tensor_tensor(out, ps, m, ALU.mult)
                        if n == T:
                            last = dve.tensor_tensor(out_s, ps_s, LMASK[0:S, lv, 0:S], ALU.mult)
                        if lv:
                            last.then_inc(dve_own.sem, 1)
                            dve.wait_ge(dve_own.sem, dve_own.next())
                            last = dve.tensor_tensor(a3, a3, ps, ALU.add)
                            if n == T:
                                last = dve.tensor_tensor(A[0:S, SEQ:T], A[0:S, SEQ:T], ps_s, ALU.add)
                        last.then_inc(masked.sem, 1)
                        dve.wait_ge(masked.sem, masked.at(lv + 1))
                    offsets(1)
                    for lv in range(1, LEVELS + 1):
                        if lv < LEVELS:
                            offsets(lv + 1)
                        pair(lv)
                        gather(lv - 1)
                    gather(LEVELS)

                @block.scalar
                def _(act):
                    act.wait_ge(forgot.sem, forgot.at(1))
                    act.activation(LG, LG, ACT.Ln).then_inc(logged.sem, 1)
                    for lv in range(1, LEVELS + 1):
                        act.wait_ge(offset.sem, offset.at(lv))
                        e = E[lv % 2][:, 0:blocks(B, lv)[1]]
                        act.activation(e, e, ACT.Abs).then_inc(act_own.sem, 1)
                        act.wait_ge(act_own.sem, act_own.next())
                        act.activation(e, e, ACT.Exp, scale=-1.0).then_inc(decayed.sem, 1)

                @block.tensor
                def _(pe):
                    pe.wait_ge(summed.sem, summed.at(1))
                    for lv in range(LEVELS + 1):
                        if lv:
                            pe.wait_ge(paired.sem, paired.at(lv))
                        if lv >= 2:
                            pe.wait_ge(masked.sem, masked.at(lv - 1))
                        qq, kk = (QE[lv % 2], E[lv % 2]) if lv else (q, k)
                        b = 3 * (lv % 2)
                        for j, (a, m) in enumerate(TOK if lv <= 3 else TOK[:-1]):
                            ps = PSf[0:m, b * 512 + j * P:b * 512 + j * P + m]
                            last = pe.matmul(ps, kk[:, a:a + m], qq[:, a:a + m], start=True, stop=True)
                        last.then_inc(scored.sem, 1)
            for c, n in ((logged, 1), (forgot, 1), (summed, 1), (offset, LEVELS), (decayed, LEVELS), (paired, LEVELS),
                         (scored, LEVELS + 1), (masked, LEVELS + 1)):
                c.adds(n)

        EB, QB, KB, DB = OT[:, 5, :], OT[:, 6, :], OT[:, 7, :], SPARE[:, 1, :]

        def inter():
            start, bexp, dexp, qkd, turned, turned_out, kv, chained, o_ready, vspread, s_in = (count("hgi_" + n) for n in (
                "start", "exp_b", "exp_rest", "decayed", "turned", "turned_taken", "kv", "chained", "out", "spread", "updated"))
            v = IC[:, :, h * P:(h + 1) * P]
            with nc.Block() as block:
                @block.sync
                def _(sp):
                    sp.dma_start(S0, io["state_hgrn"].rearrange("b h k v -> h k b v")[h]).then_inc(g.loaded.sem, 16)
                    sp.wait_ge(g.loaded.sem, g.loaded.at(16))
                    sp.wait_ge(chained.sem, chained.at(NBLK))
                    g.store(sp, io["hgrn_state_prompt"][h], CHAIN[:, NBLK - 1, :])
                    sp.wait_ge(s_in.sem, s_in.at(2))
                    g.store(sp, io["hgrn_state_sample"].rearrange("b h k v -> h k b v")[h], S0)
                    sp.wait_ge(g.stored.sem, g.stored.at(g.stores[0]))

                @block.vector
                def _(dve):
                    b3, d3 = (x[:, 0:SEQ].rearrange("p (j n) -> p j n", n=P) for x in (B, DB))
                    dve.tensor_tensor(d3, b3, b3[:, :, P - 1:P].to_broadcast([P, NBLK, P]), ALU.subtract)
                    b3, d3 = (x[:, SEQ:T].rearrange("p (j n) -> p j n", n=NS) for x in (B, DB))
                    dve.tensor_tensor(d3, b3, b3[:, :, NS - 1:NS].to_broadcast([P, NB, NS]), ALU.subtract).then_inc(start.sem, 1)
                    dve.tensor_tensor(VBD[0:S], v[0:S, 8, :].unsqueeze(1).to_broadcast([S, NB, P]),
                                      io_onehot[0:S].unsqueeze(2).to_broadcast([S, NB, P]), ALU.mult).then_inc(vspread.sem, 1)
                    dve.wait_ge(bexp.sem, bexp.at(1))
                    dve.tensor_tensor(QB, q, EB, ALU.mult)
                    dve.wait_ge(dexp.sem, dexp.at(1))
                    dve.tensor_tensor(KB, k, DB, ALU.mult).then_inc(qkd.sem, 1)
                    dve.wait_ge(kv.sem, kv.at(1))
                    for j in range(NBLK):
                        ps = PSf[:, 4 * 512 + j * P:4 * 512 + (j + 1) * P]
                        if j == 0:
                            last = dve.tensor_copy(CHAIN[:, 0, :], ps)
                        else:
                            last = dve.scalar_tensor_tensor(CHAIN[:, j, :], CHAIN[:, j - 1, :], EB[:, (j + 1) * P - 1:(j + 1) * P], ps, ALU.mult, ALU.add)
                        last.then_inc(chained.sem, 1)
                        dve.wait_ge(chained.sem, chained.at(j + 1))
                    dve.wait_ge(g.loaded.sem, g.loaded.at(16))
                    ends = EB[:, SEQ:T].rearrange("p (b t) -> p b t", t=NS)[:, :, NS - 1:NS].to_broadcast([P, NB, P])
                    dve.wait_ge(o_ready.sem, o_ready.at(1))
                    dve.tensor_tensor(S0, S0, ends, ALU.mult).then_inc(dve_own.sem, 1)
                    dve.wait_ge(dve_own.sem, dve_own.next())
                    dve.wait_ge(kv.sem, kv.at(2))
                    for c in range(2):
                        s = S0[:, 4 * c:4 * c + 4, :]
                        dve.tensor_tensor(s, s, PS[:, 6 + c, :].rearrange("p (b v) -> p b v", v=P), ALU.add).then_inc(s_in.sem, 1)

                @block.scalar
                def _(act):
                    act.activation(EB, B, ACT.Exp).then_inc(bexp.sem, 1)
                    act.wait_ge(start.sem, start.at(1))
                    act.activation(DB, DB, ACT.Exp, scale=-1.0).then_inc(dexp.sem, 1)
                    act.wait_ge(turned.sem, turned.at(1))
                    act.activation(KTK, PSf[:, 0:SEQ].rearrange("p (j n) -> p j n", n=P), ACT.Copy)
                    act.activation(KTS[0:S, :], PS[0:S, 2, 0:P], ACT.Copy).then_inc(turned_out.sem, 1)
                    act.wait_ge(o_ready.sem, o_ready.at(1))
                    act.activation(OT[:, h, 0:SEQ], PSf[:, 0:SEQ], ACT.Copy)
                    act.activation(OT[:, h, SEQ:T], PS[:, 2, 0:S], ACT.Copy)

                @block.tensor
                def _(pe):
                    pe.wait_ge(qkd.sem, qkd.at(1))
                    for j, (a, m) in enumerate(TOK):
                        last = pe.transpose(PSf[0:m, j * P:(j + 1) * P], KB[:, a:a + m], IDENT[:, :])
                    last.then_inc(turned.sem, 1)
                    pe.wait_ge(turned_out.sem, turned_out.at(1))
                    for j in range(NBLK):
                        last = pe.matmul(PSf[:, 4 * 512 + j * P:4 * 512 + (j + 1) * P], KTK[:, j, :], v[:, j, :], start=True, stop=True)
                    last.then_inc(kv.sem, 1)
                    pe.wait_ge(vspread.sem, vspread.at(1))
                    for c in range(2):
                        last = pe.matmul(PS[:, 6 + c, :], KTS[0:S, :], VBD[0:S, 4 * c:4 * c + 4, :].rearrange("p a b -> p (a b)"), start=True, stop=True)
                    last.then_inc(kv.sem, 1)
                    for j, (a, m) in enumerate(TOK):
                        o = PSf[:, j * P:j * P + m]
                        if j and j < NBLK:
                            pe.wait_ge(chained.sem, chained.at(j))
                        last = pe.matmul(o, v[0:m, j, :], A[0:m, a:a + m], start=True, stop=(j == 0 or j == NBLK))
                        if j == NBLK:
                            pe.wait_ge(g.loaded.sem, g.loaded.at(16))
                            for b in range(NB):
                                last = pe.matmul(PS[:, 2, b * NS:(b + 1) * NS], S0[:, b, :], QB[:, SEQ + b * NS:SEQ + (b + 1) * NS],
                                                 start=False, stop=True, skip_group_check=True)
                        elif j:
                            last = pe.matmul(o, CHAIN[:, j - 1, :], QB[:, a:a + m], start=False, stop=True)
                    last.then_inc(o_ready.sem, 1)
            g.loaded.adds(16)
            for c, n in ((start, 1), (bexp, 1), (dexp, 1), (qkd, 1), (turned, 1), (turned_out, 1), (kv, 2), (chained, NBLK),
                         (o_ready, 1), (vspread, 1), (s_in, 2)):
                c.adds(n)
        run(intra)
        run(inter)
    io_onehot = COL[:, 28:36]
    run(g.load, [(io_onehot, io["onehot"])])
    for h in range(HEADS):
        hgrn(h)
    run(g.tile_norm, [OT[:, h, :] for h in range(4)], [OT[:, h, :] for h in range(4)], g.ONES128[:, :],
        [COL[:, 12 + h:13 + h] for h in range(4)], [OT[:, 4 + i, :] for i in range(4)])

    def gate_out(act, tile, bank):
        for ps, a, m, rows in g.pieces(bank):
            last = act.activation(g.cut(OT, tile + 4, a, m, rows), ps, ACT.Silu)
        return last
    run(g.project, w_in[:, 1536:2048], H, KT, 2, gate_out)

    def apply_gate():
        with nc.Block() as block:
            @block.vector
            def _(dve):
                for t in range(4):
                    dve.tensor_tensor(OT[:, t, :], OT[:, t, :], OT[:, 4 + t, :], ALU.mult)
    run(apply_gate)

    KD = R[:, 0, :]
    VD = view(Rf, T, 9, 2, P)
    KC, VC = view(Rf, T + 2304, NB, WIN), view(Rf, T + 3328, NB, 2, P)
    QZ, QC = view(Rf, T + 5376, 2, 4, P), view(Rf, T + 6400, 2, P)
    BAND, SMASK = view(MASK[:, :], 0, MEM), view(MASK[:, :], MEM, 2, 192)
    SINK, SINKR = COL[:, 40:48], COL[:, 48:50]
    halves = [(slice(0, 64), 0, slice(0, 64)), (slice(64, 128), 1, slice(64, 128))]
    run(g.load, [(g.ROT[:, :], io["swa_rot"]), (COS[:, :], io["swa_cos"]), (SIN[:, :], io["swa_sin"]), (MASK[:, 0:640], io["swa_masks"]),
                 (COL[:, 36:37], io["swa_qnorm_g"]), (COL[:, 37:38], io["swa_knorm_g"]), (SINK, io["swa_sinks"].partition_broadcast(P)),
                 (SINKR, io["swa_sinks_rows"]), (KC, io["cache_swa_kT"].rearrange("b d w -> d b w")),
                 (VC[:, :, 0, 0:64], io["cache_swa_v"][:, :, 0:64].rearrange("b w d -> w b d")),
                 (VC[:, :, 1, 64:128], io["cache_swa_v"][:, :, 64:128].rearrange("b w d -> w b d"))],
        zero=(VC[:, :, 0, 64:128], VC[:, :, 1, 0:64], VD[:, :, 0, 64:128], VD[:, :, 1, 0:64], QZ))
    run(g.project, w_in[:, 2048:2560], H, KT, 2, g.to_tiles(OT, 4, ACT.Copy))
    run(g.project, w_in[:, 2560:2688], H, KT, 1, g.to_tiles(R, 0, ACT.Copy), cols=P)

    def values(eng, c, n, m, ps):
        eng.activation(VD[0:m, n, 0, 0:64], ps[:, 0:64], ACT.Copy)
        return eng.activation(VD[0:m, n, 1, 64:128], ps[:, 64:128], ACT.Copy)
    run(g.project_tokens, w_in[:, 2688:2816], H, KT, 1, values, cols=P)
    qk = [OT[:, 4 + i, :] for i in range(4)] + [KD]
    run(g.tile_norm, qk, qk, g.ONES64[:, :], [COL[:, 36:37]] * 4 + [COL[:, 37:38]], [H[:, i, :] for i in range(4)])
    run(g.rotate, qk, H[:, 7, :])

    def spread_queries():
        with nc.Block() as block:
            @block.vector
            def _(dve):
                dve.tensor_scalar(COL[:, 40:50], COL[:, 40:50], -1.0, None, ALU.mult).then_inc(dve_own.sem, 1)
                dve.wait_ge(dve_own.sem, dve_own.next())
                for bt in range(2):
                    for b in range(4):
                        a = SEQ + (bt * 4 + b) * NS
                        src = OT[:, 4:8, a:a + NS]
                        dve.tensor_copy(QC[:, bt, b * 32:(b + 1) * 32].rearrange("p (i t) -> p i t", t=NS), src)
                        dve.tensor_copy(QZ[:, bt, b, b * 32:(b + 1) * 32].rearrange("p (i t) -> p i t", t=NS), src)
    run(spread_queries)

    def prompt_unit(j, s):
        a = j * P
        first = a if j == 0 else a - P
        W = a + P - first
        r = slice(64 * s, 64 * s + 64)

        def scores(pe, ps):
            for i in range(4):
                last = pe.matmul(ps[:, i, 0:W], OT[r, 4 + i, a:a + P], KD[r, first:first + W], start=True, stop=True)
            return last

        def outputs(pe, pt, bank):
            n = W // P
            for kt in range(n):
                last = pe.matmul(PS[:, bank, :], VD[:, first // P + kt, s, :], pt[:, kt, :, :].rearrange("p a b -> p (a b)"),
                                 start=(s == 0 and kt == 0), stop=(s == 1 and kt == n - 1), skip_group_check=True)
            return last

        def place(act, bank):
            return act.activation(OT[:, 4:8, a:a + P], PS[:, bank, :].rearrange("p (i n) -> p i n", n=P), ACT.Copy)
        mask = BAND[:, MEM - W:MEM].unsqueeze(1).to_broadcast([P, 4, W])
        return Unit(P, 4, W, [(x, P) for x in range(0, W, P)], scores, outputs, place, j % 2, s == 0, s == 1, mask, SINK[:, 4 * s:4 * s + 4])

    def sample_unit(bt, s):
        r = slice(64 * s, 64 * s + 64)

        def scores(pe, ps):
            for b in range(4):
                pe.matmul(ps[:, 0, 0:WIN], QZ[r, bt, b, :], KC[r, bt * 4 + b, :], start=(b == 0), stop=(b == 3))
            return pe.matmul(ps[:, 0, WIN:WIN + S], QC[r, bt, :], KD[r, SEQ:T], start=True, stop=True)

        def outputs(pe, pt, bank):
            pe.matmul(PS[:, bank, 0:P], VD[0:S, 8, s, :], pt[0:S, 1, 0, :], start=(s == 0), stop=True, skip_group_check=True)
            for b in range(4):
                last = pe.matmul(PS[:, bank, b * 32:(b + 1) * 32], VC[:, bt * 4 + b, s, :], pt[:, 0, 0, b * 32:(b + 1) * 32],
                                 start=False, stop=True, skip_group_check=True)
            return last

        def place(act, bank):
            a = SEQ + bt * 32
            return act.activation(OT[:, 4:8, a:a + 32].rearrange("p i (b t) -> p i b t", t=NS),
                                  PS[:, bank, 0:P].rearrange("p (b i t) -> p i b t", i=4, t=NS), ACT.Copy)
        return Unit(P, 1, WIN + S, [(0, WIN), (WIN, S)], scores, outputs, place, bt, s == 0, s == 1,
                    SMASK[:, bt, :].unsqueeze(1), SINKR[:, s:s + 1])
    run(_attend, nc, g, [prompt_unit(j, s) for j in range(NBLK) for s in range(2)] + [sample_unit(bt, s) for bt in range(2) for s in range(2)],
        64 ** -0.5, 2)

    def keep_window():
        with nc.Block() as block:
            @block.sync
            def _(sp):
                g.store(sp, io["swa_kT_prompt"], KD[:, SEQ - WIN:SEQ])
                g.store(sp, io["swa_kT_sample"][:, :, WIN - NS:WIN], KD[:, SEQ:T].rearrange("p (b t) -> p b t", t=NS))
                g.store(sp, io["swa_kT_sample"][:, :, 0:WIN - NS], KC[:, :, NS:WIN])
                for s in range(2):
                    c = slice(64 * s, 64 * s + 64)
                    g.store(sp, io["swa_v_prompt"][:, c], VD[:, NBLK - 1, s, c])
                    g.store(sp, io["swa_v_sample"][0:WIN - NS, :, c], VC[NS:WIN, :, s, c])
                    g.store(sp, io["swa_v_new"][:, c], VD[0:S, 8, s, c])
                sp.wait_ge(g.stored.sem, g.stored.at(g.stores[0]))
    run(keep_window)
    run(g.project, io["od_w_out"], OT, KT, 4, g.to_residual, on="vector")


def _rope_tables(heads, dim, rot, theta):
    half = rot // 2
    inv = (np.float32(theta) ** (-np.arange(half, dtype=np.float32) / np.float32(half))).astype(np.float32)
    pos = np.concatenate([np.arange(SEQ), np.tile(2048 + np.arange(NS), NB)]).astype(np.float32)
    ang = inv[:, None] * pos[None, :]
    cos, sin, perm = np.ones((P, T), np.float32), np.zeros((P, T), np.float32), np.zeros((P, P), np.float32)
    for h in range(heads):
        for i in range(half):
            a, b = h * dim + i, h * dim + half + i
            cos[a] = cos[b] = np.cos(ang[i])
            sin[a] = sin[b] = np.sin(ang[i])
            perm[b, a], perm[a, b] = -1.0, 1.0
    return cos, sin, perm


def _retention_tables():
    lg = np.log1p(-np.exp2(-5.0 - np.arange(HEADS)))
    out = np.zeros((P, 1320), np.float32)
    n = np.arange(P)
    rel = n[None, :] - n[:, None]
    for h in range(HEADS):
        out[:, h * P:(h + 1) * P] = np.where(rel >= 0, np.exp(rel * lg[h]), 0)
        same = (n[:S, None] // NS) == (n[None, :S] // NS)
        out[:S, 1024 + h * S:1024 + (h + 1) * S] = np.where(same & (rel[:S, :S] >= 0), np.exp(rel[:S, :S] * lg[h]), 0)
        out[:, 1296 + h] = np.exp((P - 1 - n) * lg[h])
        out[:, 1300 + h] = np.exp((NS - 1 - n % NS) * lg[h])
    for pr in range(2):
        for hh in range(2):
            r, h = slice(64 * hh, 64 * hh + 64), 2 * pr + hh
            out[r, 512 + pr * P:512 + (pr + 1) * P] = np.exp((n + 1) * lg[h])
            out[r, 1280 + pr * NS:1280 + (pr + 1) * NS] = np.exp((np.arange(NS) + 1) * lg[h])
            out[r, 768 + hh * P:768 + (hh + 1) * P] = 1
            out[r, 1304 + pr], out[r, 1306 + pr] = np.exp(P * lg[h]), np.exp(NS * lg[h])
    out[:, 1308:1316] = _onehot()
    return out


def _onehot():
    return (np.arange(P)[:, None] // NS == np.arange(NB)[None, :]).astype(np.float32)


def _hgrn_masks():
    n = np.arange(P)
    out = [np.eye(P, dtype=np.float32)]
    for lv in range(1, LEVELS + 1):
        w = 2 ** lv
        same = (n[:, None] // w) == (n[None, :] // w)
        out.append((same & (n[:, None] % w < w // 2) & (n[None, :] % w >= w // 2)).astype(np.float32))
    reset = np.ones((P, T), np.float32)
    reset[:, 0:SEQ:P] = 0
    reset[:, SEQ::NS] = 0
    return np.concatenate(out, 1), reset


def _window_masks():
    q, k = np.arange(P)[:, None], np.arange(2 * WIN)[None, :] - WIN
    band = np.where((k <= q) & (q - k < WIN), 0.0, -1e30)
    row = np.arange(P)
    b, t = row // 32, row % NS
    out = [band]
    for bt in range(2):
        key = np.arange(WIN)[None, :] - WIN
        cached = np.where(t[:, None] - key < WIN, 0.0, -1e30)
        s = np.arange(S)[None, :]
        new = np.where((s // NS == bt * 4 + b[:, None]) & (s % NS <= t[:, None]), 0.0, -1e30)
        out += [cached, new]
    return np.concatenate(out, 1).astype(np.float32)


def _columns(v, n):
    return v.reshape(n, P).T


def kernel(**inputs):
    import numpy as _np
    import concourse.bacc as _bacc
    from concourse.bass_utils import run_bass_kernel_spmd as _run

    x = {k: _np.asarray(v) for k, v in inputs.items()}
    cat, c32 = _np.concatenate, _np.ascontiguousarray
    ins = {}
    ins["xT"] = cat([x["x_prompt"][0], x["x_sample"].reshape(S, D)]).T
    ins["ident"] = _np.eye(P, dtype=_np.float32)
    for l in range(2):
        ins[f"gain{l}"] = cat([_columns(x[n][l], KT) for n in ("norm_mix_g", "norm_mem_g", "norm_ffn_g")], 1)
    ins["ret_cos"], ins["ret_sin"], ins["ret_rot"] = _rope_tables(2, 64, 64, 10000.0)
    ins["ret_tables"] = _retention_tables()
    ins["ret_gn_g"] = x["ret_gn_g"][0].T
    ins["ev_w_in"], ins["ev_w_out"] = x["ev_w_in"][0], x["ev_w_out"][0]
    ins["state_ret"] = x["state_ret"][0]
    ins["mlp_wT"] = x["mlp_w_s"][0].transpose(0, 2, 1)
    ins["mlp_wTs"] = _np.tile(x["mlp_w_s"][0].transpose(0, 2, 1)[:, :NS, :NS], (1, NB, NB))
    ins["mlp_b_s"] = x["mlp_b_s"][0]
    ins["mlp_norm_g"] = x["mlp_norm_g"][0].reshape(512)
    n = _np.arange(P)
    ins["tri"] = (n[:, None] <= n[None, :]).astype(_np.float32)
    ins["tri_s"] = ((n[:S, None] <= n[None, :S]) & (n[:S, None] // NS == n[None, :S] // NS)).astype(_np.float32)
    ins["memT"] = x["mem_prompt"][0].T
    for name in ("mem_w_kv", "mem_w_q", "mem_w_o", "ffn_w_gate", "ffn_w_up", "ffn_w_down"):
        ins[name] = x[name]
    ins["mem_knorm_g"], ins["mem_qnorm_g"] = x["mem_knorm_g"][:, :, None], x["mem_qnorm_g"][:, :, None]
    ins["cache_mem_kT"] = x["cache_mem_k"].transpose(0, 1, 3, 4, 2)
    ins["cache_mem_v"] = x["cache_mem_v"].reshape(2, NB, MEM, 512)
    past = x["state_ffn_conv"].reshape(2, NB, 2, FT, P)
    ins["conv_past"] = past.transpose(0, 4, 3, 1, 2).reshape(2, P, FT, NB * 2)
    taps = cat([x["ffn_conv_w"], x["ffn_conv_b"][:, None]], 1).reshape(2, 4, FT, P)
    ins["conv_taps"] = taps.transpose(0, 3, 2, 1)
    order = cat([_np.arange(64) + 64 * h for i in range(4) for h in (i, i + 4)])
    w = x["od_w_in"][0]
    ins["od_w_in"] = cat([w[:, :2048], w[:, 2048:2560][:, order], w[:, 2560:]], 1)
    w = x["od_w_out"][0]
    ins["od_w_out"] = cat([w[:512], w[512:][order]])
    ins["state_hgrn"] = x["state_hgrn"][0]
    ins["hgrn_masks"], ins["hgrn_reset"] = _hgrn_masks()
    ins["hgrn_onorm_g"] = x["hgrn_onorm_g"][0].T
    ins["hgrn_lb_logits"] = cat([_columns(x["hgrn_lb_logits"][l], HEADS) for l in range(2)], 1)
    ins["onehot"] = _onehot()
    ins["swa_cos"], ins["swa_sin"], ins["swa_rot"] = _rope_tables(2, 64, 16, 500000.0)
    ins["swa_masks"] = _window_masks()
    ins["swa_qnorm_g"], ins["swa_knorm_g"] = (_np.tile(x[k][0], 2)[:, None] for k in ("swa_qnorm_g", "swa_knorm_g"))
    ins["swa_sinks"] = x["swa_sinks"][0]
    ins["swa_sinks_rows"] = _np.tile(_np.repeat(x["swa_sinks"][0].reshape(2, 4), NS, 1), (1, 4)).T
    ins["cache_swa_kT"] = x["cache_swa_k"][0].reshape(NB, WIN, P).transpose(0, 2, 1)
    ins["cache_swa_v"] = x["cache_swa_v"][0].reshape(NB, WIN, P)
    outs = {
        "yT": (D, T), "ret_state_prompt": (HEADS, DK_A, P), "hgrn_state_prompt": (HEADS, P, P), "swa_kT_prompt": (P, WIN),
        "swa_v_prompt": (WIN, P), "mem_kT_prompt": (2, HEADS, P, MEM), "mem_v_prompt": (2, MEM, 512), "ffn_conv": (2, P, FT, 18),
        "ret_state_sample": (NB, HEADS, DK_A, P), "chunk_v_sample": (S, 512), "hgrn_state_sample": (NB, HEADS, P, P),
        "swa_kT_sample": (P, NB, WIN), "swa_v_sample": (WIN - NS, NB, P), "swa_v_new": (S, P),
    }
    nc = _bacc.Bacc("TRN2", target_bir_lowering=False, num_devices=1)
    io, arrays = {}, {}
    for name, a in ins.items():
        a = c32(a)
        arrays[f"in_{name}"] = a
        io[name] = nc.dram_tensor(f"in_{name}", a.shape, F32, kind="ExternalInput").ap()
    for name, shape in outs.items():
        io[name] = nc.dram_tensor(f"out_{name}", shape, F32, kind="ExternalOutput").ap()
    build(nc, io)
    r = _run(nc, [arrays], core_ids=[0]).results[0]
    o = {name: r[f"out_{name}"] for name in outs}
    y = o["yT"].T
    conv = o["ffn_conv"].transpose(0, 3, 2, 1).reshape(2, 18, FF)
    swa_v = cat([o["swa_v_sample"].transpose(1, 0, 2), o["swa_v_new"].reshape(NB, NS, P)], 1)
    got = (y[:SEQ][None], y[SEQ:].reshape(NB, NS, D), o["ret_state_prompt"][None, None], o["hgrn_state_prompt"][None, None],
           o["swa_kT_prompt"].T.reshape(1, 1, WIN, 2, 64), o["swa_v_prompt"].reshape(1, 1, WIN, 2, 64),
           o["mem_kT_prompt"].transpose(0, 3, 1, 2)[:, None], o["mem_v_prompt"].reshape(2, 1, MEM, HEADS, P),
           conv[:, 0:2][:, None], o["ret_state_sample"][None], o["chunk_v_sample"].reshape(1, NB, NS, 4, P),
           o["hgrn_state_sample"][None], o["swa_kT_sample"].transpose(1, 2, 0).reshape(1, NB, WIN, 2, 64),
           swa_v.reshape(1, NB, WIN, 2, 64), conv[:, 2:18].reshape(2, NB, 2, FF))
    return tuple(c32(a) for a in got)
```

```python
from contextlib import ExitStack

import numpy as np
import concourse.bass as bass
from concourse import mybir

F32 = mybir.dt.float32
F32R = mybir.dt.float32r
ALU = mybir.AluOpType
ACT = mybir.ActivationFunctionType
AX = mybir.AxisListType

P = 128
D = 1024
KT = D // P
SEQ, NB, NS = 1024, 8, 8
S = NB * NS
T = SEQ + S
NBLK = SEQ // P
HEADS = 4
DK_A = 64
FF = 2816
FT = FF // P
MEM = 256
WIN = 128
EPS = 1e-6
PART = 6
SPANS = ((0, 384), (384, 384), (768, 320))
TOK = [(j * P, P) for j in range(NBLK)] + [(SEQ, S)]
LEVELS = 7
FIRST = 16


class Count:

    def __init__(self, sem):
        self.sem, self.base = sem, 0

    def at(self, n):
        return n + self.base

    def adds(self, n):
        self.base += n


class Chain:

    def __init__(self, sem):
        self.sem, self.n, self.term = sem, 0, None

    def now(self):
        return self.n if self.term is None else self.term + self.n

    def next(self):
        self.n += 1
        return self.now()

    def enter(self, i, per):
        self.term, self.start, self.per = i * per, self.n, per

    def leave(self, rounds):
        assert self.n - self.start == self.per, (self.n - self.start, self.per)
        self.n, self.term = self.start + rounds * self.per, None


class To:

    def __init__(self, buf=None, first=0, func=None, times=None, rows=None, residual=False):
        self.buf, self.first, self.func, self.times, self.rows, self.residual = buf, first, func, times, rows, residual


class Lead:

    def __init__(self, srcs, gain=None, inv=None, spill=False, reload=None, arriving=None):
        self.srcs, self.gain, self.inv, self.spill, self.reload, self.arriving = srcs, gain, inv, spill, reload, arriving


class Shared:
    pass


def build(nc, io):
    with ExitStack() as ctx:
        _build(nc, io, ctx)


def _build(nc, io, ctx):
    def sb(name, shape):
        return ctx.enter_context(nc.sbuf_tensor(name, shape, F32))

    def sem(name):
        return ctx.enter_context(nc.semaphore(name))

    counts = {}

    def count(name):
        if name not in counts:
            counts[name] = Count(sem(name))
        return counts[name]

    base = (nc.sbuf_base + 31) // 32 * 32
    slab = [0]

    def place(name, floats, dtype=F32, at=None):
        if at is None:
            at = slab[0]
            slab[0] += (floats + 7) // 8 * 8
        return nc.alloc_sbuf_tensor_at(name, [P, floats], dtype, offset=base + 4 * at)[:, :], at

    def tiled(v):
        return v.rearrange("p (a b) -> p a b", b=T)
    X, _ = place("residual", KT * T)
    Hf, at = place("work_h", 2 * KT * T)
    HHf, _ = place("moving_hi", KT * T, F32R, at)
    HLf, _ = place("moving_lo", KT * T, F32R, at + KT * T)
    Rf, at = place("work_r", 13 * T)
    HIDH, _ = place("hidden_hi", PART * T, F32R, at)
    HIDL, _ = place("hidden_lo", PART * T, F32R, at + PART * T)
    Wf, at = place("work_w", 6 * D)
    WRAW = [place(f"w_raw{s}", D, F32, at + s * D)[0] for s in range(2)]
    WHI = [place(f"w_hi{s}", D, F32R, at + (2 + s) * D)[0] for s in range(2)]
    WLO = [place(f"w_lo{s}", D, F32R, at + (4 + s) * D)[0] for s in range(2)]
    CST, _ = place("constants", 4 * T + 1408)
    COS, SIN, SPARE, MASK = CST[:, 0:T], CST[:, T:2 * T], tiled(CST[:, 2 * T:4 * T]), CST[:, 4 * T:4 * T + 1408]
    IDENT, ROT, ONES, ONES128, ONES64 = (place(n, P)[0] for n in ("ident", "rot", "ones1024", "ones128", "ones64"))
    GAIN, _ = place("gains", 3 * KT)
    COL, _ = place("columns", 64)
    SM, _ = place("small", 80)
    EPSC, _ = place("eps", 1)
    ONE, _ = place("one", 1)
    ctx.enter_context(nc.sbuf_tensor("slab", [P, slab[0]], F32))
    X, H, R = tiled(X), tiled(Hf), tiled(Rf)
    HH, HL, HIDH, HIDL = tiled(HHf), tiled(HLf), tiled(HIDH), tiled(HIDL)
    OT = X
    PS = ctx.enter_context(nc.psum_tensor("psum", [P, 8, 512], F32))
    OTf = X[:, :, :].rearrange("p a b -> p (a b)")
    PSf = PS[:, :, :].rearrange("p a b -> p (a b)")

    def view(flat, at, *dims):
        n = 1
        for d in dims:
            n *= d
        v = flat[:, at:at + n]
        if len(dims) == 2:
            v = v.rearrange("p (a b) -> p a b", b=dims[1])
        if len(dims) == 3:
            v = v.rearrange("p (a b c) -> p a b c", b=dims[1], c=dims[2])
        return v

    act_own, dve_own, pool_own = Chain(sem("act_own")), Chain(sem("dve_own")), Chain(sem("pool_own"))
    w_loaded = [count(f"w_loaded{s}") for s in range(2)]
    w_split = count("w_split")
    prefetched = [0]
    ahead = [False]
    tile_full, tile_free = count("tile_full"), count("tile_free")
    loaded, stored, reloaded = count("loaded"), count("stored"), count("reloaded")
    stores = [0]

    def store(eng, dst, src):
        eng.dma_start(dst, src).then_inc(stored.sem, 16)
        stores[0] += 16

    def load(pairs, zero=()):
        cleared = count("cleared")
        with nc.Block() as block:
            @block.gpsimd
            def _(pool):
                for z in zero:
                    nc.gpsimd.memset(z, 0.0).then_inc(cleared.sem, 1)

            @block.sync
            def _(sp):
                if zero:
                    sp.wait_ge(cleared.sem, cleared.at(len(zero)))
                for dst, src in pairs:
                    sp.dma_start(dst, src).then_inc(loaded.sem, 16)
                sp.wait_ge(loaded.sem, loaded.at(16 * len(pairs)))
        loaded.adds(16 * len(pairs))
        cleared.adds(len(zero))

    def slot(buf, kt):
        return buf[:, 0:kt * P].rearrange("p (k n) -> p k n", n=P)

    def chunk(w, kt, c):
        return w.rearrange("(k p) n -> p k n", p=P)[:, :, bass.ds(c * P, P)]

    def rounds(eng, chunks, body, start=0, chain=None, per=0):
        pairs = chunks // 2
        if pairs - start > 1:
            with eng.Fori(start, pairs) as i:
                if chain:
                    chain.enter(i - start, 2 * per)
                for s in range(2):
                    body(i * 2 + s, s, i)
            if chain:
                chain.leave(pairs - start)
        elif pairs - start == 1:
            for s in range(2):
                body(start * 2 + s, s, start)
        if chunks % 2 and chunks > 2 * start:
            body(chunks - 1, 0, pairs)

    def last_user(slot_, chunks):
        return chunks - 1 - (chunks - 1 - slot_) % 2

    def load_weights(sp, pick, chunks, then, o=0, all_split=False):
        def body(c, s, i):
            sp.wait_ge(w_split.sem, w_split.at(c + (o - 1)))
            src, kt = pick(c, s, i)
            sp.dma_start(slot(WRAW[s], kt), src).then_inc(w_loaded[s].sem, 16)
        rounds(sp, chunks, body, start=1 if prefetched[0] else 0)
        prefetched[0] = 0
        if then:
            pick2, n2 = then
            for c in range(min(2, n2)):
                sp.wait_ge(w_split.sem, w_split.at(o + (chunks if all_split else last_user(c, chunks) + 1)))
                src, kt = pick2(c, c, 0)
                sp.dma_start(slot(WRAW[c], kt), src).then_inc(w_loaded[c].sem, 16)
            prefetched[0] = min(2, n2)

    def halve(eng, s, kt):
        raw, hi, lo = (b[s][:, 0:kt * P] for b in (WRAW, WHI, WLO))
        if eng is nc.gpsimd:
            own = pool_own
            nc.gpsimd.tensor_tensor(hi, raw, ONE.to_broadcast([P, kt * P]), ALU.mult).then_inc(own.sem, 1)
        else:
            own = dve_own
            nc.vector.tensor_copy(hi, raw).then_inc(own.sem, 1)
        eng.wait_ge(own.sem, own.next())
        eng.tensor_tensor(lo, raw, hi.bitcast(F32), ALU.subtract).then_inc(w_split.sem, 1)

    def split_weights(eng, kt, chunks, skip, o=0):
        def body(c, s, i):
            eng.wait_ge(w_loaded[s].sem, w_loaded[s].at(i * 16 + (8 * o + 16)))
            eng.wait_ge(tile_full.sem, tile_full.at(c + (o - 1)))
            halve(eng, s, kt)
        if skip and chunks > 1:
            body(1, 1, 0)
        rounds(eng, chunks, body, start=1 if skip else 0, chain=pool_own if eng is nc.gpsimd else dve_own, per=1)

    def split_ahead(pool, chunks, then, o=0):
        if then:
            pool.wait_ge(w_loaded[0].sem, w_loaded[0].at(8 * o + 16 * ((chunks + 1) // 2) + 16))
            pool.wait_ge(tile_full.sem, tile_full.at(o + last_user(0, chunks) + 1))
            halve(nc.gpsimd, 0, then[0](0, 0, 0)[1])

    def counted(chunks):
        w_split.adds(chunks)
        tile_full.adds(chunks)
        tile_free.adds(chunks)
        w_loaded[0].adds(16 * ((chunks + 1) // 2))
        w_loaded[1].adds(16 * (chunks // 2))

    def columns(w, kt, n=None):
        return (lambda c, s, i: (chunk(w, kt, c), kt)), n

    def pass_of(pe, out, stationary, moving, k, kt):
        (sh, sl), (mh, ml) = stationary, moving
        pe.matmul(out, sh, mh, start=(k == 0), stop=False)
        pe.matmul(out, sh, ml, start=False, stop=False)
        return pe.matmul(out, sl, mh, start=False, stop=(k == kt - 1))

    squared, square_used, summed, rooted = count("squared"), count("square_used"), count("summed"), count("rooted")
    hi_made, lo_made = count("hi_made"), count("lo_made")
    arrived = [count(f"x_arrived{q}") for q in range(KT // 2)]
    SQ, ACC = [R[:, 9, :], R[:, 10, :]], R[:, 11, :]

    def lead_scalar(act, lead):
        for t, x in enumerate(lead.srcs):
            if lead.arriving and t % 2 == 0:
                act.wait_ge(arrived[t // 2].sem, 16)
            act.activation(HH[:, t, :], x, ACT.Copy, scale=1.0 if lead.gain is None else GAIN[:, lead.gain + t:lead.gain + t + 1]).then_inc(hi_made.sem, 1)
        if lead.inv is not None:
            for k, x in enumerate(lead.srcs):
                if k >= 2:
                    act.wait_ge(square_used.sem, square_used.at(k - 1))
                act.activation(SQ[k % 2], x, ACT.Square).then_inc(squared.sem, 1)
            act.wait_ge(summed.sem, summed.at(1))
            act.activation(lead.inv[:, 0:1024].rearrange("p (a b) -> p a b", b=512), PS[:, 6:8, :], ACT.Sqrt, bias=EPSC[:, 0:1])
            act.activation(lead.inv[:, 1024:T], PS[:, 2, 448:512], ACT.Sqrt, bias=EPSC[:, 0:1]).then_inc(rooted.sem, 1)

    def lead_vector(dve, lead):
        for t, x in enumerate(lead.srcs):
            dve.wait_ge(hi_made.sem, hi_made.at(t + 1))
            if lead.gain is None:
                last = dve.tensor_tensor(HL[:, t, :], x, HH[:, t, :].bitcast(F32), ALU.subtract)
            else:
                last = dve.scalar_tensor_tensor(HL[:, t, :], x, GAIN[:, lead.gain + t:lead.gain + t + 1], HH[:, t, :].bitcast(F32), ALU.mult, ALU.subtract)
            last.then_inc(lo_made.sem, 1)
        if lead.inv is not None:
            dve.wait_ge(squared.sem, squared.at(2))
            dve.tensor_tensor(ACC, SQ[0], SQ[1], ALU.add).then_inc(square_used.sem, 2)
            for k in range(2, KT):
                dve.wait_ge(square_used.sem, square_used.at(k))
                dve.wait_ge(squared.sem, squared.at(k + 1))
                dve.tensor_tensor(ACC, ACC, SQ[k % 2], ALU.add).then_inc(square_used.sem, 1)
            dve.wait_ge(rooted.sem, rooted.at(1))
            dve.reciprocal(lead.inv, lead.inv).then_inc(dve_own.sem, 1)
            dve.wait_ge(dve_own.sem, dve_own.next())
        if lead.spill:
            dve.wait_ge(stored.sem, stores[0])
        if lead.reload is not None:
            dve.wait_ge(reloaded.sem, reloaded.at(16 * KT))

    def lead_counted(lead):
        hi_made.adds(len(lead.srcs))
        lo_made.adds(len(lead.srcs))
        if lead.reload is not None:
            reloaded.adds(16 * KT)
        if lead.arriving:
            loaded.adds(16 * len(lead.arriving))
        if lead.inv is not None:
            for c, n in ((squared, KT), (square_used, KT), (summed, 1), (rooted, 1)):
                c.adds(n)

    def moved_in(block, pick, kt, chunks, then, lead, split_on="gpsimd"):
        skip, ahead[0] = ahead[0], bool(then)

        @block.sync
        def _(sp):
            if lead and lead.spill:
                store(sp, io["yT"].rearrange("(k p) t -> p k t", p=P), X[:, :, :])
            if lead and lead.reload is not None:
                for t in range(KT):
                    sp.wait_ge(lo_made.sem, lo_made.at(t + 1))
                    sp.dma_start(X[:, t, :], lead.reload[t * P:(t + 1) * P, :]).then_inc(reloaded.sem, 16)
            if lead and lead.arriving:
                for q in range(KT // 2):
                    sp.dma_start(X[:, 2 * q:2 * q + 2, :], io["xT"][2 * q * P:(2 * q + 2) * P, :].rearrange("(k p) t -> p k t", p=P)).then_inc(arrived[q].sem, 16)
                for dst, src in lead.arriving:
                    sp.dma_start(dst, src).then_inc(loaded.sem, 16)
            load_weights(sp, pick, chunks, then, all_split=split_on == "vector")
            if lead and lead.arriving:
                sp.wait_ge(loaded.sem, loaded.at(16 * len(lead.arriving)))

        @block.gpsimd
        def _(pool):
            if split_on == "gpsimd":
                split_weights(nc.gpsimd, kt, chunks, skip)
            split_ahead(pool, chunks, then)
        return skip

    def products(pe, src, kt, chunks, spans, paced=None, norm=False, turn=None, o=0):
        def ready(c):
            pe.wait_ge(w_split.sem, w_split.at(c + (o + 1)))
            pe.wait_ge(tile_free.sem, tile_free.at(c + (o - 1)))

        def body(c, s, i, norm=False):
            hi, lo = slot(WHI[s], kt), slot(WLO[s], kt)
            ready(c)
            for n, (a, m) in enumerate(spans):
                if norm and n == 2:
                    pe.wait_ge(square_used.sem, square_used.at(KT))
                    for out, (b, w) in ((PS[:, 6, :], (0, 512)), (PS[:, 7, :], (512, 512)), (PS[:, 2, 448:512], (1024, 64))):
                        last = pe.matmul(out, ONES[:, :], ACC[:, b:b + w], start=True, stop=True)
                    last.then_inc(summed.sem, 1)
                for k in range(kt):
                    last = pass_of(pe, PS[:, 3 * s + n, 0:m], (hi[:, k, :], lo[:, k, :]), (src[0][:, k, a:a + m], src[1][:, k, a:a + m]), k, kt)
            last.then_inc(tile_full.sem, 1)
        if paced:
            hi, lo = slot(WHI[0], kt), slot(WLO[0], kt)
            ready(0)
            for k in range(kt):
                paced(k)
                for n, (a, m) in enumerate(spans):
                    last = pass_of(pe, PS[:, n, 0:m], (hi[:, k, :], lo[:, k, :]), (src[0][:, k, a:a + m], src[1][:, k, a:a + m]), k, kt)
            last.then_inc(tile_full.sem, 1)
            body(1, 1, 0, norm=norm)
            if turn:
                turn(0)
        if turn:
            for c in range(2 if paced else 0, chunks):
                body(c, c % 2, c // 2)
                if c:
                    turn(c - 1)
            turn(chunks - 1)
        else:
            rounds(pe, chunks, body, start=1 if paced else 0)

    def project(pick, src, kt, chunks, to, spans=SPANS, then=None, lead=None, split_on="gpsimd"):
        row_turned, row_taken, activated = count("row_turned"), count("row_taken"), count("activated")
        groups = [(TOK[j:j + 4], j) for j in range(0, 9, 4)]
        in_place = to.times is not None and to.func is not None

        def tile(c):
            return c % 2 if to.rows is not None else c + to.first
        with nc.Block() as block:
            skip = moved_in(block, pick, kt, chunks, then, lead, split_on)

            @block.tensor
            def _(pe):
                def turn(c):
                    if in_place:
                        pe.wait_ge(activated.sem, activated.at(c + 1))
                    else:
                        pe.wait_ge(tile_free.sem, tile_free.at(c + 1))
                    for q, (toks, j) in enumerate(groups):
                        n = 3 * c + q
                        if n >= 2:
                            pe.wait_ge(row_taken.sem, row_taken.at(n - 1))
                        for x, (a, m) in enumerate(toks):
                            last = pe.transpose(PS[0:m, 6 + n % 2, x * P:(x + 1) * P], to.buf[:, tile(c), a:a + m], IDENT[:, :])
                        last.then_inc(row_turned.sem, 1)
                def paced(k):
                    pe.wait_ge(lo_made.sem, lo_made.at(k + 1))
                products(pe, src, kt, chunks, spans, paced if lead else None, lead is not None and lead.inv is not None, turn if to.rows is not None else None)

            if split_on == "vector":
                @block.vector
                def _(dve):
                    split_weights(nc.vector, kt, chunks, skip)

            elif lead or to.times is not None or to.residual:
                @block.vector
                def _(dve):
                    def body(c, s, i):
                        dve.wait_ge(tile_full.sem, tile_full.at(c + 1))
                        if to.rows is not None and c >= 2:
                            dve.wait_ge(row_turned.sem, row_turned.at(3 * c - 3))
                        for ps, a, m, rows in pieces(3 * s, spans):
                            if to.residual:
                                x = cut(X, c, a, m, rows)
                                last = dve.tensor_tensor(x, ps, x, ALU.add)
                            else:
                                last = dve.tensor_tensor(cut(to.buf, tile(c), a, m, rows), ps, shaped(to.times, a, m, rows), ALU.mult)
                        last.then_inc(tile_free.sem, 1)
                    if lead:
                        lead_vector(dve, lead)
                    if to.rows is not None:
                        for c in range(chunks):
                            body(c, c % 2, c // 2)
                    elif to.times is not None or to.residual:
                        rounds(dve, chunks, body)

            @block.scalar
            def _(act):
                def body(c, s, i):
                    if to.times is None:
                        act.wait_ge(tile_full.sem, tile_full.at(c + 1))
                        for ps, a, m, rows in pieces(3 * s, spans):
                            last = act.activation(cut(to.buf, tile(c), a, m, rows), ps, to.func or ACT.Copy)
                        last.then_inc(tile_free.sem, 1)
                    elif to.func:
                        act.wait_ge(tile_free.sem, tile_free.at(c + 1))
                        x = to.buf[:, bass.ds(tile(c), 1), :].rearrange("p a b -> p (a b)")
                        last = act.activation(x, x, to.func)
                        if to.rows is not None:
                            last.then_inc(activated.sem, 1)

                def take(c):
                    for q, (toks, j) in enumerate(groups):
                        n = 3 * c + q
                        act.wait_ge(row_turned.sem, row_turned.at(n + 1))
                        m = toks[0][1]
                        ps = PS[0:m, 6 + n % 2, 0:len(toks) * P].rearrange("p (j n) -> p j n", n=P)
                        act.activation(to.rows[0:m, j:j + len(toks), c * P:(c + 1) * P], ps, ACT.Copy).then_inc(row_taken.sem, 1)
                if lead:
                    lead_scalar(act, lead)
                if to.rows is not None:
                    for c in range(chunks):
                        if c:
                            take(c - 1)
                        if in_place:
                            body(c, c % 2, c // 2)
                    take(chunks - 1)
                elif not to.residual and (to.times is None or to.func):
                    rounds(act, chunks, body)
        counted(chunks)
        if lead:
            lead_counted(lead)
        if to.rows is not None:
            row_turned.adds(3 * chunks)
            row_taken.adds(3 * chunks)
            if in_place:
                activated.adds(chunks)

    def turn_rows(pairs):
        turned = count("turned_rows")
        with nc.Block() as block:
            @block.tensor
            def _(pe):
                for b, (srcs, dsts) in enumerate(pairs):
                    for x, v in enumerate(srcs):
                        m = v.shape[1]
                        last = pe.transpose(PS[0:m, b, x * P:(x + 1) * P], v, IDENT[:, :])
                    last.then_inc(turned.sem, 1)

            @block.scalar
            def _(act):
                for b, (srcs, dsts) in enumerate(pairs):
                    act.wait_ge(turned.sem, turned.at(b + 1))
                    m = srcs[0].shape[1]
                    ps = PS[0:m, b, 0:len(srcs) * P].rearrange("p (j n) -> p j n", n=P)
                    for dst, c in dsts:
                        act.activation(dst, ps[:, :, c], ACT.Copy)
        turned.adds(len(pairs))

    def pieces(bank, spans=SPANS):
        if len(spans) == 1:
            return [(PS[:, bank, 0:spans[0][1]], 0, spans[0][1], 1)]
        return [(PS[:, bank:bank + 2, 0:384], 0, 768, 2), (PS[:, bank + 2, 0:320], 768, 320, 1)]

    def cut(buf, tile, a, m, rows):
        v = buf[:, bass.ds(tile, 1), a:a + m].rearrange("p a b -> p (a b)")
        return v.rearrange("p (r b) -> p r b", r=rows) if rows > 1 else v

    def shaped(v, a, m, rows):
        v = v[:, a:a + m]
        return v.rearrange("p (r b) -> p r b", r=rows) if rows > 1 else v

    def tile_norm(srcs, dsts, ones, gains, scratch, width=T, center=False, times=None):
        spans = SPANS if width == T else ((0, width),)
        squared, summed, rooted = count("tile_squared"), count("tile_summed"), count("tile_rooted")
        meaned, centered, scaled = count("tile_meaned"), count("tile_centered"), count("tile_scaled")
        n_t, n_p = len(srcs), len(pieces(0, spans))
        with nc.Block() as block:
            @block.tensor
            def _(pe):
                for t in range(n_t):
                    if t >= 1:
                        pe.wait_ge(rooted.sem, rooted.at(n_p * t))
                    if center:
                        for n, (a, m) in enumerate(spans):
                            last = pe.matmul(PS[:, 3 + n, 0:m], ones, srcs[t][:, a:a + m], start=True, stop=True)
                        last.then_inc(meaned.sem, 1)
                    pe.wait_ge(squared.sem, squared.at(t + 1))
                    for n, (a, m) in enumerate(spans):
                        last = pe.matmul(PS[:, n, 0:m], ones, scratch[t % 2][:, a:a + m], start=True, stop=True)
                    last.then_inc(summed.sem, 1)

            @block.scalar
            def _(act):
                for t in range(n_t):
                    if center:
                        act.wait_ge(centered.sem, centered.at(t + 1))
                    if t >= 2:
                        act.wait_ge(summed.sem, summed.at(t - 1))
                    act.activation(scratch[t % 2], srcs[t], ACT.Square).then_inc(squared.sem, 1)
                    act.wait_ge(summed.sem, summed.at(t + 1))
                    if t >= 2:
                        act.wait_ge(scaled.sem, scaled.at(t - 1))
                    for ps, a, m, rows in pieces(0, spans):
                        act.activation(shaped(scratch[2 + t % 2], a, m, rows), ps, ACT.Sqrt, bias=EPSC[:, 0:1]).then_inc(rooted.sem, 1)

            @block.vector
            def _(dve):
                for t in range(n_t):
                    if center:
                        dve.wait_ge(meaned.sem, meaned.at(t + 1))
                        for ps, a, m, rows in pieces(3, spans):
                            v = shaped(srcs[t], a, m, rows)
                            last = dve.tensor_tensor(v, v, ps, ALU.subtract)
                        last.then_inc(centered.sem, 1)
                        dve.wait_ge(centered.sem, centered.at(t + 1))
                    dve.wait_ge(rooted.sem, rooted.at(n_p * (t + 1)))
                    inv = scratch[2 + t % 2]
                    dve.reciprocal(inv, inv).then_inc(dve_own.sem, 1)
                    dve.wait_ge(dve_own.sem, dve_own.next())
                    last = dve.scalar_tensor_tensor(srcs[t] if times else dsts[t], srcs[t], gains[t], inv, ALU.mult, ALU.mult)
                    if times:
                        last.then_inc(dve_own.sem, 1)
                        dve.wait_ge(dve_own.sem, dve_own.next())
                        last = dve.tensor_tensor(dsts[t], srcs[t], times[t], ALU.mult)
                    last.then_inc(scaled.sem, 1)
        for c, n in ((squared, n_t), (summed, n_t), (rooted, n_t * n_p), (scaled, n_t)):
            c.adds(n)
        if center:
            meaned.adds(n_t)
            centered.adds(n_t)

    def rotate(tiles, scratch):
        rotated, taken = count("rotated"), count("rotated_taken")
        with nc.Block() as block:
            @block.tensor
            def _(pe):
                for t, x in enumerate(tiles):
                    if t >= 2:
                        pe.wait_ge(taken.sem, taken.at(t - 1))
                    for n, (a, m) in enumerate(SPANS):
                        last = pe.matmul(PS[:, 3 * (t % 2) + n, 0:m], ROT[:, :], x[:, a:a + m], start=True, stop=True)
                    last.then_inc(rotated.sem, 1)

            @block.vector
            def _(dve):
                for t, x in enumerate(tiles):
                    dve.wait_ge(rotated.sem, rotated.at(t + 1))
                    for ps, a, m, rows in pieces(3 * (t % 2)):
                        o, s = scratch[:, a:a + m], SIN[:, a:a + m]
                        if rows > 1:
                            o, s = (v.rearrange("p (r b) -> p r b", r=rows) for v in (o, s))
                        last = dve.tensor_tensor(o, ps, s, ALU.mult)
                    last.then_inc(taken.sem, 1)
                    dve.tensor_tensor(x, x, COS[:, :], ALU.mult).then_inc(dve_own.sem, 1)
                    dve.wait_ge(dve_own.sem, dve_own.next())
                    dve.wait_ge(taken.sem, taken.at(t + 1))
                    dve.tensor_tensor(x, x, scratch, ALU.add).then_inc(dve_own.sem, 1)
                    dve.wait_ge(dve_own.sem, dve_own.next())
        rotated.adds(len(tiles))
        taken.adds(len(tiles))

    def tok(v, j):
        a, m = TOK[j]
        return v[..., a:a + m]

    with nc.Block() as block:
        consts = [(IDENT[:, :], io["ident"]), (GAIN[:, :], io["gain0"])]

        @block.sync
        def _(sp):
            for dst, src in consts:
                sp.dma_start(dst, src).then_inc(loaded.sem, 16)
            sp.wait_ge(loaded.sem, loaded.at(16 * len(consts)))

        @block.gpsimd
        def _(pool):
            for v, x in ((ONES, 1.0 / D), (ONES128, 1.0 / P), (EPSC, EPS), (ONES64, 0.0), (ONE, 1.0)):
                nc.gpsimd.memset(v, x).then_inc(pool_own.sem, 1)
            pool.wait_ge(pool_own.sem, 5)
            nc.gpsimd.memset(view(Rf, 4 * T + 4608, 9, 512)[64:128, 8, :], 0.0)
            nc.gpsimd.memset(ONES64[0:64, 0:64], 1.0 / 64)
            nc.gpsimd.memset(ONES64[64:128, 64:128], 1.0 / 64)
            pool.sem_inc(tile_full.sem, FIRST)
            pool.sem_inc(tile_free.sem, FIRST)
            pool.sem_inc(w_split.sem, FIRST)
        pool_own.n = 5
        tile_full.adds(FIRST)
        tile_free.adds(FIRST)
        w_split.adds(FIRST)
    loaded.adds(16 * 2)

    env = Shared()
    env.COL = COL
    env.COS = COS
    env.CST = CST
    env.EPSC = EPSC
    env.GAIN = GAIN
    env.H = H
    env.HH = HH
    env.HHf = HHf
    env.HIDH = HIDH
    env.HIDL = HIDL
    env.HL = HL
    env.HLf = HLf
    env.Hf = Hf
    env.IDENT = IDENT
    env.MASK = MASK
    env.ONES128 = ONES128
    env.ONES64 = ONES64
    env.OT = OT
    env.ONE = ONE
    env.OTf = OTf
    env.PS = PS
    env.PSf = PSf
    env.R = R
    env.ROT = ROT
    env.Rf = Rf
    env.SIN = SIN
    env.SM = SM
    env.SPARE = SPARE
    env.WHI = WHI
    env.WLO = WLO
    env.WRAW = WRAW
    env.Wf = Wf
    env.X = X
    env.act_own = act_own
    env.chunk = chunk
    env.count = count
    env.cut = cut
    env.dve_own = dve_own
    env.load = load
    env.loaded = loaded
    env.pieces = pieces
    env.pool_own = pool_own
    env.project = project
    env.rotate = rotate
    env.slot = slot
    env.store = store
    env.stored = stored
    env.stores = stores
    env.tile_norm = tile_norm
    env.view = view
    env.ahead = ahead
    env.load_weights = load_weights
    env.split_weights = split_weights
    env.split_ahead = split_ahead
    env.lo_made = lo_made
    env.rounds = rounds
    env.columns = columns
    env.products = products
    env.lead_scalar = lead_scalar
    env.lead_vector = lead_vector
    env.lead_counted = lead_counted
    env.counted = counted
    env.turn_rows = turn_rows
    env.tile_full = tile_full
    env.tile_free = tile_free

    def run(stage, *args, **options):
        stage(*args, **options)

    _layer0(nc, io, env, run)
    for l in range(2):
        if l == 1:
            _layer1(nc, io, env, run)
        _memory(nc, io, env, run, l)
        _feed_forward(nc, io, env, run, l)


def _layer0(nc, io, env, run):
    g = env
    X, H, OT, R, Rf, Hf, OTf, PS, PSf, view, count, P_ = g.X, g.H, g.OT, g.R, g.Rf, g.Hf, g.OTf, g.PS, g.PSf, g.view, g.count, P
    MASK, COS, SIN, COL, SM, IDENT = g.MASK, g.COS, g.SIN, g.COL, g.SM, g.IDENT
    act_own, dve_own = g.act_own, g.dve_own
    HHL = (g.HH, g.HL)
    VA, VB = view(Rf, 4 * T, 9, 512), view(Rf, 4 * T + 4608, 9, 512)
    STATE = [view(Rf, 4 * T + 9216, 2, 256), view(g.SPARE[:, 0, :], 0, 2, 256)]
    DMASK, QDEC, PAIR = view(MASK[:, :], 0, 4, P), view(MASK[:, :], 512, 2, P), view(MASK[:, :], 768, 256)
    DMASK_S, QDEC_S = MASK[0:S, 1024:1280].rearrange("p (h n) -> p h n", n=S), view(MASK[:, :], 1280, 2, NS)
    RC = MASK[:, 1296:1320]
    SAMPLE_STATE = view(Hf, 4 * T, NB, 2, 256)
    w_in = io["ev_w_in"]

    arriving = [(COS[:, :], io["ret_cos"]), (SIN[:, :], io["ret_sin"]), (g.ROT[:, :], io["ret_rot"]),
                (MASK[:, 0:1320], io["ret_tables"]), (COL[:, 0:4], io["ret_gn_g"])]

    INV = g.SPARE[:, 1, :]
    ws = [g.columns(w_in[:, 512 * i:512 * (i + 1)], KT, 4) for i in range(5)]
    out = g.columns(io["ev_w_out"], KT, 8)
    run(g.project, ws[1][0], HHL, KT, 4, To(OT, times=INV, rows=VA), then=ws[4], lead=Lead([X[:, k, :] for k in range(KT)], gain=0, inv=INV, arriving=arriving))
    run(g.project, ws[4][0], HHL, KT, 4, To(OT, func=ACT.Gelu, times=INV, rows=VB), then=ws[0])
    run(g.project, ws[0][0], HHL, KT, 4, To(R, 0, times=INV), then=ws[2])
    run(g.project, ws[2][0], HHL, KT, 4, To(OT, 0, func=ACT.Silu, times=INV), then=ws[3])
    run(g.project, ws[3][0], HHL, KT, 4, To(OT, 4, func=ACT.Gelu, times=INV), then=out)
    run(g.rotate, [R[:, t, :] for t in range(4)], H[:, 7, :])

    def clear_state():
        run(g.load, [(SAMPLE_STATE[64 * hh:64 * hh + 64, :, pr, 128 * hh:128 * hh + 128],
                      io["state_ret"].rearrange("b (t e) k v -> t e k b v", e=2)[pr, hh])
                     for hh in range(2) for pr in range(2)],
            zero=(SAMPLE_STATE[0:64, :, :, 128:256], SAMPLE_STATE[64:128, :, :, 0:128]))
    clear_state()

    work = [COS, SIN]

    def retention():
        a_ready, a_taken, o_ready, o_out = (count(n) for n in ("ret_scores", "ret_taken", "ret_out", "ret_out_taken"))
        kv_ready, s_ready = count("ret_kv"), count("ret_state")

        def bufs(j):
            w = work[j % 2]
            return view(w[:, :], 0, 4, P), view(w[:, :], 512, 4, 64), view(w[:, :], 768, 2, P)
        with nc.Block() as block:
            @block.tensor
            def _(pe):
                def scores(j):
                    a, m = TOK[j]
                    b = 6 * (j % 2)
                    if j >= 2:
                        pe.wait_ge(a_taken.sem, a_taken.at(j - 1))
                    for h in range(HEADS):
                        pr, r = h // 2, 64 * (h % 2)
                        pe.matmul(PS[0:m, b + h % 2, pr * P:pr * P + m], R[r:r + 64, 2 + pr, a:a + m], R[r:r + 64, pr, a:a + m], start=True, stop=True)
                    for pr in range(2):
                        last = pe.transpose(PS[0:m, 2 + b // 3, pr * P:(pr + 1) * P], R[:, 2 + pr, a:a + m], IDENT[:, :])
                    last.then_inc(a_ready.sem, 1)
                scores(0)
                for j, (a, m) in enumerate(TOK):
                    AT, KD, QD = bufs(j)
                    if j < NBLK:
                        scores(j + 1)
                    pe.wait_ge(a_taken.sem, a_taken.at(j + 1))
                    if j < NBLK:
                        if j:
                            pe.wait_ge(s_ready.sem, s_ready.at(j + 1))
                        for pr in range(2):
                            last = pe.matmul(PS[:, 5, pr * 256:(pr + 1) * 256], KD[:, 2 * pr:2 * pr + 2, :].rearrange("p a b -> p (a b)"),
                                             VA[:, j, pr * 256:(pr + 1) * 256], start=True, stop=True)
                        last.then_inc(kv_ready.sem, 1)
                    if j:
                        pe.wait_ge(o_out.sem, o_out.at(j))
                    for h in range(HEADS):
                        pr, hh = h // 2, h % 2
                        o = PS[:, 3, h * P:h * P + m]
                        pe.matmul(o, VA[0:m, j, h * P:(h + 1) * P], AT[0:m, h, 0:m], start=True, stop=(j == NBLK))
                        if j < NBLK:
                            last = pe.matmul(o, STATE[j % 2][:, pr, hh * P:(hh + 1) * P], QD[:, pr, :], start=False, stop=True)
                        else:
                            for b in range(NB):
                                last = pe.matmul(PS[:, 3, h * P + b * NS:h * P + (b + 1) * NS], SAMPLE_STATE[:, b, pr, hh * P:(hh + 1) * P],
                                                 QD[:, pr, b * NS:(b + 1) * NS], start=False, stop=True, skip_group_check=True)
                    last.then_inc(o_ready.sem, 1)

            @block.vector
            def _(dve):
                dve.memset(STATE[0], 0.0).then_inc(s_ready.sem, 1)

                def operands(j):
                    a, m = TOK[j]
                    b = 6 * (j % 2)
                    AT, KD, QD = bufs(j)
                    dve.wait_ge(a_ready.sem, a_ready.at(j + 1))
                    if j >= 2:
                        dve.wait_ge(o_ready.sem, o_ready.at(j - 1))
                    dm = DMASK if j < NBLK else DMASK_S
                    for hh in range(2):
                        dve.tensor_tensor(AT[0:m, hh:4:2, 0:m], PS[0:m, b + hh, 0:256].rearrange("p (a b) -> p a b", b=P)[:, :, 0:m], dm[0:m, hh:4:2, 0:m], ALU.mult)
                    kc = RC[0:m, 0:4] if j < NBLK else RC[0:m, 4:8]
                    dve.tensor_tensor(KD[0:m, :, :], PS[0:m, 2 + b // 3, 0:256].rearrange("p (a b) -> p a b", b=64), kc.unsqueeze(2).to_broadcast([m, 4, 64]), ALU.mult)
                    if j < NBLK:
                        last = dve.tensor_tensor(QD[:, :, :], R[:, 0:2, a:a + m], QDEC[:, :, :], ALU.mult)
                    else:
                        for pr in range(2):
                            last = dve.tensor_tensor(QD[:, pr, 0:m].rearrange("p (b t) -> p b t", t=NS), R[:, pr, a:a + m].rearrange("p (b t) -> p b t", t=NS),
                                                     QDEC_S[:, pr, :].unsqueeze(1).to_broadcast([P, NB, NS]), ALU.mult)
                    last.then_inc(a_taken.sem, 1)
                operands(0)
                for j in range(NBLK):
                    operands(j + 1)
                    dve.wait_ge(kv_ready.sem, kv_ready.at(j + 1))
                    kv = PS[:, 5, :].rearrange("p (a b) -> p a b", b=256)
                    dve.tensor_tensor(kv, kv, PAIR.unsqueeze(1).to_broadcast([P, 2, 256]), ALU.mult).then_inc(dve_own.sem, 1)
                    dve.wait_ge(dve_own.sem, dve_own.next())
                    for pr in range(2):
                        last = dve.scalar_tensor_tensor(STATE[(j + 1) % 2][:, pr, :], STATE[j % 2][:, pr, :], RC[:, 8 + pr:9 + pr], kv[:, pr, :], ALU.mult, ALU.add)
                    last.then_inc(s_ready.sem, 1)
                    dve.wait_ge(s_ready.sem, s_ready.at(j + 2))

            @block.scalar
            def _(act):
                for j, (a, m) in enumerate(TOK):
                    act.wait_ge(o_ready.sem, o_ready.at(j + 1))
                    act.activation(H[:, 0:4, a:a + m], PS[:, 3, :].rearrange("p (h n) -> p h n", n=P)[:, :, 0:m], ACT.Copy).then_inc(o_out.sem, 1)
        for c, n in ((a_ready, 9), (a_taken, 9), (o_ready, 9), (o_out, 9), (kv_ready, 8), (s_ready, 9)):
            c.adds(n)
    run(retention)

    def new_sample_states():
        spread, made, updated = count("spread"), count("states_made"), count("states_updated")
        VBD = view(Rf, 0, 2, NB, 256)
        KD = view(COS[:, :], 512, 2, P)
        with nc.Block() as block:
            @block.vector
            def _(dve):
                for pr in range(2):
                    dve.tensor_tensor(VBD[0:S, pr], VA[0:S, 8, pr * 256:(pr + 1) * 256].unsqueeze(1).to_broadcast([S, NB, 256]),
                                      RC[0:S, 12:20].unsqueeze(2).to_broadcast([S, NB, 256]), ALU.mult).then_inc(spread.sem, 1)
                for pr in range(2):
                    for c in range(4):
                        dve.wait_ge(made.sem, made.at(pr * 4 + c + 1))
                        s = SAMPLE_STATE[:, 2 * c:2 * c + 2, pr, :]
                        dve.scalar_tensor_tensor(s, s, RC[:, 10 + pr:11 + pr], PS[:, pr * 4 + c, :].rearrange("p (a b) -> p a b", b=256),
                                                 ALU.mult, ALU.add).then_inc(updated.sem, 1)

            @block.tensor
            def _(pe):
                for pr in range(2):
                    pe.wait_ge(spread.sem, spread.at(pr + 1))
                    for c in range(4):
                        pe.matmul(PS[:, pr * 4 + c, :], KD[0:S, pr, :], VBD[0:S, pr, 2 * c:2 * c + 2, :].rearrange("p a b -> p (a b)"), start=True, stop=True).then_inc(made.sem, 1)

            @block.sync
            def _(sp):
                out = io["ret_state_prompt"].rearrange("(t e) k v -> t e k v", e=2)
                for hh in range(2):
                    g.store(sp, out[:, hh].rearrange("t k v -> k t v"), STATE[NBLK % 2][64 * hh:64 * hh + 64, :, hh * P:(hh + 1) * P])
                sp.wait_ge(updated.sem, updated.at(8))
                out = io["ret_state_sample"].rearrange("b (t e) k v -> t e k b v", e=2)
                for pr in range(2):
                    for hh in range(2):
                        g.store(sp, out[pr, hh], SAMPLE_STATE[64 * hh:64 * hh + 64, :, pr, hh * P:(hh + 1) * P])
                sp.wait_ge(g.stored.sem, g.stored.at(g.stores[0]))
        for c, n in ((spread, 2), (made, 8), (updated, 8)):
            c.adds(n)
    run(new_sample_states)
    run(g.tile_norm, [H[:, h, :] for h in range(4)], [OT[:, h, :] for h in range(4)], g.ONES128[:, :], [COL[:, h:h + 1] for h in range(4)],
        [H[:, 4 + i, :] for i in range(4)], center=True, times=[OT[:, h, :] for h in range(4)])

    WT, BT, TRI = view(MASK[:, :], 0, 4, P), view(MASK[:, :], 512, 4, P), view(MASK[:, :], 1024, P)
    WTS = MASK[0:S, 1152:1408].rearrange("p (g t) -> p g t", t=S)
    GB, TRIS, BTS = COS[:, 0:512], COS[0:S, 512:576], view(COS[:, :], 576, 4, NS)
    run(g.load, [(WT, io["mlp_wT"].rearrange("g s t -> s g t")), (BT, io["mlp_b_s"].partition_broadcast(P)), (TRI, io["tri"]),
                 (WTS, io["mlp_wTs"].rearrange("g s t -> s g t")), (GB, io["mlp_norm_g"].partition_broadcast(P)), (TRIS, io["tri_s"]),
                 (BTS, io["mlp_b_s"].partition_broadcast(P)[:, :, 0:NS])])

    def gate_norm():
        centered, squared, var, rooted, rows = (count(n) for n in ("gate_centered", "gate_squared", "gate_var", "gate_rooted", "gate_rows"))
        V3 = VB.rearrange("p n (g d) -> p (n g) d", d=P)
        SQ = view(Hf, 0, 36, P)
        mean, inv = SM[:, 0:36], SM[:, 36:72]
        with nc.Block() as block:
            @block.vector
            def _(dve):
                dve.tensor_reduce(mean, V3, AX.X, ALU.add).then_inc(dve_own.sem, 1)
                dve.wait_ge(dve_own.sem, dve_own.next())
                dve.tensor_scalar(mean, mean, 1.0 / P, None, ALU.mult).then_inc(dve_own.sem, 1)
                dve.wait_ge(dve_own.sem, dve_own.next())
                dve.tensor_tensor(V3, V3, mean.unsqueeze(2).to_broadcast([P, 36, P]), ALU.subtract).then_inc(centered.sem, 1)
                dve.tensor_tensor(WT, WT, TRI.unsqueeze(1).to_broadcast([P, 4, P]), ALU.mult)
                dve.tensor_tensor(WTS, WTS, TRIS.unsqueeze(1).to_broadcast([S, 4, S]), ALU.mult)
                dve.wait_ge(squared.sem, squared.at(1))
                dve.tensor_reduce(inv, SQ, AX.X, ALU.add).then_inc(var.sem, 1)
                dve.wait_ge(rooted.sem, rooted.at(1))
                dve.reciprocal(inv, inv).then_inc(dve_own.sem, 1)
                dve.wait_ge(dve_own.sem, dve_own.next())
                dve.tensor_tensor(V3, V3, inv.unsqueeze(2).to_broadcast([P, 36, P]), ALU.mult).then_inc(dve_own.sem, 1)
                dve.wait_ge(dve_own.sem, dve_own.next())
                dve.tensor_tensor(VB, VB, GB.unsqueeze(1).to_broadcast([P, 9, 512]), ALU.mult).then_inc(rows.sem, 1)

            @block.scalar
            def _(act):
                act.wait_ge(centered.sem, centered.at(1))
                act.activation(SQ, V3, ACT.Square).then_inc(squared.sem, 1)
                act.wait_ge(var.sem, var.at(1))
                act.activation(inv, inv, ACT.Sqrt, scale=1.0 / P, bias=g.EPSC[:, 0:1]).then_inc(rooted.sem, 1)

            @block.sync
            def _(sp):
                sp.wait_ge(rows.sem, rows.at(1))
                g.store(sp, io["chunk_v_sample"], VB[0:S, 8, :])
                sp.wait_ge(g.stored.sem, g.stored.at(g.stores[0]))
        for c in (centered, squared, var, rooted, rows):
            c.adds(1)
    run(gate_norm)

    def gate_mix():
        mixed, taken = count("gate_mixed"), count("gate_taken")
        with nc.Block() as block:
            @block.tensor
            def _(pe):
                for j, (a, m) in enumerate(TOK):
                    if j >= 2:
                        pe.wait_ge(taken.sem, taken.at(j - 1))
                    w = WT if j < NBLK else WTS
                    for q in range(4):
                        last = pe.matmul(PS[:, j % 2, q * P:q * P + m], VB[0:m, j, q * P:(q + 1) * P], w[0:m, q, 0:m], start=True, stop=True)
                    last.then_inc(mixed.sem, 1)

            @block.vector
            def _(dve):
                for j, (a, m) in enumerate(TOK):
                    dve.wait_ge(mixed.sem, mixed.at(j + 1))
                    ps = PS[:, j % 2, :].rearrange("p (g t) -> p g t", t=P)
                    tmp = view(Hf, (j % 2) * 512, 4, P)
                    if j < NBLK:
                        last = dve.tensor_tensor(tmp, ps, BT, ALU.add)
                    else:
                        for q in range(4):
                            last = dve.tensor_tensor(tmp[:, q, 0:S].rearrange("p (b t) -> p b t", t=NS), ps[:, q, 0:S].rearrange("p (b t) -> p b t", t=NS),
                                                     BTS[:, q, :].unsqueeze(1).to_broadcast([P, NB, NS]), ALU.add)
                    last.then_inc(taken.sem, 1)
                    dve.wait_ge(taken.sem, taken.at(j + 1))
                    dve.tensor_tensor(OT[:, 4:8, a:a + m], OT[:, 4:8, a:a + m], tmp[:, :, 0:m], ALU.mult)
        mixed.adds(9)
        taken.adds(9)
    run(gate_mix)
    run(g.project, out[0], HHL, KT, 8, To(residual=True), then=g.columns(io["mem_w_kv"][0], KT, 8), lead=Lead([OT[:, t, :] for t in range(KT)], reload=io["xT"]))


def _attend(nc, g, units, scale, room):
    count, PS, view, Hf, SM, dve_own = g.count, g.PS, g.view, g.Hf, g.SM, g.dve_own
    scored, peaked, exped, normed, turned, pt_ready, out_ready, out_taken = (count("att_" + n) for n in (
        "scored", "peaked", "exped", "normed", "turned", "pt_ready", "out_ready", "out_taken"))
    n = len(units)
    outs, k = [], 0
    for u in units:
        k += u.last
        outs.append(k)

    def probs(u):
        return view(room, (u % 2) * 1024, 4, 256) if units[u].G > 1 else view(room, (u % 2) * 1024, 1, 256)

    def turned_probs(u):
        return view(room, 2048 + (u % 2) * 1024, 2, 4, P)

    def stat(u, k):
        return SM[:, (u % 2) * 32 + 4 * k:(u % 2) * 32 + 4 * k + 4]

    def ps_scores(u):
        b = 2 * (u % 2)
        return g.PSf[:, b * 512:b * 512 + 1024].rearrange("p (g w) -> p g w", w=256)
    with nc.Block() as block:
        @block.tensor
        def _(pe):
            def scores(u):
                if u >= 2:
                    pe.wait_ge(exped.sem, exped.at(u - 1))
                units[u].scores(pe, ps_scores(u)).then_inc(scored.sem, 1)

            def turn(u):
                pe.wait_ge(normed.sem, normed.at(u + 1))
                if u >= 1:
                    pe.wait_ge(pt_ready.sem, pt_ready.at(u))
                x = units[u]
                for kt, (a, m) in enumerate(x.keys):
                    for q in range(x.G):
                        last = pe.transpose(PS[0:m, 4 + kt, q * P:q * P + x.rows], probs(u)[0:x.rows, q, a:a + m], g.IDENT[0:x.rows, 0:x.rows])
                last.then_inc(turned.sem, 1)

            def outputs(u):
                pe.wait_ge(pt_ready.sem, pt_ready.at(u + 1))
                x = units[u]
                if x.first and outs[u] - x.last >= 2:
                    pe.wait_ge(out_taken.sem, out_taken.at(outs[u] - x.last - 1))
                x.outputs(pe, turned_probs(u), 6 + x.bank).then_inc(out_ready.sem, 1)
            scores(0)
            for u in range(n):
                if u + 1 < n:
                    scores(u + 1)
                if u:
                    outputs(u - 1)
                turn(u)
            outputs(n - 1)

        @block.vector
        def _(dve):
            def peak(u):
                x = units[u]
                r = x.rows
                dve.wait_ge(scored.sem, scored.at(u + 1))
                s = ps_scores(u)[0:r, 0:x.G, 0:x.W]
                if x.mask is not None:
                    if u >= 2:
                        dve.wait_ge(turned.sem, turned.at(u - 1))
                    p = probs(u)[0:r, :, 0:x.W]
                    dve.tensor_tensor(p, s, x.mask, ALU.add).then_inc(dve_own.sem, 1)
                    dve.wait_ge(dve_own.sem, dve_own.next())
                    s = p
                mx, nm, df = stat(u, 0)[0:r, 0:x.G], stat(u, 1)[0:r, 0:x.G], stat(u, 2)[0:r, 0:x.G]
                dve.tensor_reduce(mx, s, AX.X, ALU.max).then_inc(dve_own.sem, 1)
                dve.wait_ge(dve_own.sem, dve_own.next())
                if x.sink is None:
                    last = dve.tensor_scalar(nm, mx, -scale, None, ALU.mult)
                else:
                    dve.scalar_tensor_tensor(nm, mx, -scale, x.sink, ALU.mult, ALU.min).then_inc(dve_own.sem, 1)
                    dve.wait_ge(dve_own.sem, dve_own.next())
                    last = dve.tensor_tensor(df, nm, x.sink, ALU.subtract)
                last.then_inc(peaked.sem, 1)

            def norm(u):
                x = units[u]
                r = x.rows
                dve.wait_ge(exped.sem, exped.at(u + 1))
                es, l, inv = (stat(u, k)[0:r, 0:x.G] for k in (3, 4, 5))
                if x.sink is not None:
                    dve.tensor_tensor(l, l, es, ALU.add).then_inc(dve_own.sem, 1)
                    dve.wait_ge(dve_own.sem, dve_own.next())
                dve.reciprocal(inv, l).then_inc(dve_own.sem, 1)
                dve.wait_ge(dve_own.sem, dve_own.next())
                p = probs(u)[0:r, :, 0:x.W]
                dve.tensor_tensor(p, p, inv.unsqueeze(2).to_broadcast([r, x.G, x.W]), ALU.mult).then_inc(normed.sem, 1)
            peak(0)
            for u in range(n):
                if u + 1 < n:
                    peak(u + 1)
                norm(u)

        @block.scalar
        def _(act):
            def place(u):
                if units[u].last:
                    act.wait_ge(out_ready.sem, out_ready.at(u + 1))
                    units[u].place(act, 6 + units[u].bank).then_inc(out_taken.sem, 1)
            for u in range(n + 2):
                if u < n:
                    x = units[u]
                    r = x.rows
                    act.wait_ge(peaked.sem, peaked.at(u + 1))
                    if u >= 2:
                        act.wait_ge(turned.sem, turned.at(u - 1))
                    for q in range(x.G):
                        src = ps_scores(u)[0:r, q, 0:x.W] if x.mask is None else probs(u)[0:r, q, 0:x.W]
                        last = act.activation(probs(u)[0:r, q, 0:x.W], src, ACT.Exp, bias=stat(u, 1)[0:r, q:q + 1], scale=scale,
                                              accum_out=stat(u, 4)[0:r, q:q + 1])
                    if x.sink is not None:
                        last = act.activation(stat(u, 3)[0:r, 0:x.G], stat(u, 2)[0:r, 0:x.G], ACT.Exp)
                    last.then_inc(exped.sem, 1)
                if 1 <= u <= n:
                    v = u - 1
                    act.wait_ge(turned.sem, turned.at(v + 1))
                    if v >= 2:
                        act.wait_ge(out_ready.sem, out_ready.at(v - 1))
                    x = units[v]
                    for kt, (a, m) in enumerate(x.keys):
                        w = x.G * P if x.G > 1 else x.rows
                        last = act.activation(turned_probs(v)[0:m, kt].rearrange("p a b -> p (a b)")[:, 0:w], PS[0:m, 4 + kt, 0:w], ACT.Copy)
                    last.then_inc(pt_ready.sem, 1)
                if u >= 2:
                    place(u - 2)
    for c in (scored, peaked, exped, normed, turned, pt_ready, out_ready):
        c.adds(n)
    out_taken.adds(outs[-1])


class Unit:
    def __init__(self, rows, G, W, keys, scores, outputs, place, bank, first=True, last=True, mask=None, sink=None):
        self.rows, self.G, self.W, self.keys, self.scores, self.outputs, self.place = rows, G, W, keys, scores, outputs, place
        self.bank, self.first, self.last, self.mask, self.sink = bank, first, last, mask, sink


def _memory(nc, io, env, run, l):
    g = env
    H, OT, R, Rf, Hf, OTf, view, COL = g.H, g.OT, g.R, g.Rf, g.Hf, g.OTf, g.view, g.COL
    MT, MK, MV = view(Rf, 4096, KT, MEM), view(Rf, 0, HEADS, MEM), view(Rf, 1024, 2, 512)
    MTH, MTL = view(g.HHf, 0, KT, MEM), view(g.HLf, 0, KT, MEM)
    Q, OUT = R[:, 4:8, :], R[:, 9:13, :]
    QZ = [view(Rf, 2048, 8, P), view(Rf, 3072, 8, P), view(g.Wf, 3 * D, 8, P), view(g.Wf, 5 * D, 8, P)]
    CST = g.CST
    w_kv = io["mem_w_kv"][l]
    cached = [g.count(f"memory_cached{bt}") for bt in range(2)]
    run(g.load, [(MT, io["memT"].rearrange("(k p) m -> p k m", p=P)), (COL[:, 8:9], io["mem_knorm_g"][l]), (COL[:, 9:10], io["mem_qnorm_g"][l])])

    def split_memory():
        halved = g.count("memory_halved")
        with nc.Block() as block:
            @block.scalar
            def _(act):
                act.activation(MTH, MT, ACT.Copy).then_inc(halved.sem, 1)

            @block.vector
            def _(dve):
                dve.wait_ge(halved.sem, halved.at(1))
                dve.tensor_tensor(MTL, MT, MTH.bitcast(F32), ALU.subtract)
        halved.adds(1)
    run(split_memory)

    KV = view(CST, 0, KT, MEM)
    w_q, w_o = g.columns(io["mem_w_q"][l], KT, 4), g.columns(io["mem_w_o"][l], 4, 8)
    run(g.project, g.columns(w_kv, KT)[0], (MTH, MTL), KT, 8, To(KV, 0), spans=((0, MEM),), then=w_q, split_on="vector")
    run(g.turn_rows, [([KV[:, 4 + h, kt * P:(kt + 1) * P] for h in range(4)], [(MV[:, kt, :].rearrange("p (h n) -> p h n", n=P), slice(0, P))]) for kt in range(2)])
    run(g.tile_norm, [KV[:, h, :] for h in range(4)], [MK[:, h, :] for h in range(4)], g.ONES128[:, :], [COL[:, 8:9]] * 4,
        [CST[:, 2048 + i * MEM:2048 + (i + 1) * MEM] for i in range(4)], width=MEM)
    INV = R[:, 12, :]
    scratch = [CST[:, i * T:(i + 1) * T] for i in range(4)]
    run(g.project, w_q[0], (g.HH, g.HL), KT, 4, To(R, 4, times=INV), then=w_o, lead=Lead([g.X[:, k, :] for k in range(KT)], gain=KT, inv=INV))

    def fetch_caches():
        with nc.Block() as block:
            @block.sync
            def _(sp):
                for bt in range(2):
                    for dst, src in caches(bt):
                        sp.dma_start(dst, src).then_inc(cached[bt].sem, 16)

            @block.gpsimd
            def _(pool):
                for z in QZ:
                    nc.gpsimd.memset(z, 0.0)

    def caches(bt):
        b = slice(4 * bt, 4 * bt + 4)
        return [(view(Hf, bt * 8192, 16, MEM), io["cache_mem_kT"][l, b].rearrange("b h d m -> d (b h) m")),
                (view(Hf, bt * 8192 + 4096, 8, 512), io["cache_mem_v"][l, b].rearrange("b (k p) n -> p (b k) n", p=P))]
    run(fetch_caches)
    run(g.tile_norm, [Q[:, h, :] for h in range(4)], [Q[:, h, :] for h in range(4)], g.ONES128[:, :], [COL[:, 9:10]] * 4, scratch)

    def prompt_unit(j):
        a = j * P

        def scores(pe, ps):
            for h in range(HEADS):
                last = pe.matmul(ps[:, h, :], Q[:, h, a:a + P], MK[:, h, :], start=True, stop=True)
            return last

        def outputs(pe, pt, bank):
            for h in range(HEADS):
                for kt in range(2):
                    last = pe.matmul(g.PS[:, bank, h * P:(h + 1) * P], MV[:, kt, h * P:(h + 1) * P], pt[:, kt, h, :], start=(kt == 0), stop=(kt == 1))
            return last

        def place(act, bank):
            return act.activation(OUT[:, :, a:a + P], g.PS[:, bank, :].rearrange("p (h n) -> p h n", n=P), ACT.Copy)
        return Unit(P, HEADS, MEM, [(0, P), (P, P)], scores, outputs, place, j % 2)

    def sample_unit(bt, bank):
        KC, VC = view(Hf, bt * 8192, 16, MEM), view(Hf, bt * 8192 + 4096, 8, 512)

        def scores(pe, ps):
            pe.wait_ge(cached[bt].sem, cached[bt].at(32))
            for i in range(16):
                last = pe.matmul(ps[:, 0, :], QZ[2 * bt + i // 8][:, i % 8, :], KC[:, i, :], start=(i == 0), stop=(i == 15))
            return last

        def outputs(pe, pt, bank):
            for i in range(16):
                for kt in range(2):
                    last = pe.matmul(g.PS[:, bank, i * NS:(i + 1) * NS], VC[:, (i // 4) * 2 + kt, (i % 4) * P:(i % 4 + 1) * P],
                                     pt[:, kt, 0, i * NS:(i + 1) * NS], start=(kt == 0), stop=(kt == 1))
            return last

        def place(act, bank):
            a = SEQ + bt * 32
            return act.activation(OUT[:, :, a:a + 32].rearrange("p h (b t) -> p h b t", t=NS),
                                  g.PS[:, bank, 0:P].rearrange("p (b h t) -> p h b t", h=4, t=NS), ACT.Copy)
        return Unit(P, 1, MEM, [(0, P), (P, P)], scores, outputs, place, bank)

    def spread_queries():
        with nc.Block() as block:
            @block.vector
            def _(dve):
                for b in range(NB):
                    for h in range(HEADS):
                        i = (b % 4) * HEADS + h
                        dve.tensor_copy(QZ[2 * (b // 4) + i // 8][:, i % 8, i * NS:(i + 1) * NS], Q[:, h, SEQ + b * NS:SEQ + (b + 1) * NS])
    run(spread_queries)
    run(_attend, nc, g, [prompt_unit(j) for j in range(NBLK)] + [sample_unit(0, 0), sample_unit(1, 1)], HD_X ** -0.5, CST)
    for c in cached:
        c.adds(32)

    def keep_memory():
        with nc.Block() as block:
            @block.sync
            def _(sp):
                g.store(sp, io["mem_kT_prompt"][l].rearrange("h d m -> d h m"), MK)
                g.store(sp, io["mem_v_prompt"][l].rearrange("(k p) n -> p k n", p=P), MV)
                sp.wait_ge(g.stored.sem, g.stored.at(g.stores[0]))
    run(keep_memory)
    run(g.project, w_o[0], (g.HH, g.HL), 4, 8, To(residual=True), then=_gate_and_up(g, io, l, 0, PART), lead=Lead([OUT[:, h, :] for h in range(HEADS)]))


HD_X = 128


def _feed_forward(nc, io, env, run, l):
    g = env
    X, H, OT, R, OTf, PS, view, count, dve_own, act_own = g.X, g.H, g.OT, g.R, g.OTf, g.PS, g.view, g.count, g.dve_own, g.act_own
    GW = 2 + SEQ + NB * (2 + NS)
    GATE = [g.CST[:, i * GW:(i + 1) * GW] for i in range(2)]
    CONV = [g.CST[:, 2 * GW + i * T:2 * GW + (i + 1) * T] for i in range(2)]
    at = 2 * GW + 2 * T
    PAST = view(g.CST, at, FT, NB * 2)
    TAPS = view(g.CST, at + FT * 16, FT, 4)
    KEEP = view(g.CST, at + FT * 20, FT, 18)
    INV = R[:, 12, :]
    run(g.load, [(PAST, io["conv_past"][l]), (TAPS, io["conv_taps"][l])], zero=tuple(x[:, 0:2] for x in GATE))

    parts, o = [], 0
    for first in range(0, FT, PART):
        tiles = min(PART, FT - first)
        parts.append((first, tiles, o, o + 2 * tiles))
        o += 2 * tiles + 8
    total = o

    def steps():
        ws = []
        for first, tiles, o_hidden, o_down in parts:
            ws.append((_gate_and_up(g, io, l, first, tiles), KT, o_hidden))
            ws.append((g.columns(io["ffn_w_down"][l, first * P:(first + tiles) * P, :], tiles, 8), tiles, o_down))
        last = g.columns(io["od_w_in"][:, 1024:1536], KT, 4) if l == 0 else None
        return [(w, kt, o, (ws[i + 1][0] if i + 1 < len(ws) else last)) for i, (w, kt, o) in enumerate(ws)]

    def feed_forward():
        convolved, gelued, made = count("ff_convolved"), count("ff_gelued"), count("ff_made")
        full, free = g.tile_full, g.tile_free
        lead = Lead([X[:, k, :] for k in range(KT)], gain=2 * KT, inv=INV)
        skip = g.ahead[0]
        g.ahead[0] = l == 0
        with nc.Block() as block:
            @block.sync
            def _(sp):
                for (pick, chunks), kt, o, then in steps():
                    g.load_weights(sp, pick, chunks, then, o)
                sp.wait_ge(convolved.sem, convolved.at(FT))
                g.store(sp, io["ffn_conv"][l], KEEP)
                if l == 1:
                    for c in range(KT):
                        sp.wait_ge(free.sem, free.at(parts[-1][3] + c + 1))
                        g.store(sp, io["yT"][c * P:(c + 1) * P, :], X[:, c, :])
                sp.wait_ge(g.stored.sem, g.stored.at(g.stores[0]))

            @block.gpsimd
            def _(pool):
                for i, ((pick, chunks), kt, o, then) in enumerate(steps()):
                    g.split_weights(nc.gpsimd, kt, chunks, skip if i == 0 else True, o)
                    g.split_ahead(pool, chunks, then, o)

            @block.tensor
            def _(pe):
                def tile_halved(k):
                    pe.wait_ge(g.lo_made.sem, g.lo_made.at(k + 1))
                for first, tiles, o_hidden, o_down in parts:
                    def tile_made(k):
                        pe.wait_ge(made.sem, made.at(first + k + 1))
                    g.products(pe, (g.HH, g.HL), KT, 2 * tiles, SPANS, None if first else tile_halved, not first, o=o_hidden)
                    g.products(pe, (g.HIDH, g.HIDL), tiles, 8, SPANS, tile_made, o=o_down)

            @block.scalar
            def _(act):
                g.lead_scalar(act, lead)
                with act.Fori(0, FT // 2) as i:
                    for t in range(2):
                        act.wait_ge(convolved.sem, convolved.at(i * 2 + (t + 1)))
                        act.activation(CONV[t], CONV[t], ACT.Gelu).then_inc(gelued.sem, 1)

            def onto_residual(dve, c, s, o):
                dve.wait_ge(full.sem, full.at(c + (o + 1)))
                for ps, a, m, rows in g.pieces(3 * s):
                    x = g.cut(X, c, a, m, rows)
                    last = dve.tensor_tensor(x, ps, x, ALU.add)
                last.then_inc(free.sem, 1)

            def hidden_tile(dve, i, t, first, o):
                G, C = GATE[t], CONV[t]
                f = i * 2 + (first + t)

                def tap(k):
                    return TAPS[:, bass.ds(f, 1), k:k + 1].rearrange("p a b -> p (a b)")
                SG = G[:, 2 + SEQ:GW].rearrange("p (b t) -> p b t", t=2 + NS)
                SC = C[:, SEQ:T].rearrange("p (b t) -> p b t", t=NS)
                dve.tensor_copy(SG[:, :, 0:2], PAST[:, bass.ds(f, 1), :].rearrange("p a (b t) -> p (a b) t", t=2)).then_inc(dve_own.sem, 1)
                dve_own.next()
                dve.wait_ge(full.sem, full.at(i * 4 + (o + 2 * t + 1)))
                dve.tensor_tensor(G[:, 2:770].rearrange("p (r b) -> p r b", r=2), PS[:, 0:2, 0:384],
                                  INV[:, 0:768].rearrange("p (r b) -> p r b", r=2), ALU.mult)
                dve.tensor_tensor(G[:, 770:2 + SEQ], PS[:, 2, 0:256], INV[:, 768:SEQ], ALU.mult)
                dve.tensor_tensor(SG[:, :, 2:2 + NS], PS[:, 2, 256:320].rearrange("p (b t) -> p b t", t=NS),
                                  INV[:, SEQ:T].rearrange("p (b t) -> p b t", t=NS), ALU.mult).then_inc(free.sem, 1)
                dve.wait_ge(free.sem, free.at(i * 4 + (o + 2 * t + 1)))
                dve.wait_ge(dve_own.sem, dve_own.now())
                dve.tensor_scalar(C[:, 0:SEQ], G[:, 0:SEQ], tap(0), tap(3), ALU.mult, ALU.add)
                dve.tensor_scalar(SC, SG[:, :, 0:NS], tap(0), tap(3), ALU.mult, ALU.add).then_inc(dve_own.sem, 1)
                dve.wait_ge(dve_own.sem, dve_own.next())
                dve.scalar_tensor_tensor(C[:, 0:SEQ], G[:, 1:1 + SEQ], tap(1), C[:, 0:SEQ], ALU.mult, ALU.add)
                dve.scalar_tensor_tensor(SC, SG[:, :, 1:1 + NS], tap(1), SC, ALU.mult, ALU.add).then_inc(dve_own.sem, 1)
                dve.wait_ge(dve_own.sem, dve_own.next())
                dve.scalar_tensor_tensor(C[:, 0:SEQ], G[:, 2:2 + SEQ], tap(2), C[:, 0:SEQ], ALU.mult, ALU.add)
                dve.scalar_tensor_tensor(SC, SG[:, :, 2:2 + NS], tap(2), SC, ALU.mult, ALU.add)
                keep = KEEP[:, bass.ds(f, 1), :].rearrange("p a b -> p (a b)")
                dve.tensor_copy(keep[:, 0:2], G[:, SEQ:SEQ + 2])
                dve.tensor_copy(keep[:, 2:18].rearrange("p (b t) -> p b t", t=2), SG[:, :, NS:NS + 2]).then_inc(convolved.sem, 1)
                dve.wait_ge(gelued.sem, gelued.at(i * 2 + (first + t + 1)))
                dve.wait_ge(full.sem, full.at(i * 4 + (o + 2 * t + 2)))
                for ps, a, m, rows in g.pieces(3):
                    c = C[:, a:a + m].rearrange("p (r b) -> p r b", r=rows) if rows > 1 else C[:, a:a + m]
                    last = dve.tensor_tensor(c, ps, c, ALU.mult)
                last.then_inc(free.sem, 1)
                dve.wait_ge(free.sem, free.at(i * 4 + (o + 2 * t + 2)))
                dve.tensor_tensor(C, C, INV, ALU.mult).then_inc(dve_own.sem, 1)
                dve.wait_ge(dve_own.sem, dve_own.next())
                hi, lo = (b[:, bass.ds(i * 2 + t, 1), :].rearrange("p a b -> p (a b)") for b in (g.HIDH, g.HIDL))
                dve.tensor_copy(hi, C).then_inc(dve_own.sem, 1)
                dve.wait_ge(dve_own.sem, dve_own.next())
                dve.tensor_tensor(lo, C, hi.bitcast(F32), ALU.subtract).then_inc(made.sem, 1)

            @block.vector
            def _(dve):
                g.lead_vector(dve, lead)
                for first, tiles, o_hidden, o_down in parts:
                    with dve.Fori(0, tiles // 2) as i:
                        dve_own.enter(i, 2 * 5)
                        for t in range(2):
                            hidden_tile(dve, i, t, first, o_hidden)
                    dve_own.leave(tiles // 2)
                    g.rounds(dve, 8, lambda c, s, i: onto_residual(dve, c, s, o_down))
        for c in (convolved, gelued, made):
            c.adds(FT)
        g.counted(total)
        g.lead_counted(lead)
    run(feed_forward)


def _gate_and_up(g, io, l, first, tiles):
    ws = io["ffn_w_gate"][l], io["ffn_w_up"][l]
    return (lambda c, s, i: (g.chunk(ws[s], KT, i + first), KT)), 2 * tiles


def _layer1(nc, io, env, run):
    g = env
    X, H, OT, R, Rf, Hf, OTf, PS, PSf, view, count = g.X, g.H, g.OT, g.R, g.Rf, g.Hf, g.OTf, g.PS, g.PSf, g.view, g.count
    MASK, COS, SIN, COL, SM, IDENT, SPARE = g.MASK, g.COS, g.SIN, g.COL, g.SM, g.IDENT, g.SPARE
    act_own, dve_own = g.act_own, g.dve_own
    HHL = (g.HH, g.HL)
    IC = view(Rf, 8 * T, 9, 512)
    LMASK = view(MASK[:, :], 0, LEVELS + 1, P)
    RESET = SPARE[:, 0, :]
    w_in = io["od_w_in"]
    WSf = [g.Wf[:, 0:2048], g.Wf[:, 2048:4096]]
    run(g.load, [(g.GAIN[:, :], io["gain1"]), (MASK[:, 0:1024], io["hgrn_masks"]), (RESET, io["hgrn_reset"]),
                 (COL[:, 12:16], io["hgrn_onorm_g"]), (COL[:, 16:24], io["hgrn_lb_logits"])])

    def lower_bound():
        peaked, exped = count("lb_peaked"), count("lb_exped")
        a, b, m = COL[:, 16:20], COL[:, 20:24], COL[:, 24:28]
        with nc.Block() as block:
            @block.vector
            def _(dve):
                dve.tensor_tensor(m, a, b, ALU.max).then_inc(dve_own.sem, 1)
                dve.wait_ge(dve_own.sem, dve_own.next())
                dve.tensor_tensor(a, a, m, ALU.subtract)
                dve.tensor_tensor(b, b, m, ALU.subtract).then_inc(peaked.sem, 1)
                dve.wait_ge(exped.sem, exped.at(1))
                dve.tensor_tensor(m, a, b, ALU.add).then_inc(dve_own.sem, 1)
                dve.wait_ge(dve_own.sem, dve_own.next())
                dve.reciprocal(m, m).then_inc(dve_own.sem, 1)
                dve.wait_ge(dve_own.sem, dve_own.next())
                dve.tensor_tensor(b, b, m, ALU.mult).then_inc(dve_own.sem, 1)
                dve.wait_ge(dve_own.sem, dve_own.next())
                dve.tensor_scalar(a, b, -1.0, 1.0, ALU.mult, ALU.add)

            @block.scalar
            def _(act):
                act.wait_ge(peaked.sem, peaked.at(1))
                act.activation(COL[:, 16:24], COL[:, 16:24], ACT.Exp).then_inc(exped.sem, 1)
        peaked.adds(1)
        exped.adds(1)
    run(lower_bound)
    INV = SPARE[:, 1, :]
    ws = [g.columns(w_in[:, 512 * i:512 * (i + 1)], KT, 4) for i in range(5)]
    run(g.project, ws[2][0], HHL, KT, 4, To(OT, times=INV, rows=IC), then=ws[0], lead=Lead([X[:, k, :] for k in range(KT)], gain=0, inv=INV, spill=True))
    run(g.project, ws[0][0], HHL, KT, 4, To(R, 0, func=ACT.Silu, times=INV), then=ws[1])
    run(g.project, ws[1][0], HHL, KT, 4, To(R, 4, func=ACT.Sigmoid, times=INV))

    def hgrn(h):
        q, k = R[:, h, :], R[:, 4 + h, :]
        B, LG = OT[:, 4, :], OT[:, 5, :]
        A = WSf[0][:, 0:T]
        KTS = WSf[0][:, T:T + P]
        CHAIN, S0 = view(WSf[1], 0, NBLK, P), view(WSf[1], 1024, NB, P)
        KTK = view(COS[:, :], 0, NBLK, P)
        VBD = view(SIN[:, :], 0, NB, P)
        E = [OT[:, 5, :], OT[:, 7, :]]
        QE = [OT[:, 6, :], g.Wf[:, 4096:4096 + T]]
        logged, forgot, summed = (count("hg_" + n) for n in ("logged", "forgot", "summed"))
        offset, decayed, paired, scored, masked = (count("hg_" + n) for n in ("offset", "decayed", "paired", "scored", "masked"))
        lo = COL[:, 16 + h:17 + h]
        bound = COL[:, 20 + h:21 + h]

        def blocks(v, lv, flat=False):
            s2 = 2 ** lv
            n = T if s2 <= NS else SEQ
            return v[:, 0:n].rearrange("p (b t) -> p b t", t=s2), n

        def intra():
            with nc.Block() as block:
                @block.vector
                def _(dve):
                    dve.tensor_scalar(k, k, lo, bound, ALU.mult, ALU.add).then_inc(dve_own.sem, 1)
                    dve.wait_ge(dve_own.sem, dve_own.next())
                    dve.tensor_scalar(LG, k, 2.0 ** -64, None, ALU.max).then_inc(forgot.sem, 1)
                    dve.tensor_scalar(k, k, -1.0, 1.0, ALU.mult, ALU.add).then_inc(dve_own.sem, 1)
                    dve.wait_ge(dve_own.sem, dve_own.next())
                    dve.wait_ge(logged.sem, logged.at(1))
                    dve.tensor_tensor_scan(B, RESET, LG, 0.0, ALU.mult, ALU.add).then_inc(summed.sem, 1)
                    dve.wait_ge(summed.sem, summed.at(1))

                    def offsets(lv):
                        if lv > 2:
                            dve.wait_ge(scored.sem, scored.at(lv - 1))
                        bb, n = blocks(B, lv)
                        e, _ = blocks(E[lv % 2], lv)
                        mid = bb[:, :, 2 ** (lv - 1) - 1:2 ** (lv - 1)]
                        dve.tensor_tensor(e, bb, mid.to_broadcast(list(bb.shape)), ALU.subtract).then_inc(offset.sem, 1)

                    def pair(lv):
                        n = blocks(B, lv)[1]
                        dve.wait_ge(decayed.sem, decayed.at(lv))
                        e, x = E[lv % 2][:, 0:n], QE[lv % 2][:, 0:n]
                        dve.tensor_tensor(x, e, q[:, 0:n], ALU.mult)
                        dve.tensor_tensor(e, e, k[:, 0:n], ALU.mult).then_inc(paired.sem, 1)

                    def gather(lv):
                        dve.wait_ge(scored.sem, scored.at(lv + 1))
                        n = SEQ if lv and 2 ** lv > NS else T
                        b = 3 * (lv % 2)
                        ps = PSf[:, b * 512:b * 512 + SEQ].rearrange("p (j n) -> p j n", n=P)
                        ps_s = PS[0:S, b + 2, 0:S]
                        a3 = A[:, 0:SEQ].rearrange("p (j n) -> p j n", n=P)
                        m = LMASK[:, lv, :].unsqueeze(1).to_broadcast([P, NBLK, P])
                        out, out_s = (a3, A[0:S, SEQ:T]) if lv == 0 else (ps, ps_s)
                        last = dve.tensor_tensor(out, ps, m, ALU.mult)
                        if n == T:
                            last = dve.tensor_tensor(out_s, ps_s, LMASK[0:S, lv, 0:S], ALU.mult)
                        if lv:
                            last.then_inc(dve_own.sem, 1)
                            dve.wait_ge(dve_own.sem, dve_own.next())
                            last = dve.tensor_tensor(a3, a3, ps, ALU.add)
                            if n == T:
                                last = dve.tensor_tensor(A[0:S, SEQ:T], A[0:S, SEQ:T], ps_s, ALU.add)
                        last.then_inc(masked.sem, 1)
                        dve.wait_ge(masked.sem, masked.at(lv + 1))
                    offsets(1)
                    for lv in range(1, LEVELS + 1):
                        if lv < LEVELS:
                            offsets(lv + 1)
                        pair(lv)
                        gather(lv - 1)
                    gather(LEVELS)

                @block.scalar
                def _(act):
                    act.wait_ge(forgot.sem, forgot.at(1))
                    act.activation(LG, LG, ACT.Ln).then_inc(logged.sem, 1)
                    for lv in range(1, LEVELS + 1):
                        act.wait_ge(offset.sem, offset.at(lv))
                        e = E[lv % 2][:, 0:blocks(B, lv)[1]]
                        act.activation(e, e, ACT.Abs).then_inc(act_own.sem, 1)
                        act.wait_ge(act_own.sem, act_own.next())
                        act.activation(e, e, ACT.Exp, scale=-1.0).then_inc(decayed.sem, 1)

                @block.tensor
                def _(pe):
                    pe.wait_ge(summed.sem, summed.at(1))
                    for lv in range(LEVELS + 1):
                        if lv:
                            pe.wait_ge(paired.sem, paired.at(lv))
                        if lv >= 2:
                            pe.wait_ge(masked.sem, masked.at(lv - 1))
                        qq, kk = (QE[lv % 2], E[lv % 2]) if lv else (q, k)
                        b = 3 * (lv % 2)
                        for j, (a, m) in enumerate(TOK if lv <= 3 else TOK[:-1]):
                            ps = PSf[0:m, b * 512 + j * P:b * 512 + j * P + m]
                            last = pe.matmul(ps, kk[:, a:a + m], qq[:, a:a + m], start=True, stop=True)
                        last.then_inc(scored.sem, 1)
            for c, n in ((logged, 1), (forgot, 1), (summed, 1), (offset, LEVELS), (decayed, LEVELS), (paired, LEVELS),
                         (scored, LEVELS + 1), (masked, LEVELS + 1)):
                c.adds(n)

        EB, QB, KB, DB = OT[:, 5, :], OT[:, 6, :], OT[:, 7, :], g.Wf[:, 4096:4096 + T]

        def inter():
            start, bexp, dexp, qkd, turned, turned_out, kv, chained, o_ready, vspread, s_in = (count("hgi_" + n) for n in (
                "start", "exp_b", "exp_rest", "decayed", "turned", "turned_taken", "kv", "chained", "out", "spread", "updated"))
            v = IC[:, :, h * P:(h + 1) * P]
            with nc.Block() as block:
                @block.sync
                def _(sp):
                    sp.dma_start(S0, io["state_hgrn"].rearrange("b h k v -> h k b v")[h]).then_inc(g.loaded.sem, 16)
                    sp.wait_ge(g.loaded.sem, g.loaded.at(16))
                    sp.wait_ge(chained.sem, chained.at(NBLK))
                    g.store(sp, io["hgrn_state_prompt"][h], CHAIN[:, NBLK - 1, :])
                    sp.wait_ge(s_in.sem, s_in.at(2))
                    g.store(sp, io["hgrn_state_sample"].rearrange("b h k v -> h k b v")[h], S0)
                    sp.wait_ge(g.stored.sem, g.stored.at(g.stores[0]))

                @block.vector
                def _(dve):
                    b3, d3 = (x[:, 0:SEQ].rearrange("p (j n) -> p j n", n=P) for x in (B, DB))
                    dve.tensor_tensor(d3, b3, b3[:, :, P - 1:P].to_broadcast([P, NBLK, P]), ALU.subtract)
                    b3, d3 = (x[:, SEQ:T].rearrange("p (j n) -> p j n", n=NS) for x in (B, DB))
                    dve.tensor_tensor(d3, b3, b3[:, :, NS - 1:NS].to_broadcast([P, NB, NS]), ALU.subtract).then_inc(start.sem, 1)
                    dve.tensor_tensor(VBD[0:S], v[0:S, 8, :].unsqueeze(1).to_broadcast([S, NB, P]),
                                      io_onehot[0:S].unsqueeze(2).to_broadcast([S, NB, P]), ALU.mult).then_inc(vspread.sem, 1)
                    dve.wait_ge(bexp.sem, bexp.at(1))
                    dve.tensor_tensor(QB, q, EB, ALU.mult)
                    dve.wait_ge(dexp.sem, dexp.at(1))
                    dve.tensor_tensor(KB, k, DB, ALU.mult).then_inc(qkd.sem, 1)
                    dve.wait_ge(kv.sem, kv.at(1))
                    for j in range(NBLK):
                        ps = PSf[:, 4 * 512 + j * P:4 * 512 + (j + 1) * P]
                        if j == 0:
                            last = dve.tensor_copy(CHAIN[:, 0, :], ps)
                        else:
                            last = dve.scalar_tensor_tensor(CHAIN[:, j, :], CHAIN[:, j - 1, :], EB[:, (j + 1) * P - 1:(j + 1) * P], ps, ALU.mult, ALU.add)
                        last.then_inc(chained.sem, 1)
                        dve.wait_ge(chained.sem, chained.at(j + 1))
                    dve.wait_ge(g.loaded.sem, g.loaded.at(16))
                    ends = EB[:, SEQ:T].rearrange("p (b t) -> p b t", t=NS)[:, :, NS - 1:NS].to_broadcast([P, NB, P])
                    dve.wait_ge(o_ready.sem, o_ready.at(1))
                    dve.tensor_tensor(S0, S0, ends, ALU.mult).then_inc(dve_own.sem, 1)
                    dve.wait_ge(dve_own.sem, dve_own.next())
                    dve.wait_ge(kv.sem, kv.at(2))
                    for c in range(2):
                        s = S0[:, 4 * c:4 * c + 4, :]
                        dve.tensor_tensor(s, s, PS[:, 6 + c, :].rearrange("p (b v) -> p b v", v=P), ALU.add).then_inc(s_in.sem, 1)

                @block.scalar
                def _(act):
                    act.activation(EB, B, ACT.Exp).then_inc(bexp.sem, 1)
                    act.wait_ge(start.sem, start.at(1))
                    act.activation(DB, DB, ACT.Exp, scale=-1.0).then_inc(dexp.sem, 1)
                    act.wait_ge(turned.sem, turned.at(1))
                    act.activation(KTK, PSf[:, 0:SEQ].rearrange("p (j n) -> p j n", n=P), ACT.Copy)
                    act.activation(KTS[0:S, :], PS[0:S, 2, 0:P], ACT.Copy).then_inc(turned_out.sem, 1)
                    act.wait_ge(o_ready.sem, o_ready.at(1))
                    act.activation(OT[:, h, 0:SEQ], PSf[:, 0:SEQ], ACT.Copy)
                    act.activation(OT[:, h, SEQ:T], PS[:, 2, 0:S], ACT.Copy)

                @block.tensor
                def _(pe):
                    pe.wait_ge(qkd.sem, qkd.at(1))
                    for j, (a, m) in enumerate(TOK):
                        last = pe.transpose(PSf[0:m, j * P:(j + 1) * P], KB[:, a:a + m], IDENT[:, :])
                    last.then_inc(turned.sem, 1)
                    pe.wait_ge(turned_out.sem, turned_out.at(1))
                    for j in range(NBLK):
                        last = pe.matmul(PSf[:, 4 * 512 + j * P:4 * 512 + (j + 1) * P], KTK[:, j, :], v[:, j, :], start=True, stop=True)
                    last.then_inc(kv.sem, 1)
                    pe.wait_ge(vspread.sem, vspread.at(1))
                    for c in range(2):
                        last = pe.matmul(PS[:, 6 + c, :], KTS[0:S, :], VBD[0:S, 4 * c:4 * c + 4, :].rearrange("p a b -> p (a b)"), start=True, stop=True)
                    last.then_inc(kv.sem, 1)
                    for j, (a, m) in enumerate(TOK):
                        o = PSf[:, j * P:j * P + m]
                        if j and j < NBLK:
                            pe.wait_ge(chained.sem, chained.at(j))
                        last = pe.matmul(o, v[0:m, j, :], A[0:m, a:a + m], start=True, stop=(j == 0 or j == NBLK))
                        if j == NBLK:
                            pe.wait_ge(g.loaded.sem, g.loaded.at(16))
                            for b in range(NB):
                                last = pe.matmul(PS[:, 2, b * NS:(b + 1) * NS], S0[:, b, :], QB[:, SEQ + b * NS:SEQ + (b + 1) * NS],
                                                 start=False, stop=True, skip_group_check=True)
                        elif j:
                            last = pe.matmul(o, CHAIN[:, j - 1, :], QB[:, a:a + m], start=False, stop=True)
                    last.then_inc(o_ready.sem, 1)
            g.loaded.adds(16)
            for c, n in ((start, 1), (bexp, 1), (dexp, 1), (qkd, 1), (turned, 1), (turned_out, 1), (kv, 2), (chained, NBLK),
                         (o_ready, 1), (vspread, 1), (s_in, 2)):
                c.adds(n)
        run(intra)
        run(inter)
    io_onehot = COL[:, 28:36]
    run(g.load, [(io_onehot, io["onehot"])])
    for h in range(HEADS):
        hgrn(h)
    run(g.tile_norm, [OT[:, h, :] for h in range(4)], [OT[:, h, :] for h in range(4)], g.ONES128[:, :],
        [COL[:, 12 + h:13 + h] for h in range(4)], [OT[:, 4 + i, :] for i in range(4)])

    run(g.project, ws[3][0], HHL, KT, 4, To(OT, 4, func=ACT.Silu, times=INV), then=ws[4])

    def apply_gate():
        with nc.Block() as block:
            @block.vector
            def _(dve):
                for t in range(4):
                    dve.tensor_tensor(OT[:, t, :], OT[:, t, :], OT[:, 4 + t, :], ALU.mult)
    run(apply_gate)

    KD, V = R[:, 8, :], R[:, 9, :]
    VD = view(Rf, T, 9, 2, P)
    KC, VC = view(Rf, T + 2304, NB, WIN), view(Rf, T + 3328, NB, 2, P)
    QZ, QC = view(Rf, T + 5376, 2, 4, P), view(Rf, T + 6400, 2, P)
    BAND, SMASK = view(MASK[:, :], 0, MEM), view(MASK[:, :], MEM, 2, 192)
    SINK, SINKR = COL[:, 40:48], COL[:, 48:50]
    halves = [(slice(0, 64), 0, slice(0, 64)), (slice(64, 128), 1, slice(64, 128))]
    run(g.load, [(g.ROT[:, :], io["swa_rot"]), (COS[:, :], io["swa_cos"]), (SIN[:, :], io["swa_sin"]), (MASK[:, 0:640], io["swa_masks"]),
                 (COL[:, 36:37], io["swa_qnorm_g"]), (COL[:, 37:38], io["swa_knorm_g"]), (SINK, io["swa_sinks"].partition_broadcast(P)),
                 (SINKR, io["swa_sinks_rows"]), (KC, io["cache_swa_kT"].rearrange("b d w -> d b w")),
                 (VC[:, :, 0, 0:64], io["cache_swa_v"][:, :, 0:64].rearrange("b w d -> w b d")),
                 (VC[:, :, 1, 64:128], io["cache_swa_v"][:, :, 64:128].rearrange("b w d -> w b d"))],
        zero=(VC[:, :, 0, 64:128], VC[:, :, 1, 0:64], VD[:, :, 0, 64:128], VD[:, :, 1, 0:64], QZ))
    w_kv, out = g.columns(w_in[:, 2560:2816], KT, 2), g.columns(io["od_w_out"], KT, 8)
    run(g.project, ws[4][0], HHL, KT, 4, To(OT, 4, times=INV), then=w_kv)
    run(g.project, w_kv[0], HHL, KT, 2, To(R, 8, times=INV), then=out)
    run(g.turn_rows, [([V[:, a:a + m] for a, m in toks], [(VD[0:toks[0][1], j:j + len(toks), 0, 0:64], slice(0, 64)), (VD[0:toks[0][1], j:j + len(toks), 1, 64:128], slice(64, 128))])
                      for toks, j in ((TOK[0:4], 0), (TOK[4:8], 4), (TOK[8:9], 8))])
    qk = [OT[:, 4 + i, :] for i in range(4)] + [KD]
    run(g.tile_norm, qk, qk, g.ONES64[:, :], [COL[:, 36:37]] * 4 + [COL[:, 37:38]], [H[:, i, :] for i in range(4)])
    run(g.rotate, qk, H[:, 7, :])

    def spread_queries():
        with nc.Block() as block:
            @block.vector
            def _(dve):
                dve.tensor_scalar(COL[:, 40:50], COL[:, 40:50], -1.0, None, ALU.mult).then_inc(dve_own.sem, 1)
                dve.wait_ge(dve_own.sem, dve_own.next())
                for bt in range(2):
                    for b in range(4):
                        a = SEQ + (bt * 4 + b) * NS
                        src = OT[:, 4:8, a:a + NS]
                        dve.tensor_copy(QC[:, bt, b * 32:(b + 1) * 32].rearrange("p (i t) -> p i t", t=NS), src)
                        dve.tensor_copy(QZ[:, bt, b, b * 32:(b + 1) * 32].rearrange("p (i t) -> p i t", t=NS), src)
    run(spread_queries)

    def prompt_unit(j, s):
        a = j * P
        first = a if j == 0 else a - P
        W = a + P - first
        r = slice(64 * s, 64 * s + 64)

        def scores(pe, ps):
            for i in range(4):
                last = pe.matmul(ps[:, i, 0:W], OT[r, 4 + i, a:a + P], KD[r, first:first + W], start=True, stop=True)
            return last

        def outputs(pe, pt, bank):
            n = W // P
            for kt in range(n):
                last = pe.matmul(PS[:, bank, :], VD[:, first // P + kt, s, :], pt[:, kt, :, :].rearrange("p a b -> p (a b)"),
                                 start=(s == 0 and kt == 0), stop=(s == 1 and kt == n - 1), skip_group_check=True)
            return last

        def place(act, bank):
            return act.activation(OT[:, 4:8, a:a + P], PS[:, bank, :].rearrange("p (i n) -> p i n", n=P), ACT.Copy)
        mask = BAND[:, MEM - W:MEM].unsqueeze(1).to_broadcast([P, 4, W])
        return Unit(P, 4, W, [(x, P) for x in range(0, W, P)], scores, outputs, place, j % 2, s == 0, s == 1, mask, SINK[:, 4 * s:4 * s + 4])

    def sample_unit(bt, s):
        r = slice(64 * s, 64 * s + 64)

        def scores(pe, ps):
            for b in range(4):
                pe.matmul(ps[:, 0, 0:WIN], QZ[r, bt, b, :], KC[r, bt * 4 + b, :], start=(b == 0), stop=(b == 3))
            return pe.matmul(ps[:, 0, WIN:WIN + S], QC[r, bt, :], KD[r, SEQ:T], start=True, stop=True)

        def outputs(pe, pt, bank):
            pe.matmul(PS[:, bank, 0:P], VD[0:S, 8, s, :], pt[0:S, 1, 0, :], start=(s == 0), stop=True, skip_group_check=True)
            for b in range(4):
                last = pe.matmul(PS[:, bank, b * 32:(b + 1) * 32], VC[:, bt * 4 + b, s, :], pt[:, 0, 0, b * 32:(b + 1) * 32],
                                 start=False, stop=True, skip_group_check=True)
            return last

        def place(act, bank):
            a = SEQ + bt * 32
            return act.activation(OT[:, 4:8, a:a + 32].rearrange("p i (b t) -> p i b t", t=NS),
                                  PS[:, bank, 0:P].rearrange("p (b i t) -> p i b t", i=4, t=NS), ACT.Copy)
        return Unit(P, 1, WIN + S, [(0, WIN), (WIN, S)], scores, outputs, place, bt, s == 0, s == 1,
                    SMASK[:, bt, :].unsqueeze(1), SINKR[:, s:s + 1])
    run(_attend, nc, g, [prompt_unit(j, s) for j in range(NBLK) for s in range(2)] + [sample_unit(bt, s) for bt in range(2) for s in range(2)],
        64 ** -0.5, Hf)

    def keep_window():
        with nc.Block() as block:
            @block.sync
            def _(sp):
                g.store(sp, io["swa_kT_prompt"], KD[:, SEQ - WIN:SEQ])
                g.store(sp, io["swa_kT_sample"][:, :, WIN - NS:WIN], KD[:, SEQ:T].rearrange("p (b t) -> p b t", t=NS))
                g.store(sp, io["swa_kT_sample"][:, :, 0:WIN - NS], KC[:, :, NS:WIN])
                for s in range(2):
                    c = slice(64 * s, 64 * s + 64)
                    g.store(sp, io["swa_v_prompt"][:, c], VD[:, NBLK - 1, s, c])
                    g.store(sp, io["swa_v_sample"][0:WIN - NS, :, c], VC[NS:WIN, :, s, c])
                    g.store(sp, io["swa_v_new"][:, c], VD[0:S, 8, s, c])
                sp.wait_ge(g.stored.sem, g.stored.at(g.stores[0]))
    run(keep_window)
    run(g.project, out[0], HHL, KT, 8, To(residual=True), then=g.columns(io["mem_w_kv"][1], KT, 8), lead=Lead([OT[:, t, :] for t in range(KT)], reload=io["yT"]))


def _rope_tables(heads, dim, rot, theta):
    half = rot // 2
    inv = (np.float32(theta) ** (-np.arange(half, dtype=np.float32) / np.float32(half))).astype(np.float32)
    pos = np.concatenate([np.arange(SEQ), np.tile(2048 + np.arange(NS), NB)]).astype(np.float32)
    ang = inv[:, None] * pos[None, :]
    cos, sin, perm = np.ones((P, T), np.float32), np.zeros((P, T), np.float32), np.zeros((P, P), np.float32)
    for h in range(heads):
        for i in range(half):
            a, b = h * dim + i, h * dim + half + i
            cos[a] = cos[b] = np.cos(ang[i])
            sin[a] = sin[b] = np.sin(ang[i])
            perm[b, a], perm[a, b] = -1.0, 1.0
    return cos, sin, perm


def _retention_tables():
    scale = DK_A ** -0.5
    lg = np.log1p(-np.exp2(-5.0 - np.arange(HEADS)))
    out = np.zeros((P, 1320), np.float32)
    n = np.arange(P)
    rel = n[None, :] - n[:, None]
    for h in range(HEADS):
        out[:, h * P:(h + 1) * P] = np.where(rel >= 0, np.exp(rel * lg[h]), 0) * scale
        same = (n[:S, None] // NS) == (n[None, :S] // NS)
        out[:S, 1024 + h * S:1024 + (h + 1) * S] = np.where(same & (rel[:S, :S] >= 0), np.exp(rel[:S, :S] * lg[h]), 0) * scale
        out[:, 1296 + h] = np.exp((P - 1 - n) * lg[h]) * scale
        out[:, 1300 + h] = np.exp((NS - 1 - n % NS) * lg[h]) * scale
    for pr in range(2):
        for hh in range(2):
            r, h = slice(64 * hh, 64 * hh + 64), 2 * pr + hh
            out[r, 512 + pr * P:512 + (pr + 1) * P] = np.exp((n + 1) * lg[h])
            out[r, 1280 + pr * NS:1280 + (pr + 1) * NS] = np.exp((np.arange(NS) + 1) * lg[h])
            out[r, 768 + hh * P:768 + (hh + 1) * P] = 1
            out[r, 1304 + pr], out[r, 1306 + pr] = np.exp(P * lg[h]), np.exp(NS * lg[h])
    out[:, 1308:1316] = _onehot()
    return out


def _onehot():
    return (np.arange(P)[:, None] // NS == np.arange(NB)[None, :]).astype(np.float32)


def _hgrn_masks():
    n = np.arange(P)
    out = [np.eye(P, dtype=np.float32)]
    for lv in range(1, LEVELS + 1):
        w = 2 ** lv
        same = (n[:, None] // w) == (n[None, :] // w)
        out.append((same & (n[:, None] % w < w // 2) & (n[None, :] % w >= w // 2)).astype(np.float32))
    reset = np.ones((P, T), np.float32)
    reset[:, 0:SEQ:P] = 0
    reset[:, SEQ::NS] = 0
    return np.concatenate(out, 1), reset


def _window_masks():
    q, k = np.arange(P)[:, None], np.arange(2 * WIN)[None, :] - WIN
    band = np.where((k <= q) & (q - k < WIN), 0.0, -1e30)
    row = np.arange(P)
    b, t = row // 32, row % NS
    out = [band]
    for bt in range(2):
        key = np.arange(WIN)[None, :] - WIN
        cached = np.where(t[:, None] - key < WIN, 0.0, -1e30)
        s = np.arange(S)[None, :]
        new = np.where((s // NS == bt * 4 + b[:, None]) & (s % NS <= t[:, None]), 0.0, -1e30)
        out += [cached, new]
    return np.concatenate(out, 1).astype(np.float32)


def _columns(v, n):
    return v.reshape(n, P).T


def kernel(**inputs):
    import numpy as _np
    import concourse.bacc as _bacc
    from concourse.bass_utils import run_bass_kernel_spmd as _run

    x = {k: _np.asarray(v) for k, v in inputs.items()}
    cat, c32 = _np.concatenate, _np.ascontiguousarray
    ins = {}
    ins["xT"] = cat([x["x_prompt"][0], x["x_sample"].reshape(S, D)]).T
    ins["ident"] = _np.eye(P, dtype=_np.float32)
    for l in range(2):
        ins[f"gain{l}"] = cat([_columns(x[n][l], KT) for n in ("norm_mix_g", "norm_mem_g", "norm_ffn_g")], 1)
    ins["ret_cos"], ins["ret_sin"], ins["ret_rot"] = _rope_tables(2, 64, 64, 10000.0)
    ins["ret_tables"] = _retention_tables()
    ins["ret_gn_g"] = x["ret_gn_g"][0].T
    ins["ev_w_in"], ins["ev_w_out"] = x["ev_w_in"][0], x["ev_w_out"][0]
    ins["state_ret"] = x["state_ret"][0]
    ins["mlp_wT"] = x["mlp_w_s"][0].transpose(0, 2, 1)
    ins["mlp_wTs"] = _np.tile(x["mlp_w_s"][0].transpose(0, 2, 1)[:, :NS, :NS], (1, NB, NB))
    ins["mlp_b_s"] = x["mlp_b_s"][0]
    ins["mlp_norm_g"] = x["mlp_norm_g"][0].reshape(512)
    n = _np.arange(P)
    ins["tri"] = (n[:, None] <= n[None, :]).astype(_np.float32)
    ins["tri_s"] = ((n[:S, None] <= n[None, :S]) & (n[:S, None] // NS == n[None, :S] // NS)).astype(_np.float32)
    ins["memT"] = x["mem_prompt"][0].T
    for name in ("mem_w_kv", "mem_w_q", "mem_w_o", "ffn_w_gate", "ffn_w_up", "ffn_w_down"):
        ins[name] = x[name]
    ins["mem_knorm_g"], ins["mem_qnorm_g"] = x["mem_knorm_g"][:, :, None], x["mem_qnorm_g"][:, :, None]
    ins["cache_mem_kT"] = x["cache_mem_k"].transpose(0, 1, 3, 4, 2)
    ins["cache_mem_v"] = x["cache_mem_v"].reshape(2, NB, MEM, 512)
    past = x["state_ffn_conv"].reshape(2, NB, 2, FT, P)
    ins["conv_past"] = past.transpose(0, 4, 3, 1, 2).reshape(2, P, FT, NB * 2)
    taps = cat([x["ffn_conv_w"], x["ffn_conv_b"][:, None]], 1).reshape(2, 4, FT, P)
    ins["conv_taps"] = taps.transpose(0, 3, 2, 1)
    order = cat([_np.arange(64) + 64 * h for i in range(4) for h in (i, i + 4)])
    w = x["od_w_in"][0]
    ins["od_w_in"] = cat([w[:, :2048], w[:, 2048:2560][:, order], w[:, 2560:]], 1)
    w = x["od_w_out"][0]
    ins["od_w_out"] = cat([w[:512], w[512:][order]])
    ins["state_hgrn"] = x["state_hgrn"][0]
    ins["hgrn_masks"], ins["hgrn_reset"] = _hgrn_masks()
    ins["hgrn_onorm_g"] = x["hgrn_onorm_g"][0].T
    ins["hgrn_lb_logits"] = cat([_columns(x["hgrn_lb_logits"][l], HEADS) for l in range(2)], 1)
    ins["onehot"] = _onehot()
    ins["swa_cos"], ins["swa_sin"], ins["swa_rot"] = _rope_tables(2, 64, 16, 500000.0)
    ins["swa_masks"] = _window_masks()
    ins["swa_qnorm_g"], ins["swa_knorm_g"] = (_np.tile(x[k][0], 2)[:, None] for k in ("swa_qnorm_g", "swa_knorm_g"))
    ins["swa_sinks"] = x["swa_sinks"][0]
    ins["swa_sinks_rows"] = _np.tile(_np.repeat(x["swa_sinks"][0].reshape(2, 4), NS, 1), (1, 4)).T
    ins["cache_swa_kT"] = x["cache_swa_k"][0].reshape(NB, WIN, P).transpose(0, 2, 1)
    ins["cache_swa_v"] = x["cache_swa_v"][0].reshape(NB, WIN, P)
    outs = {
        "yT": (D, T), "ret_state_prompt": (HEADS, DK_A, P), "hgrn_state_prompt": (HEADS, P, P), "swa_kT_prompt": (P, WIN),
        "swa_v_prompt": (WIN, P), "mem_kT_prompt": (2, HEADS, P, MEM), "mem_v_prompt": (2, MEM, 512), "ffn_conv": (2, P, FT, 18),
        "ret_state_sample": (NB, HEADS, DK_A, P), "chunk_v_sample": (S, 512), "hgrn_state_sample": (NB, HEADS, P, P),
        "swa_kT_sample": (P, NB, WIN), "swa_v_sample": (WIN - NS, NB, P), "swa_v_new": (S, P),
    }
    nc = _bacc.Bacc("TRN2", target_bir_lowering=False, num_devices=1)
    io, arrays = {}, {}
    for name, a in ins.items():
        a = c32(a)
        arrays[f"in_{name}"] = a
        io[name] = nc.dram_tensor(f"in_{name}", a.shape, F32, kind="ExternalInput").ap()
    for name, shape in outs.items():
        io[name] = nc.dram_tensor(f"out_{name}", shape, F32, kind="ExternalOutput").ap()
    build(nc, io)
    r = _run(nc, [arrays], core_ids=[0]).results[0]
    o = {name: r[f"out_{name}"] for name in outs}
    y = o["yT"].T
    conv = o["ffn_conv"].transpose(0, 3, 2, 1).reshape(2, 18, FF)
    swa_v = cat([o["swa_v_sample"].transpose(1, 0, 2), o["swa_v_new"].reshape(NB, NS, P)], 1)
    got = (y[:SEQ][None], y[SEQ:].reshape(NB, NS, D), o["ret_state_prompt"][None, None], o["hgrn_state_prompt"][None, None],
           o["swa_kT_prompt"].T.reshape(1, 1, WIN, 2, 64), o["swa_v_prompt"].reshape(1, 1, WIN, 2, 64),
           o["mem_kT_prompt"].transpose(0, 3, 1, 2)[:, None], o["mem_v_prompt"].reshape(2, 1, MEM, HEADS, P),
           conv[:, 0:2][:, None], o["ret_state_sample"][None], o["chunk_v_sample"].reshape(1, NB, NS, 4, P),
           o["hgrn_state_sample"][None], o["swa_kT_sample"].transpose(1, 2, 0).reshape(1, NB, WIN, 2, 64),
           swa_v.reshape(1, NB, WIN, 2, 64), conv[:, 2:18].reshape(2, NB, 2, FF))
    return tuple(c32(a) for a in got)
```

```python
from contextlib import ExitStack

import numpy as np
import concourse.bass as bass
from concourse import mybir

F32 = mybir.dt.float32
F32R = mybir.dt.float32r
ALU = mybir.AluOpType
ACT = mybir.ActivationFunctionType
AX = mybir.AxisListType

P = 128
D = 1024
KT = D // P
SEQ, NB, NS = 1024, 8, 8
S = NB * NS
T = SEQ + S
NBLK = SEQ // P
HEADS = 4
DK_A = 64
FF = 2816
FT = FF // P
MEM = 256
WIN = 128
EPS = 1e-6
PART = 6
SPANS = ((0, 384), (384, 384), (768, 320))
TOK = [(j * P, P) for j in range(NBLK)] + [(SEQ, S)]
LEVELS = 7
FIRST = 16


class Count:

    def __init__(self, sem):
        self.sem, self.base = sem, 0

    def at(self, n):
        return n + self.base

    def adds(self, n):
        self.base += n


class Chain:

    def __init__(self, sem):
        self.sem, self.n, self.term = sem, 0, None

    def now(self):
        return self.n if self.term is None else self.term + self.n

    def next(self):
        self.n += 1
        return self.now()

    def enter(self, i, per):
        self.term, self.start, self.per = i * per, self.n, per

    def leave(self, rounds):
        assert self.n - self.start == self.per, (self.n - self.start, self.per)
        self.n, self.term = self.start + rounds * self.per, None


class To:

    def __init__(self, buf=None, first=0, func=None, times=None, rows=None, residual=False, norm=None, rotate=None, into=None,
                 squares=False, heads=None, tiles=None):
        self.heads, self.tiles = heads, tiles
        self.buf, self.first, self.func, self.times, self.rows, self.residual = buf, first, func, times, rows, residual
        self.norm, self.rotate, self.into, self.squares = norm, rotate, into, squares


class Meanwhile:

    def __init__(self, vector, scalar):
        self.vector, self.scalar = vector, scalar


class Lead:

    def __init__(self, srcs, gain=None, inv=None, spill=False, reload=None, arriving=None, summed=False):
        self.summed = summed
        self.srcs, self.gain, self.inv, self.spill, self.reload, self.arriving = srcs, gain, inv, spill, reload, arriving


class Shared:
    pass


def build(nc, io):
    with ExitStack() as ctx:
        _build(nc, io, ctx)


def _build(nc, io, ctx):
    def sb(name, shape):
        return ctx.enter_context(nc.sbuf_tensor(name, shape, F32))

    def sem(name):
        return ctx.enter_context(nc.semaphore(name))

    counts = {}

    def count(name):
        if name not in counts:
            counts[name] = Count(sem(name))
        return counts[name]

    base = (nc.sbuf_base + 31) // 32 * 32
    slab = [0]

    def place(name, floats, dtype=F32, at=None):
        if at is None:
            at = slab[0]
            slab[0] += (floats + 7) // 8 * 8
        return nc.alloc_sbuf_tensor_at(name, [P, floats], dtype, offset=base + 4 * at)[:, :], at

    def tiled(v):
        return v.rearrange("p (a b) -> p a b", b=T)
    X, _ = place("residual", KT * T)
    Hf, at = place("work_h", 2 * KT * T)
    HHf, _ = place("moving_hi", KT * T, F32R, at)
    HLf, _ = place("moving_lo", KT * T, F32R, at + KT * T)
    Rf, at = place("work_r", 13 * T)
    HIDH, _ = place("hidden_hi", PART * T, F32R, at)
    HIDL, _ = place("hidden_lo", PART * T, F32R, at + PART * T)
    Wf, at = place("work_w", 6 * D)
    WRAW = [place(f"w_raw{s}", D, F32, at + s * D)[0] for s in range(2)]
    WHI = [place(f"w_hi{s}", D, F32R, at + (2 + s) * D)[0] for s in range(2)]
    WLO = [place(f"w_lo{s}", D, F32R, at + (4 + s) * D)[0] for s in range(2)]
    CST, _ = place("constants", 4 * T + 1408)
    COS, SIN, SPARE, MASK = CST[:, 0:T], CST[:, T:2 * T], tiled(CST[:, 2 * T:4 * T]), CST[:, 4 * T:4 * T + 1408]
    IDENT, ROT, ONES, ONES128, ONES64 = (place(n, P)[0] for n in ("ident", "rot", "ones1024", "ones128", "ones64"))
    GAIN, _ = place("gains", 3 * KT)
    COL, _ = place("columns", 64)
    SM, _ = place("small", 80)
    EPSC, _ = place("eps", 1)
    ONE, _ = place("one", 1)
    CENTER, _ = place("center", P)
    ctx.enter_context(nc.sbuf_tensor("slab", [P, slab[0]], F32))
    X, H, R = tiled(X), tiled(Hf), tiled(Rf)
    HH, HL, HIDH, HIDL = tiled(HHf), tiled(HLf), tiled(HIDH), tiled(HIDL)
    OT = X
    PS = ctx.enter_context(nc.psum_tensor("psum", [P, 8, 512], F32))
    OTf = X[:, :, :].rearrange("p a b -> p (a b)")
    PSf = PS[:, :, :].rearrange("p a b -> p (a b)")

    def view(flat, at, *dims):
        n = 1
        for d in dims:
            n *= d
        v = flat[:, at:at + n]
        if len(dims) == 2:
            v = v.rearrange("p (a b) -> p a b", b=dims[1])
        if len(dims) == 3:
            v = v.rearrange("p (a b c) -> p a b c", b=dims[1], c=dims[2])
        return v

    dve_own, pool_own = Chain(sem("dve_own")), Chain(sem("pool_own"))
    w_loaded = [count(f"w_loaded{s}") for s in range(2)]
    w_split = count("w_split")
    prefetched = [0]
    ahead = [False]
    tile_full, tile_free = count("tile_full"), count("tile_free")
    loaded, stored, reloaded = count("loaded"), count("stored"), count("reloaded")
    stores = [0]

    def store(eng, dst, src):
        eng.dma_start(dst, src).then_inc(stored.sem, 16)
        stores[0] += 16

    def load(pairs, zero=()):
        cleared = count("cleared")
        with nc.Block() as block:
            @block.gpsimd
            def _(pool):
                for z in zero:
                    nc.gpsimd.memset(z, 0.0).then_inc(cleared.sem, 1)

            @block.sync
            def _(sp):
                if zero:
                    sp.wait_ge(cleared.sem, cleared.at(len(zero)))
                for dst, src in pairs:
                    sp.dma_start(dst, src).then_inc(loaded.sem, 16)
                sp.wait_ge(loaded.sem, loaded.at(16 * len(pairs)))
        loaded.adds(16 * len(pairs))
        cleared.adds(len(zero))

    def slot(buf, kt):
        return buf[:, 0:kt * P].rearrange("p (k n) -> p k n", n=P)

    def chunk(w, kt, c):
        return w.rearrange("(k p) n -> p k n", p=P)[:, :, bass.ds(c * P, P)]

    def rounds(eng, chunks, body, start=0, chain=None, per=0):
        pairs = chunks // 2
        if pairs - start > 1:
            with eng.Fori(start, pairs) as i:
                if chain:
                    chain.enter(i - start, 2 * per)
                for s in range(2):
                    body(i * 2 + s, s, i)
            if chain:
                chain.leave(pairs - start)
        elif pairs - start == 1:
            for s in range(2):
                body(start * 2 + s, s, start)
        if chunks % 2 and chunks > 2 * start:
            body(chunks - 1, 0, pairs)

    def last_user(slot_, chunks):
        return chunks - 1 - (chunks - 1 - slot_) % 2

    def load_weights(sp, pick, chunks, then, o=0, all_split=False):
        def body(c, s, i):
            sp.wait_ge(w_split.sem, w_split.at(c + (o - 1)))
            src, kt = pick(c, s, i)
            sp.dma_start(slot(WRAW[s], kt), src).then_inc(w_loaded[s].sem, 16)
        rounds(sp, chunks, body, start=1 if prefetched[0] else 0)
        prefetched[0] = 0
        if then:
            pick2, n2 = then
            for c in range(min(2, n2)):
                sp.wait_ge(w_split.sem, w_split.at(o + (chunks if all_split else last_user(c, chunks) + 1)))
                src, kt = pick2(c, c, 0)
                sp.dma_start(slot(WRAW[c], kt), src).then_inc(w_loaded[c].sem, 16)
            prefetched[0] = min(2, n2)

    def halve(eng, s, kt):
        raw, hi, lo = (b[s][:, 0:kt * P] for b in (WRAW, WHI, WLO))
        if eng is nc.gpsimd:
            own = pool_own
            nc.gpsimd.tensor_tensor(hi, raw, ONE.to_broadcast([P, kt * P]), ALU.mult).then_inc(own.sem, 1)
        else:
            own = dve_own
            nc.vector.tensor_copy(hi, raw).then_inc(own.sem, 1)
        eng.wait_ge(own.sem, own.next())
        eng.tensor_tensor(lo, raw, hi.bitcast(F32), ALU.subtract).then_inc(w_split.sem, 1)

    def split_weights(eng, kt, chunks, skip, o=0):
        def body(c, s, i):
            eng.wait_ge(w_loaded[s].sem, w_loaded[s].at(i * 16 + (8 * o + 16)))
            eng.wait_ge(tile_full.sem, tile_full.at(c + (o - 1)))
            halve(eng, s, kt)
        if skip and chunks > 1:
            body(1, 1, 0)
        rounds(eng, chunks, body, start=1 if skip else 0, chain=pool_own if eng is nc.gpsimd else dve_own, per=1)

    def split_ahead(pool, chunks, then, o=0):
        if then:
            pool.wait_ge(w_loaded[0].sem, w_loaded[0].at(8 * o + 16 * ((chunks + 1) // 2) + 16))
            pool.wait_ge(tile_full.sem, tile_full.at(o + last_user(0, chunks) + 1))
            halve(nc.gpsimd, 0, then[0](0, 0, 0)[1])

    def counted(chunks):
        w_split.adds(chunks)
        tile_full.adds(chunks)
        tile_free.adds(chunks)
        w_loaded[0].adds(16 * ((chunks + 1) // 2))
        w_loaded[1].adds(16 * (chunks // 2))

    def columns(w, kt, n=None):
        return (lambda c, s, i: (chunk(w, kt, c), kt)), n

    def pass_of(pe, out, stationary, moving, k, kt):
        (sh, sl), (mh, ml) = stationary, moving
        pe.matmul(out, sh, mh, start=(k == 0), stop=False)
        pe.matmul(out, sh, ml, start=False, stop=False)
        return pe.matmul(out, sl, mh, start=False, stop=(k == kt - 1))

    squared, square_used, summed, rooted = count("squared"), count("square_used"), count("summed"), count("rooted")
    hi_made, lo_made = count("hi_made"), count("lo_made")
    arrived = [count(f"x_arrived{q}") for q in range(KT // 2)]
    SQ, ACC = [R[:, 9, :], R[:, 10, :]], R[:, 11, :]

    def lead_scalar(act, lead):
        for t, x in enumerate(lead.srcs):
            if lead.arriving and t % 2 == 0:
                act.wait_ge(arrived[t // 2].sem, 16)
            act.activation(HH[:, t, :], x, ACT.Copy, scale=1.0 if lead.gain is None else GAIN[:, lead.gain + t:lead.gain + t + 1]).then_inc(hi_made.sem, 1)
            if lead.summed and t == 1:
                roots(act, lead, 5)
        if lead.inv is not None and not lead.summed:
            for k, x in enumerate(lead.srcs):
                if k >= 2:
                    act.wait_ge(square_used.sem, square_used.at(k - 1))
                act.activation(SQ[k % 2], x, ACT.Square).then_inc(squared.sem, 1)
            roots(act, lead, 2)

    def roots(act, lead, bank):
        act.wait_ge(summed.sem, summed.at(1))
        act.activation(lead.inv[:, 0:1024].rearrange("p (a b) -> p a b", b=512), PS[:, 6:8, :], ACT.Sqrt, bias=EPSC[:, 0:1])
        act.activation(lead.inv[:, 1024:T], PS[:, bank, 448:512], ACT.Sqrt, bias=EPSC[:, 0:1]).then_inc(rooted.sem, 1)

    def sum_squares(pe, bank):
        for out, (b, w) in ((PS[:, 6, :], (0, 512)), (PS[:, 7, :], (512, 512)), (PS[:, bank, 448:512], (1024, 64))):
            last = pe.matmul(out, ONES[:, :], ACC[:, b:b + w], start=True, stop=True)
        last.then_inc(summed.sem, 1)

    def onto_residual(dve, c, s, o, squares):
        dve.wait_ge(tile_full.sem, tile_full.at(c + (o + 1)))
        for ps, a, m, rows in pieces(3 * s):
            x = cut(X, c, a, m, rows)
            last = dve.tensor_tensor(x, ps, x, ALU.add)
        last.then_inc(tile_free.sem, 1)
        if squares:
            dve.wait_ge(squared.sem, squared.at(c + 1))
            dve.tensor_tensor(ACC, ACC, SQ[1], ALU.add).then_inc(square_used.sem, 1)
            dve.wait_ge(square_used.sem, square_used.at(c + 1))

    def square_residual(act, c, o):
        act.wait_ge(tile_free.sem, tile_free.at(c + (o + 1)))
        act.activation(SQ[1], X[:, bass.ds(c, 1), :].rearrange("p a b -> p (a b)"), ACT.Square).then_inc(squared.sem, 1)

    def lead_vector(dve, lead):
        for t, x in enumerate(lead.srcs):
            dve.wait_ge(hi_made.sem, hi_made.at(t + 1))
            if lead.gain is None:
                last = dve.tensor_tensor(HL[:, t, :], x, HH[:, t, :].bitcast(F32), ALU.subtract)
            else:
                last = dve.scalar_tensor_tensor(HL[:, t, :], x, GAIN[:, lead.gain + t:lead.gain + t + 1], HH[:, t, :].bitcast(F32), ALU.mult, ALU.subtract)
            last.then_inc(lo_made.sem, 1)
        if lead.inv is not None:
            if not lead.summed:
                dve.wait_ge(squared.sem, squared.at(2))
                dve.tensor_tensor(ACC, SQ[0], SQ[1], ALU.add).then_inc(square_used.sem, 2)
                for k in range(2, KT):
                    dve.wait_ge(square_used.sem, square_used.at(k))
                    dve.wait_ge(squared.sem, squared.at(k + 1))
                    dve.tensor_tensor(ACC, ACC, SQ[k % 2], ALU.add).then_inc(square_used.sem, 1)
            dve.wait_ge(rooted.sem, rooted.at(1))
            dve.reciprocal(lead.inv, lead.inv).then_inc(dve_own.sem, 1)
            dve.wait_ge(dve_own.sem, dve_own.next())
        if lead.spill:
            dve.wait_ge(stored.sem, stores[0])
        if lead.reload is not None:
            dve.wait_ge(reloaded.sem, reloaded.at(16 * KT))

    def lead_counted(lead):
        hi_made.adds(len(lead.srcs))
        lo_made.adds(len(lead.srcs))
        if lead.reload is not None:
            reloaded.adds(16 * KT)
        if lead.inv is not None:
            for c, n in ((squared, 0 if lead.summed else KT), (square_used, 0 if lead.summed else KT), (summed, 1), (rooted, 1)):
                c.adds(n)

    def moved_in(block, pick, kt, chunks, then, lead, split_on="gpsimd", loads=(), after_split=None):
        skip, ahead[0] = ahead[0], bool(then)

        @block.sync
        def _(sp):
            if lead and lead.spill:
                store(sp, io["yT"].rearrange("(k p) t -> p k t", p=P), X[:, :, :])
            if lead and lead.reload is not None:
                for t in range(KT):
                    sp.wait_ge(lo_made.sem, lo_made.at(t + 1))
                    sp.dma_start(X[:, t, :], lead.reload[t * P:(t + 1) * P, :]).then_inc(reloaded.sem, 16)
            if lead and lead.arriving:
                for q in range(KT // 2):
                    sp.dma_start(X[:, 2 * q:2 * q + 2, :], io["xT"][2 * q * P:(2 * q + 2) * P, :].rearrange("(k p) t -> p k t", p=P)).then_inc(arrived[q].sem, 16)
            load_weights(sp, pick, chunks, then, all_split=split_on == "vector")
            for dst, src in loads:
                sp.dma_start(dst, src).then_inc(loaded.sem, 16)
            if loads:
                sp.wait_ge(loaded.sem, loaded.at(16 * len(loads)))

        @block.gpsimd
        def _(pool):
            if split_on == "gpsimd":
                split_weights(nc.gpsimd, kt, chunks, skip)
            split_ahead(pool, chunks, then)
            if after_split:
                after_split(pool)
        return skip

    def products(pe, src, kt, chunks, spans, paced=None, norm=False, turn=None, o=0, summed_before=False):
        def ready(c):
            pe.wait_ge(w_split.sem, w_split.at(c + (o + 1)))
            pe.wait_ge(tile_free.sem, tile_free.at(c + (o - 1)))

        def body(c, s, i, norm=False):
            hi, lo = slot(WHI[s], kt), slot(WLO[s], kt)
            ready(c)
            for n, (a, m) in enumerate(spans):
                if norm and n == 2:
                    pe.wait_ge(square_used.sem, square_used.at(KT))
                    sum_squares(pe, 2)
                for k in range(kt):
                    last = pass_of(pe, PS[:, 3 * s + n, 0:m], (hi[:, k, :], lo[:, k, :]), (src[0][:, k, a:a + m], src[1][:, k, a:a + m]), k, kt)
            last.then_inc(tile_full.sem, 1)
        if paced:
            hi, lo = slot(WHI[0], kt), slot(WLO[0], kt)
            if summed_before:
                sum_squares(pe, 5)
            ready(0)
            for k in range(kt):
                paced(k)
                for n, (a, m) in enumerate(spans):
                    last = pass_of(pe, PS[:, n, 0:m], (hi[:, k, :], lo[:, k, :]), (src[0][:, k, a:a + m], src[1][:, k, a:a + m]), k, kt)
            last.then_inc(tile_full.sem, 1)
            if summed_before:
                pe.wait_ge(rooted.sem, rooted.at(1))
            body(1, 1, 0, norm=norm)
            if turn:
                turn(0)
        if turn:
            for c in range(2 if paced else 0, chunks):
                body(c, c % 2, c // 2)
                if c:
                    turn(c - 1)
            turn(chunks - 1)
        else:
            rounds(pe, chunks, body, start=1 if paced else 0)

    def project(pick, src, kt, chunks, to, spans=SPANS, then=None, lead=None, split_on="gpsimd",
                loads=(), meanwhile=None, zero=()):
        turned, taken, activated, normed = count("tile_turned"), count("turned_taken"), count("activated"), count("head_normed")
        head_squared = count("head_squared")
        groups = [(TOK[j:j + 4], j) for j in range(0, 9, 4)]
        in_place = to.times is not None and to.func is not None
        again = chunks if to.rows is not None or to.rotate else to.norm[2] if to.norm else 0
        ranges = [(0, 512), (512, 512), (1024, 64)]

        def tile(c):
            return c % 2 if to.rows is not None else c + to.first

        def whole(c):
            return to.tiles[c] if to.tiles else to.buf[:, tile(c), :]
        def after_split(pool):
            for z in zero:
                nc.gpsimd.memset(z, 0.0)
            for c in range(chunks if to.into else 0):
                pool.wait_ge(activated.sem, activated.at(c + 1))
                if to.heads:
                    pool.wait_ge(normed.sem, normed.at(c + 1))
                nc.gpsimd.tensor_tensor(to.into[c], to.into[c], whole(c), ALU.mult)
        with nc.Block() as block:
            skip = moved_in(block, pick, kt, chunks, then, lead, split_on, loads, after_split)

            @block.tensor
            def _(pe):
                def turn(c):
                    if c >= again:
                        return
                    if to.norm:
                        pe.wait_ge(head_squared.sem, head_squared.at(c + 1))
                    elif in_place:
                        pe.wait_ge(activated.sem, activated.at(c + 1))
                    else:
                        pe.wait_ge(tile_free.sem, tile_free.at(c + 1))
                    for q, (toks, j) in enumerate(groups):
                        n = 3 * c + q
                        b, w = ranges[q]
                        if n >= 2:
                            pe.wait_ge(taken.sem, taken.at(n - 1))
                        if to.norm:
                            last = pe.matmul(PS[:, 6 + n % 2, 0:w], to.norm[0], to.norm[3][:, b:b + w], start=True, stop=True)
                        elif to.rotate:
                            last = pe.matmul(PS[:, 6 + n % 2, 0:w], to.rotate[0], whole(c)[:, b:b + w], start=True, stop=True)
                        else:
                            for x, (a, m) in enumerate(toks):
                                last = pe.transpose(PS[0:m, 6 + n % 2, x * P:(x + 1) * P], to.buf[:, tile(c), a:a + m], IDENT[:, :])
                        last.then_inc(turned.sem, 1)
                def paced(k):
                    pe.wait_ge(lo_made.sem, lo_made.at(k + 1))
                normed_lead = lead is not None and lead.inv is not None
                products(pe, src, kt, chunks, spans, paced if lead else None, normed_lead and not lead.summed, turn if again else None,
                         summed_before=normed_lead and lead.summed)

            if split_on == "vector":
                @block.vector
                def _(dve):
                    split_weights(nc.vector, kt, chunks, skip)

            elif lead or to.times is not None or to.residual:
                @block.vector
                def _(dve):
                    def body(c, s, i):
                        if to.residual:
                            return onto_residual(dve, c, s, 0, to.squares)
                        dve.wait_ge(tile_full.sem, tile_full.at(c + 1))
                        if to.rows is not None and c >= 2:
                            dve.wait_ge(turned.sem, turned.at(3 * c - 3))
                        for ps, a, m, rows in pieces(3 * s, spans):
                            last = dve.tensor_tensor(shaped(whole(c), a, m, rows) if to.tiles else cut(to.buf, tile(c), a, m, rows), ps, shaped(to.times, a, m, rows), ALU.mult)
                        last.then_inc(tile_free.sem, 1)
                    if lead:
                        lead_vector(dve, lead)
                    if to.squares:
                        if lead:
                            dve.wait_ge(lo_made.sem, lo_made.at(len(lead.srcs)))
                        dve.memset(ACC, 0.0).then_inc(dve_own.sem, 1)
                        dve.wait_ge(dve_own.sem, dve_own.next())
                    def norm(c):
                        if not to.norm or c >= again:
                            return
                        root = to.norm[4]
                        dve.wait_ge(taken.sem, taken.at(3 * c + 3))
                        dve.reciprocal(root, root).then_inc(dve_own.sem, 1)
                        dve.wait_ge(dve_own.sem, dve_own.next())
                        x, gain = to.heads[c] if to.heads else whole(c), to.norm[1][c]
                        dve.scalar_tensor_tensor(x, x, gain, root, ALU.mult, ALU.mult).then_inc(normed.sem, 1)

                    def rotate_tile(c):
                        if not to.rotate:
                            return
                        _, cos, sin, partner = to.rotate
                        for q, (b, w) in enumerate(ranges):
                            n = 3 * c + q
                            dve.wait_ge(turned.sem, turned.at(n + 1))
                            dve.tensor_tensor(partner[:, b:b + w], PS[:, 6 + n % 2, 0:w], sin[:, b:b + w], ALU.mult).then_inc(taken.sem, 1)
                        dve.tensor_tensor(whole(c), whole(c), cos, ALU.mult).then_inc(dve_own.sem, 1)
                        dve.wait_ge(taken.sem, taken.at(3 * c + 3))
                        dve.wait_ge(dve_own.sem, dve_own.next())
                        dve.tensor_tensor(whole(c), whole(c), partner, ALU.add).then_inc(dve_own.sem, 1)
                        dve.wait_ge(dve_own.sem, dve_own.next())
                    if again or meanwhile:
                        for c in range(chunks):
                            body(c, c % 2, c // 2)
                            if c:
                                norm(c - 1)
                                rotate_tile(c - 1)
                            if meanwhile and c < len(meanwhile.vector):
                                meanwhile.vector[c](dve)
                        norm(chunks - 1)
                        rotate_tile(chunks - 1)
                    elif to.times is not None or to.residual:
                        rounds(dve, chunks, body)

            @block.scalar
            def _(act):
                def body(c, s, i):
                    if to.times is None:
                        act.wait_ge(tile_full.sem, tile_full.at(c + 1))
                        for ps, a, m, rows in pieces(3 * s, spans):
                            last = act.activation(cut(to.buf, tile(c), a, m, rows), ps, to.func or ACT.Copy)
                        last.then_inc(tile_free.sem, 1)
                    elif to.func:
                        act.wait_ge(tile_free.sem, tile_free.at(c + 1))
                        x = to.buf[:, bass.ds(tile(c), 1), :].rearrange("p a b -> p (a b)")
                        last = act.activation(x, x, to.func)
                        if to.rows is not None or to.into:
                            last.then_inc(activated.sem, 1)

                def take(c):
                    if c >= again:
                        return
                    for q, (toks, j) in enumerate(groups):
                        n = 3 * c + q
                        b, w = ranges[q]
                        if to.norm and q == 0 and c:
                            act.wait_ge(normed.sem, normed.at(c))
                        act.wait_ge(turned.sem, turned.at(n + 1))
                        if to.norm:
                            act.activation(to.norm[4][:, b:b + w], PS[:, 6 + n % 2, 0:w], ACT.Sqrt, bias=EPSC[:, 0:1]).then_inc(taken.sem, 1)
                        else:
                            m = toks[0][1]
                            ps = PS[0:m, 6 + n % 2, 0:len(toks) * P].rearrange("p (j n) -> p j n", n=P)
                            act.activation(to.rows[0:m, j:j + len(toks), c * P:(c + 1) * P], ps, ACT.Copy).then_inc(taken.sem, 1)

                def square(c):
                    if c >= again:
                        return
                    if not to.heads:
                        act.wait_ge(tile_free.sem, tile_free.at(c + 1))
                    if c:
                        act.wait_ge(turned.sem, turned.at(3 * c))
                    act.activation(to.norm[3], to.heads[c] if to.heads else whole(c), ACT.Square).then_inc(head_squared.sem, 1)
                if lead:
                    lead_scalar(act, lead)
                if meanwhile:
                    meanwhile.scalar(act)
                if to.rows is not None or to.norm:
                    for c in range(chunks):
                        if c:
                            take(c - 1)
                        if in_place:
                            body(c, c % 2, c // 2)
                        if to.norm:
                            square(c)
                    take(chunks - 1)
                elif to.squares:
                    rounds(act, chunks, lambda c, s, i: square_residual(act, c, 0))
                elif not to.residual and (to.times is None or to.func):
                    rounds(act, chunks, body)
        counted(chunks)
        loaded.adds(16 * len(loads))
        if to.squares:
            squared.adds(KT)
            square_used.adds(KT)
        if lead:
            lead_counted(lead)
        turned.adds(3 * again)
        taken.adds(3 * again)
        if in_place and (to.into or to.rows is not None):
            activated.adds(chunks)
        if to.norm:
            normed.adds(again)
            head_squared.adds(again)

    def turn_rows(pairs):
        turned = count("turned_rows")
        with nc.Block() as block:
            @block.tensor
            def _(pe):
                for b, (srcs, dsts) in enumerate(pairs):
                    for x, v in enumerate(srcs):
                        m = v.shape[1]
                        last = pe.transpose(PS[0:m, b, x * P:(x + 1) * P], v, IDENT[:, :])
                    last.then_inc(turned.sem, 1)

            @block.scalar
            def _(act):
                for b, (srcs, dsts) in enumerate(pairs):
                    act.wait_ge(turned.sem, turned.at(b + 1))
                    m = srcs[0].shape[1]
                    ps = PS[0:m, b, 0:len(srcs) * P].rearrange("p (j n) -> p j n", n=P)
                    for dst, c in dsts:
                        act.activation(dst, ps[:, :, c], ACT.Copy)
        turned.adds(len(pairs))

    def pieces(bank, spans=SPANS):
        if len(spans) == 1:
            return [(PS[:, bank, 0:spans[0][1]], 0, spans[0][1], 1)]
        return [(PS[:, bank:bank + 2, 0:384], 0, 768, 2), (PS[:, bank + 2, 0:320], 768, 320, 1)]

    def cut(buf, tile, a, m, rows):
        v = buf[:, bass.ds(tile, 1), a:a + m].rearrange("p a b -> p (a b)")
        return v.rearrange("p (r b) -> p r b", r=rows) if rows > 1 else v

    def shaped(v, a, m, rows):
        v = v[:, a:a + m]
        return v.rearrange("p (r b) -> p r b", r=rows) if rows > 1 else v

    def tile_norm(srcs, dsts, ones, gains, scratch, width=T, center=False, times=None, loads=(), beside=None):
        spans = SPANS if width == T else ((0, width),)
        squared, summed, rooted = count("tile_squared"), count("tile_summed"), count("tile_rooted")
        meaned, centered, scaled, turned = count("tile_meaned"), count("tile_centered"), count("tile_scaled"), count("tile_center_made")
        n_t, n_p = len(srcs), len(pieces(0, spans))

        def sums(t):
            return 3 if center else 3 * (t % 2)
        with nc.Block() as block:
            @block.tensor
            def _(pe):
                def take_mean(t):
                    if t >= 1:
                        pe.wait_ge(centered.sem, centered.at(t))
                    for n, (a, m) in enumerate(spans):
                        last = pe.matmul(PS[:, n, 0:m], CENTER, srcs[t][:, a:a + m], start=True, stop=True)
                    last.then_inc(meaned.sem, 1)
                if center:
                    pe.wait_ge(turned.sem, turned.at(1))
                    take_mean(0)
                for t in range(n_t):
                    if center and t + 1 < n_t:
                        take_mean(t + 1)
                    pe.wait_ge(squared.sem, squared.at(t + 1))
                    if center and t >= 1:
                        pe.wait_ge(rooted.sem, rooted.at(n_p * t))
                    elif t >= 2:
                        pe.wait_ge(rooted.sem, rooted.at(n_p * (t - 1)))
                    for n, (a, m) in enumerate(spans):
                        last = pe.matmul(PS[:, sums(t) + n, 0:m], ones, scratch[t % 2][:, a:a + m], start=True, stop=True)
                    last.then_inc(summed.sem, 1)
                    if beside:
                        beside[0](pe, t)

            @block.scalar
            def _(act):
                def square(t):
                    if center:
                        act.wait_ge(meaned.sem, meaned.at(t + 1))
                        for ps, a, m, rows in pieces(0, spans):
                            last = act.activation(shaped(srcs[t], a, m, rows), ps, ACT.Copy)
                        last.then_inc(centered.sem, 1)
                        act.wait_ge(centered.sem, centered.at(t + 1))
                    if t >= 2:
                        act.wait_ge(summed.sem, summed.at(t - 1))
                    act.activation(scratch[t % 2], srcs[t], ACT.Square).then_inc(squared.sem, 1)
                square(0)
                for t in range(n_t):
                    if t + 1 < n_t:
                        square(t + 1)
                    act.wait_ge(summed.sem, summed.at(t + 1))
                    if t >= 2:
                        act.wait_ge(scaled.sem, scaled.at(t - 1))
                    for ps, a, m, rows in pieces(sums(t), spans):
                        act.activation(shaped(scratch[2 + t % 2], a, m, rows), ps, ACT.Sqrt, bias=EPSC[:, 0:1]).then_inc(rooted.sem, 1)

            @block.vector
            def _(dve):
                if center:
                    dve.tensor_tensor(CENTER, IDENT, ones, ALU.subtract).then_inc(turned.sem, 1)
                for t in range(n_t):
                    dve.wait_ge(rooted.sem, rooted.at(n_p * (t + 1)))
                    inv = scratch[2 + t % 2]
                    dve.reciprocal(inv, inv).then_inc(dve_own.sem, 1)
                    dve.wait_ge(dve_own.sem, dve_own.next())
                    dve.scalar_tensor_tensor(srcs[t] if times else dsts[t], srcs[t], gains[t], inv, ALU.mult, ALU.mult).then_inc(scaled.sem, 1)
                    if beside:
                        beside[1](dve, t)

            if times:
                @block.gpsimd
                def _(pool):
                    for t in range(n_t):
                        pool.wait_ge(scaled.sem, scaled.at(t + 1))
                        nc.gpsimd.tensor_tensor(dsts[t], srcs[t], times[t], ALU.mult)
                        if beside:
                            beside[2](pool, t)

            if loads:
                @block.sync
                def _(sp):
                    for dst, src in loads:
                        sp.dma_start(dst, src).then_inc(loaded.sem, 16)
                    sp.wait_ge(loaded.sem, loaded.at(16 * len(loads)))
                    if beside:
                        beside[3](sp)
        for c, n in ((squared, n_t), (summed, n_t), (rooted, n_t * n_p), (scaled, n_t)):
            c.adds(n)
        loaded.adds(16 * len(loads))
        if center:
            meaned.adds(n_t)
            centered.adds(n_t)
            turned.adds(1)

    def rotate(tiles, scratch):
        rotated, taken, cosined, added = count("rotated"), count("rotated_taken"), count("rotated_cos"), count("rotated_added")
        with nc.Block() as block:
            @block.tensor
            def _(pe):
                for t, x in enumerate(tiles):
                    if t >= 2:
                        pe.wait_ge(taken.sem, taken.at(t - 1))
                    for n, (a, m) in enumerate(SPANS):
                        last = pe.matmul(PS[:, 3 * (t % 2) + n, 0:m], ROT[:, :], x[:, a:a + m], start=True, stop=True)
                    last.then_inc(rotated.sem, 1)

            @block.gpsimd
            def _(pool):
                for t, x in enumerate(tiles):
                    pool.wait_ge(rotated.sem, rotated.at(t + 1))
                    nc.gpsimd.tensor_tensor(x, x, COS[:, :], ALU.mult).then_inc(cosined.sem, 1)

            @block.vector
            def _(dve):
                for t, x in enumerate(tiles):
                    dve.wait_ge(rotated.sem, rotated.at(t + 1))
                    if t >= 2:
                        dve.wait_ge(added.sem, added.at(t - 1))
                    for ps, a, m, rows in pieces(3 * (t % 2)):
                        last = dve.tensor_tensor(shaped(scratch[t % 2], a, m, rows), ps, shaped(SIN, a, m, rows), ALU.mult)
                    last.then_inc(taken.sem, 1)
                    dve.wait_ge(cosined.sem, cosined.at(t + 1))
                    dve.wait_ge(taken.sem, taken.at(t + 1))
                    dve.tensor_tensor(x, x, scratch[t % 2], ALU.add).then_inc(added.sem, 1)
        for c in (rotated, taken, cosined, added):
            c.adds(len(tiles))

    with nc.Block() as block:
        consts = [(IDENT[:, :], io["ident"]), (GAIN[:, :], io["gain0"])]

        @block.sync
        def _(sp):
            for dst, src in consts:
                sp.dma_start(dst, src).then_inc(loaded.sem, 16)
            for c in range(2):
                sp.dma_start(slot(WRAW[c], KT), chunk(io["ev_w_in"][:, 512:1024], KT, c)).then_inc(w_loaded[c].sem, 16)
            prefetched[0] = 2
            sp.wait_ge(loaded.sem, loaded.at(16 * len(consts)))

        @block.gpsimd
        def _(pool):
            for v, x in ((ONES, 1.0 / D), (ONES128, 1.0 / P), (EPSC, EPS), (ONES64, 0.0), (ONE, 1.0)):
                nc.gpsimd.memset(v, x).then_inc(pool_own.sem, 1)
            pool_own.n = 8
            pool.wait_ge(pool_own.sem, 5)
            nc.gpsimd.memset(view(Rf, 4 * T + 4608, 9, 512)[64:128, 8, :], 0.0).then_inc(pool_own.sem, 1)
            nc.gpsimd.memset(ONES64[0:64, 0:64], 1.0 / 64).then_inc(pool_own.sem, 1)
            nc.gpsimd.memset(ONES64[64:128, 64:128], 1.0 / 64).then_inc(pool_own.sem, 1)
            pool.wait_ge(pool_own.sem, 8)
            pool.sem_inc(tile_full.sem, FIRST)
            pool.sem_inc(tile_free.sem, FIRST)
            pool.sem_inc(w_split.sem, FIRST)
        tile_full.adds(FIRST)
        tile_free.adds(FIRST)
        w_split.adds(FIRST)
    loaded.adds(16 * 2)

    env = Shared()
    env.COL = COL
    env.COS = COS
    env.CST = CST
    env.EPSC = EPSC
    env.GAIN = GAIN
    env.H = H
    env.HH = HH
    env.HHf = HHf
    env.HIDH = HIDH
    env.HIDL = HIDL
    env.HL = HL
    env.HLf = HLf
    env.Hf = Hf
    env.IDENT = IDENT
    env.MASK = MASK
    env.ONES128 = ONES128
    env.ONES64 = ONES64
    env.OT = OT
    env.ONE = ONE
    env.OTf = OTf
    env.PS = PS
    env.PSf = PSf
    env.R = R
    env.ROT = ROT
    env.Rf = Rf
    env.SIN = SIN
    env.SM = SM
    env.SPARE = SPARE
    env.WHI = WHI
    env.WLO = WLO
    env.WRAW = WRAW
    env.Wf = Wf
    env.X = X
    env.chunk = chunk
    env.count = count
    env.cut = cut
    env.dve_own = dve_own
    env.load = load
    env.loaded = loaded
    env.pieces = pieces
    env.pool_own = pool_own
    env.project = project
    env.rotate = rotate
    env.slot = slot
    env.store = store
    env.stored = stored
    env.stores = stores
    env.tile_norm = tile_norm
    env.view = view
    env.ahead = ahead
    env.load_weights = load_weights
    env.split_weights = split_weights
    env.split_ahead = split_ahead
    env.lo_made = lo_made
    env.rounds = rounds
    env.columns = columns
    env.products = products
    env.lead_scalar = lead_scalar
    env.onto_residual = onto_residual
    env.square_residual = square_residual
    env.ACC = ACC
    env.squared = squared
    env.square_used = square_used
    env.prefetched = prefetched
    env.halve = halve
    env.w_loaded = w_loaded
    env.lead_vector = lead_vector
    env.lead_counted = lead_counted
    env.counted = counted
    env.turn_rows = turn_rows
    env.tile_full = tile_full
    env.tile_free = tile_free

    def run(stage, *args, **options):
        stage(*args, **options)

    _layer0(nc, io, env, run)
    for l in range(2):
        if l == 1:
            _layer1(nc, io, env, run)
        _memory(nc, io, env, run, l)
        _feed_forward(nc, io, env, run, l)


def _layer0(nc, io, env, run):
    g = env
    X, H, OT, R, Rf, Hf, OTf, PS, PSf, view, count, P_ = g.X, g.H, g.OT, g.R, g.Rf, g.Hf, g.OTf, g.PS, g.PSf, g.view, g.count, P
    MASK, COS, SIN, COL, SM, IDENT = g.MASK, g.COS, g.SIN, g.COL, g.SM, g.IDENT
    dve_own = g.dve_own
    HHL = (g.HH, g.HL)
    VA, VB = view(Rf, 4 * T, 9, 512), view(Rf, 4 * T + 4608, 9, 512)
    STATE = [view(Rf, 4 * T + 9216, 2, 256), view(g.SPARE[:, 0, :], 0, 2, 256)]
    DMASK, QDEC, PAIR = view(MASK[:, :], 0, 4, P), view(MASK[:, :], 512, 2, P), view(MASK[:, :], 768, 256)
    DMASK_S, QDEC_S = MASK[0:S, 1024:1280].rearrange("p (h n) -> p h n", n=S), view(MASK[:, :], 1280, 2, NS)
    RC = MASK[:, 1296:1320]
    SAMPLE_STATE = view(Hf, 4 * T, NB, 2, 256)
    w_in = io["ev_w_in"]

    GB = g.SPARE[:, 0, 512:1024]
    tables = [(COS[:, :], io["ret_cos"]), (SIN[:, :], io["ret_sin"]), (g.ROT[:, :], io["ret_rot"]),
              (MASK[:, 0:1320], io["ret_tables"]), (COL[:, 0:4], io["ret_gn_g"]), (GB, io["mlp_norm_g"].partition_broadcast(P))]

    INV = g.SPARE[:, 1, :]
    ws = [g.columns(w_in[:, 512 * i:512 * (i + 1)], KT, 4) for i in range(5)]
    out = g.columns(io["ev_w_out"], KT, 8)
    run(g.project, ws[1][0], HHL, KT, 4, To(OT, times=INV, rows=VA), then=ws[4], lead=Lead([X[:, k, :] for k in range(KT)], gain=0, inv=INV, arriving=True), loads=tables)
    run(g.project, ws[4][0], HHL, KT, 4, To(OT, func=ACT.Gelu, times=INV, rows=VB), then=ws[0])
    centered, squared, var, rooted, rows = (count(n) for n in ("gate_centered", "gate_squared", "gate_var", "gate_rooted", "gate_rows"))
    V3 = VB.rearrange("p n (g d) -> p (n g) d", d=P)
    V_SQ = [(view(OTf, 4 * T, 32, P), slice(0, 32)), (view(g.CST, 0, 4, P), slice(32, 36))]
    mean, inv = SM[:, 0:36], SM[:, 36:72]

    def center_rows(dve):
        dve.tensor_reduce(mean, V3, AX.X, ALU.add).then_inc(dve_own.sem, 1)
        dve.wait_ge(dve_own.sem, dve_own.next())
        dve.tensor_scalar(mean, mean, 1.0 / P, None, ALU.mult).then_inc(dve_own.sem, 1)
        dve.wait_ge(dve_own.sem, dve_own.next())
        dve.tensor_tensor(V3, V3, mean.unsqueeze(2).to_broadcast([P, 36, P]), ALU.subtract).then_inc(centered.sem, 1)

    def scale_rows(dve):
        dve.wait_ge(squared.sem, squared.at(1))
        for sq, groups in V_SQ:
            last = dve.tensor_reduce(inv[:, groups], sq, AX.X, ALU.add)
        last.then_inc(var.sem, 1)
        dve.wait_ge(rooted.sem, rooted.at(1))
        dve.reciprocal(inv, inv).then_inc(dve_own.sem, 1)
        dve.wait_ge(dve_own.sem, dve_own.next())
        dve.tensor_tensor(V3, V3, inv.unsqueeze(2).to_broadcast([P, 36, P]), ALU.mult).then_inc(dve_own.sem, 1)
        dve.wait_ge(dve_own.sem, dve_own.next())

    def gain_rows(dve):
        dve.tensor_tensor(VB, VB, GB.unsqueeze(1).to_broadcast([P, 9, 512]), ALU.mult).then_inc(rows.sem, 1)

    def root_rows(act):
        act.wait_ge(centered.sem, centered.at(1))
        for sq, groups in V_SQ:
            last = act.activation(sq, V3[:, groups, :], ACT.Square)
        last.then_inc(squared.sem, 1)
        act.wait_ge(var.sem, var.at(1))
        act.activation(inv, inv, ACT.Sqrt, scale=1.0 / P, bias=g.EPSC[:, 0:1]).then_inc(rooted.sem, 1)
    run(g.project, ws[0][0], HHL, KT, 4, To(R, 0, times=INV, rotate=(g.ROT, COS, SIN, OT[:, 0, :])), then=ws[2])
    run(g.project, ws[2][0], HHL, KT, 4, To(OT, 0, func=ACT.Silu, times=INV), then=ws[3], meanwhile=Meanwhile([center_rows, scale_rows, gain_rows], root_rows))
    for c in (centered, squared, var, rooted, rows):
        c.adds(1)
    run(g.project, ws[3][0], HHL, KT, 4, To(OT, 4, func=ACT.Gelu, times=INV), then=out)

    def clear_state():
        run(g.load, [(SAMPLE_STATE[64 * hh:64 * hh + 64, :, pr, 128 * hh:128 * hh + 128],
                      io["state_ret"].rearrange("b (t e) k v -> t e k b v", e=2)[pr, hh])
                     for hh in range(2) for pr in range(2)],
            zero=(SAMPLE_STATE[0:64, :, :, 128:256], SAMPLE_STATE[64:128, :, :, 0:128]))
    clear_state()

    work = [COS, SIN]

    def retention():
        a_ready, a_taken, o_ready, o_out = (count(n) for n in ("ret_scores", "ret_taken", "ret_out", "ret_out_taken"))
        kv_ready, s_ready = count("ret_kv"), count("ret_state")

        def bufs(j):
            w = work[j % 2]
            return view(w[:, :], 0, 4, P), view(w[:, :], 512, 4, 64), view(w[:, :], 768, 2, P)
        with nc.Block() as block:
            @block.tensor
            def _(pe):
                def scores(j):
                    a, m = TOK[j]
                    b = 6 * (j % 2)
                    if j >= 2:
                        pe.wait_ge(a_taken.sem, a_taken.at(j - 1))
                    for h in range(HEADS):
                        pr, r = h // 2, 64 * (h % 2)
                        pe.matmul(PS[0:m, b + h % 2, pr * P:pr * P + m], R[r:r + 64, 2 + pr, a:a + m], R[r:r + 64, pr, a:a + m], start=True, stop=True)
                    for pr in range(2):
                        last = pe.transpose(PS[0:m, 2 + b // 3, pr * P:(pr + 1) * P], R[:, 2 + pr, a:a + m], IDENT[:, :])
                    last.then_inc(a_ready.sem, 1)
                scores(0)
                for j, (a, m) in enumerate(TOK):
                    AT, KD, QD = bufs(j)
                    if j < NBLK:
                        scores(j + 1)
                    pe.wait_ge(a_taken.sem, a_taken.at(j + 1))
                    if j < NBLK:
                        if j:
                            pe.wait_ge(s_ready.sem, s_ready.at(j + 1))
                        for pr in range(2):
                            last = pe.matmul(PS[:, 5, pr * 256:(pr + 1) * 256], KD[:, 2 * pr:2 * pr + 2, :].rearrange("p a b -> p (a b)"),
                                             VA[:, j, pr * 256:(pr + 1) * 256], start=True, stop=True)
                        last.then_inc(kv_ready.sem, 1)
                    if j:
                        pe.wait_ge(o_out.sem, o_out.at(j))
                    for h in range(HEADS):
                        pr, hh = h // 2, h % 2
                        o = PS[:, 3, h * P:h * P + m]
                        pe.matmul(o, VA[0:m, j, h * P:(h + 1) * P], AT[0:m, h, 0:m], start=True, stop=(j == NBLK))
                        if j < NBLK:
                            last = pe.matmul(o, STATE[j % 2][:, pr, hh * P:(hh + 1) * P], QD[:, pr, :], start=False, stop=True)
                        else:
                            for b in range(NB):
                                last = pe.matmul(PS[:, 3, h * P + b * NS:h * P + (b + 1) * NS], SAMPLE_STATE[:, b, pr, hh * P:(hh + 1) * P],
                                                 QD[:, pr, b * NS:(b + 1) * NS], start=False, stop=True, skip_group_check=True)
                    last.then_inc(o_ready.sem, 1)

            @block.vector
            def _(dve):
                dve.memset(STATE[0], 0.0).then_inc(s_ready.sem, 1)

                def operands(j):
                    a, m = TOK[j]
                    b = 6 * (j % 2)
                    AT, KD, QD = bufs(j)
                    dve.wait_ge(a_ready.sem, a_ready.at(j + 1))
                    if j >= 2:
                        dve.wait_ge(o_ready.sem, o_ready.at(j - 1))
                    dm = DMASK if j < NBLK else DMASK_S
                    for hh in range(2):
                        dve.tensor_tensor(AT[0:m, hh:4:2, 0:m], PS[0:m, b + hh, 0:256].rearrange("p (a b) -> p a b", b=P)[:, :, 0:m], dm[0:m, hh:4:2, 0:m], ALU.mult)
                    kc = RC[0:m, 0:4] if j < NBLK else RC[0:m, 4:8]
                    dve.tensor_tensor(KD[0:m, :, :], PS[0:m, 2 + b // 3, 0:256].rearrange("p (a b) -> p a b", b=64), kc.unsqueeze(2).to_broadcast([m, 4, 64]), ALU.mult)
                    if j < NBLK:
                        last = dve.tensor_tensor(QD[:, :, :], R[:, 0:2, a:a + m], QDEC[:, :, :], ALU.mult)
                    else:
                        for pr in range(2):
                            last = dve.tensor_tensor(QD[:, pr, 0:m].rearrange("p (b t) -> p b t", t=NS), R[:, pr, a:a + m].rearrange("p (b t) -> p b t", t=NS),
                                                     QDEC_S[:, pr, :].unsqueeze(1).to_broadcast([P, NB, NS]), ALU.mult)
                    last.then_inc(a_taken.sem, 1)
                operands(0)
                for j in range(NBLK):
                    operands(j + 1)
                    dve.wait_ge(kv_ready.sem, kv_ready.at(j + 1))
                    kv = PS[:, 5, :].rearrange("p (a b) -> p a b", b=256)
                    dve.tensor_tensor(kv, kv, PAIR.unsqueeze(1).to_broadcast([P, 2, 256]), ALU.mult).then_inc(dve_own.sem, 1)
                    dve.wait_ge(dve_own.sem, dve_own.next())
                    for pr in range(2):
                        last = dve.scalar_tensor_tensor(STATE[(j + 1) % 2][:, pr, :], STATE[j % 2][:, pr, :], RC[:, 8 + pr:9 + pr], kv[:, pr, :], ALU.mult, ALU.add)
                    last.then_inc(s_ready.sem, 1)
                    dve.wait_ge(s_ready.sem, s_ready.at(j + 2))

            @block.scalar
            def _(act):
                for j, (a, m) in enumerate(TOK):
                    act.wait_ge(o_ready.sem, o_ready.at(j + 1))
                    act.activation(H[:, 0:4, a:a + m], PS[:, 3, :].rearrange("p (h n) -> p h n", n=P)[:, :, 0:m], ACT.Copy).then_inc(o_out.sem, 1)
        for c, n in ((a_ready, 9), (a_taken, 9), (o_ready, 9), (o_out, 9), (kv_ready, 8), (s_ready, 9)):
            c.adds(n)
    run(retention)

    def new_sample_states():
        spread, made, updated = count("spread"), count("states_made"), count("states_updated")
        VBD = view(Rf, 0, 2, NB, 256)
        KD = view(COS[:, :], 512, 2, P)
        with nc.Block() as block:
            @block.vector
            def _(dve):
                for pr in range(2):
                    dve.tensor_tensor(VBD[0:S, pr], VA[0:S, 8, pr * 256:(pr + 1) * 256].unsqueeze(1).to_broadcast([S, NB, 256]),
                                      RC[0:S, 12:20].unsqueeze(2).to_broadcast([S, NB, 256]), ALU.mult).then_inc(spread.sem, 1)
                for pr in range(2):
                    for c in range(4):
                        dve.wait_ge(made.sem, made.at(pr * 4 + c + 1))
                        s = SAMPLE_STATE[:, 2 * c:2 * c + 2, pr, :]
                        dve.scalar_tensor_tensor(s, s, RC[:, 10 + pr:11 + pr], PS[:, pr * 4 + c, :].rearrange("p (a b) -> p a b", b=256),
                                                 ALU.mult, ALU.add).then_inc(updated.sem, 1)

            @block.tensor
            def _(pe):
                for pr in range(2):
                    pe.wait_ge(spread.sem, spread.at(pr + 1))
                    for c in range(4):
                        pe.matmul(PS[:, pr * 4 + c, :], KD[0:S, pr, :], VBD[0:S, pr, 2 * c:2 * c + 2, :].rearrange("p a b -> p (a b)"), start=True, stop=True).then_inc(made.sem, 1)

            @block.sync
            def _(sp):
                out = io["ret_state_prompt"].rearrange("(t e) k v -> t e k v", e=2)
                for hh in range(2):
                    g.store(sp, out[:, hh].rearrange("t k v -> k t v"), STATE[NBLK % 2][64 * hh:64 * hh + 64, :, hh * P:(hh + 1) * P])
                sp.wait_ge(updated.sem, updated.at(8))
                out = io["ret_state_sample"].rearrange("b (t e) k v -> t e k b v", e=2)
                for pr in range(2):
                    for hh in range(2):
                        g.store(sp, out[pr, hh], SAMPLE_STATE[64 * hh:64 * hh + 64, :, pr, hh * P:(hh + 1) * P])
                sp.wait_ge(g.stored.sem, g.stored.at(g.stores[0]))
        for c, n in ((spread, 2), (made, 8), (updated, 8)):
            c.adds(n)
    run(new_sample_states)
    WT, BT, TRI = view(MASK[:, :], 0, 4, P), view(MASK[:, :], 512, 4, P), view(MASK[:, :], 1024, P)
    WTS = MASK[0:S, 1152:1408].rearrange("p (g t) -> p g t", t=S)
    TRIS, BTS = COS[0:S, 512:576], view(COS[:, :], 576, 4, NS)
    mixed, mix_taken, causal = count("gate_mixed"), count("gate_taken"), count("gate_causal")
    steps = [range(0), range(0, 3), range(3, 6), range(6, 9)]

    def mix_product(pe, t):
        if t == 1:
            pe.wait_ge(causal.sem, causal.at(2))
        for j in steps[t]:
            a, m = TOK[j]
            if j >= 2:
                pe.wait_ge(mix_taken.sem, mix_taken.at(j - 1))
            w = WT if j < NBLK else WTS
            for q in range(4):
                last = pe.matmul(PS[:, 6 + j % 2, q * P:q * P + m], VB[0:m, j, q * P:(q + 1) * P], w[0:m, q, 0:m], start=True, stop=True)
            last.then_inc(mixed.sem, 1)

    def mix_bias(dve, t):
        if t == 0:
            dve.wait_ge(g.loaded.sem, g.loaded.at(16 * 6))
            dve.tensor_tensor(WT, WT, TRI.unsqueeze(1).to_broadcast([P, 4, P]), ALU.mult).then_inc(causal.sem, 1)
            dve.tensor_tensor(WTS, WTS, TRIS.unsqueeze(1).to_broadcast([S, 4, S]), ALU.mult).then_inc(causal.sem, 1)
        for j in steps[t]:
            a, m = TOK[j]
            dve.wait_ge(mixed.sem, mixed.at(j + 1))
            ps, tmp = PS[:, 6 + j % 2, :].rearrange("p (g t) -> p g t", t=P), mix_room(j)
            if j < NBLK:
                last = dve.tensor_tensor(tmp, ps, BT, ALU.add)
            else:
                for q in range(4):
                    last = dve.tensor_tensor(tmp[:, q, 0:S].rearrange("p (b t) -> p b t", t=NS), ps[:, q, 0:S].rearrange("p (b t) -> p b t", t=NS),
                                             BTS[:, q, :].unsqueeze(1).to_broadcast([P, NB, NS]), ALU.add)
            last.then_inc(mix_taken.sem, 1)

    def mix_room(j):
        return view(Rf, j * 512, 4, P)

    def mix_gate(pool, t):
        for j in steps[t]:
            a, m = TOK[j]
            pool.wait_ge(mix_taken.sem, mix_taken.at(j + 1))
            nc.gpsimd.tensor_tensor(OT[:, 4:8, a:a + m], OT[:, 4:8, a:a + m], mix_room(j)[:, :, 0:m], ALU.mult)

    def keep_chunk(sp):
        g.store(sp, io["chunk_v_sample"], VB[0:S, 8, :])
        sp.wait_ge(g.stored.sem, g.stored.at(g.stores[0]))
    run(g.tile_norm, [H[:, h, :] for h in range(4)], [OT[:, h, :] for h in range(4)], g.ONES128[:, :], [COL[:, h:h + 1] for h in range(4)],
        [H[:, 4 + i, :] for i in range(4)], center=True, times=[OT[:, h, :] for h in range(4)],
        loads=[(WT, io["mlp_wT"].rearrange("g s t -> s g t")), (BT, io["mlp_b_s"].partition_broadcast(P)), (TRI, io["tri"]),
               (WTS, io["mlp_wTs"].rearrange("g s t -> s g t")), (TRIS, io["tri_s"]), (BTS, io["mlp_b_s"].partition_broadcast(P)[:, :, 0:NS])],
        beside=(mix_product, mix_bias, mix_gate, keep_chunk))
    mixed.adds(9)
    mix_taken.adds(9)
    causal.adds(2)

    run(g.project, out[0], HHL, KT, 8, To(residual=True, squares=True), then=g.columns(io["mem_w_kv"][0], KT, 8), lead=Lead([OT[:, t, :] for t in range(KT)], reload=io["xT"]),
        loads=_memory_loads(g, io, 0))


def _attend(nc, g, units, scale, room):
    count, PS, view, Hf, SM, dve_own = g.count, g.PS, g.view, g.Hf, g.SM, g.dve_own
    scored, peaked, exped, normed, turned, pt_ready, out_ready, out_taken = (count("att_" + n) for n in (
        "scored", "peaked", "exped", "normed", "turned", "pt_ready", "out_ready", "out_taken"))
    n = len(units)
    outs, k = [], 0
    for u in units:
        k += u.last
        outs.append(k)

    def probs(u):
        return view(room, (u % 2) * 1024, 4, 256) if units[u].G > 1 else view(room, (u % 2) * 1024, 1, 256)

    def turned_probs(u):
        return view(room, 2048 + (u % 2) * 1024, 2, 4, P)

    def stat(u, k):
        return SM[:, (u % 2) * 32 + 4 * k:(u % 2) * 32 + 4 * k + 4]

    def ps_scores(u):
        b = 2 * (u % 2)
        return g.PSf[:, b * 512:b * 512 + 1024].rearrange("p (g w) -> p g w", w=256)
    with nc.Block() as block:
        @block.tensor
        def _(pe):
            def scores(u):
                if u >= 2:
                    pe.wait_ge(exped.sem, exped.at(u - 1))
                units[u].scores(pe, ps_scores(u)).then_inc(scored.sem, 1)

            def turn(u):
                pe.wait_ge(normed.sem, normed.at(u + 1))
                if u >= 1:
                    pe.wait_ge(pt_ready.sem, pt_ready.at(u))
                x = units[u]
                for kt, (a, m) in enumerate(x.keys):
                    for q in range(x.G):
                        last = pe.transpose(PS[0:m, 4 + kt, q * P:q * P + x.rows], probs(u)[0:x.rows, q, a:a + m], g.IDENT[0:x.rows, 0:x.rows])
                last.then_inc(turned.sem, 1)

            def outputs(u):
                pe.wait_ge(pt_ready.sem, pt_ready.at(u + 1))
                x = units[u]
                if x.first and outs[u] - x.last >= 2:
                    pe.wait_ge(out_taken.sem, out_taken.at(outs[u] - x.last - 1))
                x.outputs(pe, turned_probs(u), 6 + x.bank).then_inc(out_ready.sem, 1)
            scores(0)
            scores(1)
            for u in range(n):
                if u + 2 < n:
                    scores(u + 2)
                if u:
                    outputs(u - 1)
                turn(u)
            outputs(n - 1)

        @block.vector
        def _(dve):
            def peak(u):
                x = units[u]
                r = x.rows
                dve.wait_ge(scored.sem, scored.at(u + 1))
                s = ps_scores(u)[0:r, 0:x.G, 0:x.W]
                if x.mask is not None:
                    if u >= 2:
                        dve.wait_ge(turned.sem, turned.at(u - 1))
                    p = probs(u)[0:r, :, 0:x.W]
                    dve.tensor_tensor(p, s, x.mask, ALU.add).then_inc(dve_own.sem, 1)
                    dve.wait_ge(dve_own.sem, dve_own.next())
                    s = p
                mx, nm, df = stat(u, 0)[0:r, 0:x.G], stat(u, 1)[0:r, 0:x.G], stat(u, 2)[0:r, 0:x.G]
                dve.tensor_reduce(mx, s, AX.X, ALU.max).then_inc(dve_own.sem, 1)
                dve.wait_ge(dve_own.sem, dve_own.next())
                if x.sink is None:
                    last = dve.tensor_scalar(nm, mx, -scale, None, ALU.mult)
                else:
                    dve.scalar_tensor_tensor(nm, mx, -scale, x.sink, ALU.mult, ALU.min).then_inc(dve_own.sem, 1)
                    dve.wait_ge(dve_own.sem, dve_own.next())
                    last = dve.tensor_tensor(df, nm, x.sink, ALU.subtract)
                last.then_inc(peaked.sem, 1)

            def norm(u):
                x = units[u]
                r = x.rows
                dve.wait_ge(exped.sem, exped.at(u + 1))
                es, l, inv = (stat(u, k)[0:r, 0:x.G] for k in (3, 4, 5))
                if x.sink is not None:
                    dve.tensor_tensor(l, l, es, ALU.add).then_inc(dve_own.sem, 1)
                    dve.wait_ge(dve_own.sem, dve_own.next())
                dve.reciprocal(inv, l).then_inc(dve_own.sem, 1)
                dve.wait_ge(dve_own.sem, dve_own.next())
                p = probs(u)[0:r, :, 0:x.W]
                dve.tensor_tensor(p, p, inv.unsqueeze(2).to_broadcast([r, x.G, x.W]), ALU.mult).then_inc(normed.sem, 1)
            peak(0)
            for u in range(n):
                if u + 1 < n:
                    peak(u + 1)
                norm(u)

        @block.scalar
        def _(act):
            def place(u):
                if units[u].last:
                    act.wait_ge(out_ready.sem, out_ready.at(u + 1))
                    units[u].place(act, 6 + units[u].bank).then_inc(out_taken.sem, 1)
            for u in range(n + 2):
                if u < n:
                    x = units[u]
                    r = x.rows
                    act.wait_ge(peaked.sem, peaked.at(u + 1))
                    if u >= 2:
                        act.wait_ge(turned.sem, turned.at(u - 1))
                    for q in range(x.G):
                        src = ps_scores(u)[0:r, q, 0:x.W] if x.mask is None else probs(u)[0:r, q, 0:x.W]
                        last = act.activation(probs(u)[0:r, q, 0:x.W], src, ACT.Exp, bias=stat(u, 1)[0:r, q:q + 1], scale=scale,
                                              accum_out=stat(u, 4)[0:r, q:q + 1])
                    if x.sink is not None:
                        last = act.activation(stat(u, 3)[0:r, 0:x.G], stat(u, 2)[0:r, 0:x.G], ACT.Exp)
                    last.then_inc(exped.sem, 1)
                if 1 <= u <= n:
                    v = u - 1
                    act.wait_ge(turned.sem, turned.at(v + 1))
                    if v >= 2:
                        act.wait_ge(out_ready.sem, out_ready.at(v - 1))
                    x = units[v]
                    for kt, (a, m) in enumerate(x.keys):
                        w = x.G * P if x.G > 1 else x.rows
                        last = act.activation(turned_probs(v)[0:m, kt].rearrange("p a b -> p (a b)")[:, 0:w], PS[0:m, 4 + kt, 0:w], ACT.Copy)
                    last.then_inc(pt_ready.sem, 1)
                if u >= 2:
                    place(u - 2)
    for c in (scored, peaked, exped, normed, turned, pt_ready, out_ready):
        c.adds(n)
    out_taken.adds(outs[-1])


class Unit:
    def __init__(self, rows, G, W, keys, scores, outputs, place, bank, first=True, last=True, mask=None, sink=None):
        self.rows, self.G, self.W, self.keys, self.scores, self.outputs, self.place = rows, G, W, keys, scores, outputs, place
        self.bank, self.first, self.last, self.mask, self.sink = bank, first, last, mask, sink


def _memory_loads(g, io, l):
    return [(g.view(g.Rf, 4096, KT, MEM), io["memT"].rearrange("(k p) m -> p k m", p=P)),
            (g.COL[:, 8:9], io["mem_knorm_g"][l]), (g.COL[:, 9:10], io["mem_qnorm_g"][l])]


def _memory(nc, io, env, run, l):
    g = env
    H, OT, R, Rf, Hf, OTf, view, COL = g.H, g.OT, g.R, g.Rf, g.Hf, g.OTf, g.view, g.COL
    MT, MK, MV = view(Rf, 4096, KT, MEM), view(Rf, 0, HEADS, MEM), view(Rf, 1024, 2, 512)
    MTH, MTL = view(g.HHf, 0, KT, MEM), view(g.HLf, 0, KT, MEM)
    Q, OUT = R[:, 4:8, :], R[:, 9:13, :]
    QZ = [view(Rf, at, 8, P) for at in (2048, 3072, 8 * T)] + [view(g.CST, 4096, 8, P)]
    CST = g.CST
    w_kv = io["mem_w_kv"][l]
    cached = [g.count(f"memory_cached{bt}") for bt in range(2)]

    def split_memory():
        halved = g.count("memory_halved")
        with nc.Block() as block:
            @block.scalar
            def _(act):
                act.activation(MTH, MT, ACT.Copy).then_inc(halved.sem, 1)

            @block.vector
            def _(dve):
                dve.wait_ge(halved.sem, halved.at(1))
                dve.tensor_tensor(MTL, MT, MTH.bitcast(F32), ALU.subtract)
        halved.adds(1)
    run(split_memory)

    KV = view(CST, 0, KT, MEM)
    w_q, w_o = g.columns(io["mem_w_q"][l], KT, 4), g.columns(io["mem_w_o"][l], 4, 8)
    run(g.project, g.columns(w_kv, KT)[0], (MTH, MTL), KT, 8, To(KV, 0), spans=((0, MEM),), then=w_q, split_on="vector")
    run(g.turn_rows, [([KV[:, 4 + h, kt * P:(kt + 1) * P] for h in range(4)], [(MV[:, kt, :].rearrange("p (h n) -> p h n", n=P), slice(0, P))]) for kt in range(2)])
    run(g.tile_norm, [KV[:, h, :] for h in range(4)], [MK[:, h, :] for h in range(4)], g.ONES128[:, :], [COL[:, 8:9]] * 4,
        [CST[:, 2048 + i * MEM:2048 + (i + 1) * MEM] for i in range(4)], width=MEM)
    INV = R[:, 12, :]
    run(g.project, w_q[0], (g.HH, g.HL), KT, 4, To(R, 4, times=INV, norm=(g.ONES128, [COL[:, 9:10]] * 4, 4, CST[:, 0:T], CST[:, T:2 * T])), then=w_o, lead=Lead([g.X[:, k, :] for k in range(KT)], gain=KT, inv=INV, summed=True), zero=QZ)

    def prepare_samples():
        with nc.Block() as block:
            @block.sync
            def _(sp):
                for bt in range(2):
                    for dst, src in caches(bt):
                        sp.dma_start(dst, src).then_inc(cached[bt].sem, 16)

            @block.scalar
            def _(act):
                for b in range(NB // 2, NB):
                    for h in range(HEADS):
                        i = (b % 4) * HEADS + h
                        act.activation(QZ[2 * (b // 4) + i // 8][:, i % 8, i * NS:(i + 1) * NS], Q[:, h, SEQ + b * NS:SEQ + (b + 1) * NS], ACT.Copy)

            @block.vector
            def _(dve):
                for b in range(NB // 2):
                    for h in range(HEADS):
                        i = (b % 4) * HEADS + h
                        dve.tensor_copy(QZ[2 * (b // 4) + i // 8][:, i % 8, i * NS:(i + 1) * NS], Q[:, h, SEQ + b * NS:SEQ + (b + 1) * NS])

    def caches(bt):
        b = slice(4 * bt, 4 * bt + 4)
        return [(view(Hf, bt * 8192, 16, MEM), io["cache_mem_kT"][l, b].rearrange("b h d m -> d (b h) m")),
                (view(Hf, bt * 8192 + 4096, 8, 512), io["cache_mem_v"][l, b].rearrange("b (k p) n -> p (b k) n", p=P))]
    run(prepare_samples)

    def prompt_unit(j):
        a = j * P

        def scores(pe, ps):
            for h in range(HEADS):
                last = pe.matmul(ps[:, h, :], Q[:, h, a:a + P], MK[:, h, :], start=True, stop=True)
            return last

        def outputs(pe, pt, bank):
            for h in range(HEADS):
                for kt in range(2):
                    last = pe.matmul(g.PS[:, bank, h * P:(h + 1) * P], MV[:, kt, h * P:(h + 1) * P], pt[:, kt, h, :], start=(kt == 0), stop=(kt == 1))
            return last

        def place(act, bank):
            return act.activation(OUT[:, :, a:a + P], g.PS[:, bank, :].rearrange("p (h n) -> p h n", n=P), ACT.Copy)
        return Unit(P, HEADS, MEM, [(0, P), (P, P)], scores, outputs, place, j % 2)

    def sample_unit(bt, bank):
        KC, VC = view(Hf, bt * 8192, 16, MEM), view(Hf, bt * 8192 + 4096, 8, 512)

        def scores(pe, ps):
            pe.wait_ge(cached[bt].sem, cached[bt].at(32))
            for i in range(16):
                last = pe.matmul(ps[:, 0, :], QZ[2 * bt + i // 8][:, i % 8, :], KC[:, i, :], start=(i == 0), stop=(i == 15))
            return last

        def outputs(pe, pt, bank):
            for i in range(16):
                for kt in range(2):
                    last = pe.matmul(g.PS[:, bank, i * NS:(i + 1) * NS], VC[:, (i // 4) * 2 + kt, (i % 4) * P:(i % 4 + 1) * P],
                                     pt[:, kt, 0, i * NS:(i + 1) * NS], start=(kt == 0), stop=(kt == 1))
            return last

        def place(act, bank):
            a = SEQ + bt * 32
            return act.activation(OUT[:, :, a:a + 32].rearrange("p h (b t) -> p h b t", t=NS),
                                  g.PS[:, bank, 0:P].rearrange("p (b h t) -> p h b t", h=4, t=NS), ACT.Copy)
        return Unit(P, 1, MEM, [(0, P), (P, P)], scores, outputs, place, bank)

    run(_attend, nc, g, [prompt_unit(j) for j in range(NBLK)] + [sample_unit(0, 0), sample_unit(1, 1)], HD_X ** -0.5, CST)
    for c in cached:
        c.adds(32)

    def keep_memory():
        with nc.Block() as block:
            @block.sync
            def _(sp):
                g.store(sp, io["mem_kT_prompt"][l].rearrange("h d m -> d h m"), MK)
                g.store(sp, io["mem_v_prompt"][l].rearrange("(k p) n -> p k n", p=P), MV)
                sp.wait_ge(g.stored.sem, g.stored.at(g.stores[0]))
    run(keep_memory)
    run(g.project, w_o[0], (g.HH, g.HL), 4, 8, To(residual=True, squares=True), then=_gate_and_up(g, io, l, 0, PART), lead=Lead([OUT[:, h, :] for h in range(HEADS)]),
        loads=_conv_loads(g, io, l))


HD_X = 128


def _feed_forward(nc, io, env, run, l):
    g = env
    X, H, OT, R, OTf, PS, view, count, dve_own = g.X, g.H, g.OT, g.R, g.OTf, g.PS, g.view, g.count, g.dve_own
    GW = 2 + SEQ + NB * (2 + NS)
    GATE = [g.CST[:, i * GW:(i + 1) * GW] for i in range(2)]
    CONV = [g.CST[:, 2 * GW + i * T:2 * GW + (i + 1) * T] for i in range(2)]
    at = 2 * GW + 2 * T
    PAST, TAPS = (dst for dst, src in _conv_loads(g, io, l))
    KEEP = view(g.CST, at + FT * 20, FT, 18)
    INV = R[:, 12, :]

    parts, o = [], 0
    for first in range(0, FT, PART):
        tiles = min(PART, FT - first)
        parts.append((first, tiles, o, o + 2 * tiles))
        o += 2 * tiles + 8
    total = o

    def steps():
        ws = []
        for first, tiles, o_hidden, o_down in parts:
            ws.append((_gate_and_up(g, io, l, first, tiles), KT, o_hidden))
            ws.append((g.columns(io["ffn_w_down"][l, first * P:(first + tiles) * P, :], tiles, 8), tiles, o_down))
        last = g.columns(io["od_w_in"][:, 1024:1536], KT, 4) if l == 0 else None
        return [(w, kt, o, (ws[i + 1][0] if i + 1 < len(ws) else last)) for i, (w, kt, o) in enumerate(ws)]

    def feed_forward():
        convolved, gelued, made = count("ff_convolved"), count("ff_gelued"), count("ff_made")
        full, free = g.tile_full, g.tile_free
        lead = Lead([X[:, k, :] for k in range(KT)], gain=2 * KT, inv=INV, summed=True)
        skip = g.ahead[0]
        g.ahead[0] = l == 0
        with nc.Block() as block:
            @block.sync
            def _(sp):
                for (pick, chunks), kt, o, then in steps():
                    g.load_weights(sp, pick, chunks, then, o)
                sp.wait_ge(convolved.sem, convolved.at(FT))
                g.store(sp, io["ffn_conv"][l], KEEP)
                if l == 1:
                    for c in range(KT):
                        sp.wait_ge(free.sem, free.at(parts[-1][3] + c + 1))
                        g.store(sp, io["yT"][c * P:(c + 1) * P, :], X[:, c, :])
                sp.wait_ge(g.stored.sem, g.stored.at(g.stores[0]))

            @block.gpsimd
            def _(pool):
                for i, ((pick, chunks), kt, o, then) in enumerate(steps()):
                    g.split_weights(nc.gpsimd, kt, chunks, skip if i == 0 else True, o)
                    g.split_ahead(pool, chunks, then, o)

            @block.tensor
            def _(pe):
                def tile_halved(k):
                    pe.wait_ge(g.lo_made.sem, g.lo_made.at(k + 1))
                for first, tiles, o_hidden, o_down in parts:
                    def tile_made(k):
                        pe.wait_ge(made.sem, made.at(first + k + 1))
                    g.products(pe, (g.HH, g.HL), KT, 2 * tiles, SPANS, None if first else tile_halved, o=o_hidden, summed_before=not first)
                    g.products(pe, (g.HIDH, g.HIDL), tiles, 8, SPANS, tile_made, o=o_down)

            @block.scalar
            def _(act):
                g.lead_scalar(act, lead)
                with act.Fori(0, FT // 2) as i:
                    for t in range(2):
                        act.wait_ge(convolved.sem, convolved.at(i * 2 + (t + 1)))
                        act.activation(CONV[t], CONV[t], ACT.Gelu).then_inc(gelued.sem, 1)
                if l == 0:
                    g.rounds(act, 8, lambda c, s, i: g.square_residual(act, c, parts[-1][3]))

            def hidden_tile(dve, i, t, first, o):
                G, C = GATE[t], CONV[t]
                f = i * 2 + (first + t)

                def tap(k):
                    return TAPS[:, bass.ds(f, 1), k:k + 1].rearrange("p a b -> p (a b)")
                SG = G[:, 2 + SEQ:GW].rearrange("p (b t) -> p b t", t=2 + NS)
                SC = C[:, SEQ:T].rearrange("p (b t) -> p b t", t=NS)
                dve.tensor_copy(SG[:, :, 0:2], PAST[:, bass.ds(f, 1), :].rearrange("p a (b t) -> p (a b) t", t=2)).then_inc(dve_own.sem, 1)
                dve_own.next()
                dve.wait_ge(full.sem, full.at(i * 4 + (o + 2 * t + 1)))
                dve.tensor_tensor(G[:, 2:770].rearrange("p (r b) -> p r b", r=2), PS[:, 0:2, 0:384],
                                  INV[:, 0:768].rearrange("p (r b) -> p r b", r=2), ALU.mult)
                dve.tensor_tensor(G[:, 770:2 + SEQ], PS[:, 2, 0:256], INV[:, 768:SEQ], ALU.mult)
                dve.tensor_tensor(SG[:, :, 2:2 + NS], PS[:, 2, 256:320].rearrange("p (b t) -> p b t", t=NS),
                                  INV[:, SEQ:T].rearrange("p (b t) -> p b t", t=NS), ALU.mult).then_inc(free.sem, 1)
                dve.wait_ge(free.sem, free.at(i * 4 + (o + 2 * t + 1)))
                dve.wait_ge(dve_own.sem, dve_own.now())
                dve.tensor_scalar(C[:, 0:SEQ], G[:, 0:SEQ], tap(0), tap(3), ALU.mult, ALU.add)
                dve.tensor_scalar(SC, SG[:, :, 0:NS], tap(0), tap(3), ALU.mult, ALU.add).then_inc(dve_own.sem, 1)
                dve.wait_ge(dve_own.sem, dve_own.next())
                dve.scalar_tensor_tensor(C[:, 0:SEQ], G[:, 1:1 + SEQ], tap(1), C[:, 0:SEQ], ALU.mult, ALU.add)
                dve.scalar_tensor_tensor(SC, SG[:, :, 1:1 + NS], tap(1), SC, ALU.mult, ALU.add).then_inc(dve_own.sem, 1)
                dve.wait_ge(dve_own.sem, dve_own.next())
                dve.scalar_tensor_tensor(C[:, 0:SEQ], G[:, 2:2 + SEQ], tap(2), C[:, 0:SEQ], ALU.mult, ALU.add)
                dve.scalar_tensor_tensor(SC, SG[:, :, 2:2 + NS], tap(2), SC, ALU.mult, ALU.add)
                keep = KEEP[:, bass.ds(f, 1), :].rearrange("p a b -> p (a b)")
                dve.tensor_copy(keep[:, 0:2], G[:, SEQ:SEQ + 2])
                dve.tensor_copy(keep[:, 2:18].rearrange("p (b t) -> p b t", t=2), SG[:, :, NS:NS + 2]).then_inc(convolved.sem, 1)
                dve.wait_ge(gelued.sem, gelued.at(i * 2 + (first + t + 1)))
                dve.wait_ge(full.sem, full.at(i * 4 + (o + 2 * t + 2)))
                for ps, a, m, rows in g.pieces(3):
                    c = C[:, a:a + m].rearrange("p (r b) -> p r b", r=rows) if rows > 1 else C[:, a:a + m]
                    last = dve.tensor_tensor(c, ps, c, ALU.mult)
                last.then_inc(free.sem, 1)
                dve.wait_ge(free.sem, free.at(i * 4 + (o + 2 * t + 2)))
                dve.tensor_tensor(C, C, INV, ALU.mult).then_inc(dve_own.sem, 1)
                dve.wait_ge(dve_own.sem, dve_own.next())
                hi, lo = (b[:, bass.ds(i * 2 + t, 1), :].rearrange("p a b -> p (a b)") for b in (g.HIDH, g.HIDL))
                dve.tensor_copy(hi, C).then_inc(dve_own.sem, 1)
                dve.wait_ge(dve_own.sem, dve_own.next())
                dve.tensor_tensor(lo, C, hi.bitcast(F32), ALU.subtract).then_inc(made.sem, 1)

            @block.vector
            def _(dve):
                for G in GATE:
                    dve.memset(G[:, 0:2], 0.0)
                g.lead_vector(dve, lead)
                for first, tiles, o_hidden, o_down in parts:
                    with dve.Fori(0, tiles // 2) as i:
                        dve_own.enter(i, 2 * 5)
                        for t in range(2):
                            hidden_tile(dve, i, t, first, o_hidden)
                    dve_own.leave(tiles // 2)
                    squares = l == 0 and first == parts[-1][0]
                    if squares:
                        dve.memset(g.ACC, 0.0).then_inc(dve_own.sem, 1)
                        dve.wait_ge(dve_own.sem, dve_own.next())
                    g.rounds(dve, 8, lambda c, s, i: g.onto_residual(dve, c, s, o_down, squares))
        for c in (convolved, gelued, made):
            c.adds(FT)
        g.counted(total)
        g.lead_counted(lead)
        if l == 0:
            g.squared.adds(KT)
            g.square_used.adds(KT)
    run(feed_forward)


def _conv_loads(g, io, l):
    at = 2 * (2 + SEQ + NB * (2 + NS)) + 2 * T
    return [(g.view(g.CST, at, FT, NB * 2), io["conv_past"][l]), (g.view(g.CST, at + FT * 16, FT, 4), io["conv_taps"][l])]


def _gate_and_up(g, io, l, first, tiles):
    ws = io["ffn_w_gate"][l], io["ffn_w_up"][l]
    return (lambda c, s, i: (g.chunk(ws[s], KT, i + first), KT)), 2 * tiles


def _layer1(nc, io, env, run):
    g = env
    X, H, OT, R, Rf, Hf, OTf, PS, PSf, view, count = g.X, g.H, g.OT, g.R, g.Rf, g.Hf, g.OTf, g.PS, g.PSf, g.view, g.count
    MASK, COS, SIN, COL, SM, IDENT, SPARE = g.MASK, g.COS, g.SIN, g.COL, g.SM, g.IDENT, g.SPARE
    dve_own = g.dve_own
    HHL = (g.HH, g.HL)
    IC = view(Rf, 8 * T, 9, 512)
    DIAGONAL, LMASK = MASK[:, 0:P], view(MASK[:, :], P, LEVELS, P // 2)
    RESET = SPARE[:, 0, :]
    w_in = io["od_w_in"]
    ONE_HOT = COL[:, 28:36]
    run(g.load, [(g.GAIN[:, :], io["gain1"]), (MASK[:, 0:P + LEVELS * P // 2], io["hgrn_masks"]), (RESET, io["hgrn_reset"]),
                 (COL[:, 12:16], io["hgrn_onorm_g"]), (COL[:, 16:24], io["hgrn_lb_logits"]), (ONE_HOT, io["onehot"])])

    def lower_bound():
        peaked, exped = count("lb_peaked"), count("lb_exped")
        a, b, m = COL[:, 16:20], COL[:, 20:24], COL[:, 24:28]
        with nc.Block() as block:
            @block.vector
            def _(dve):
                dve.tensor_tensor(m, a, b, ALU.max).then_inc(dve_own.sem, 1)
                dve.wait_ge(dve_own.sem, dve_own.next())
                dve.tensor_tensor(a, a, m, ALU.subtract)
                dve.tensor_tensor(b, b, m, ALU.subtract).then_inc(peaked.sem, 1)
                dve.wait_ge(exped.sem, exped.at(1))
                dve.tensor_tensor(m, a, b, ALU.add).then_inc(dve_own.sem, 1)
                dve.wait_ge(dve_own.sem, dve_own.next())
                dve.reciprocal(m, m).then_inc(dve_own.sem, 1)
                dve.wait_ge(dve_own.sem, dve_own.next())
                dve.tensor_tensor(b, b, m, ALU.mult).then_inc(dve_own.sem, 1)
                dve.wait_ge(dve_own.sem, dve_own.next())
                dve.tensor_scalar(a, b, -1.0, 1.0, ALU.mult, ALU.add)

            @block.scalar
            def _(act):
                act.wait_ge(peaked.sem, peaked.at(1))
                act.activation(COL[:, 16:24], COL[:, 16:24], ACT.Exp).then_inc(exped.sem, 1)
        peaked.adds(1)
        exped.adds(1)
    run(lower_bound)
    INV = SPARE[:, 1, :]
    ws = [g.columns(w_in[:, 512 * i:512 * (i + 1)], KT, 4) for i in range(5)]
    run(g.project, ws[2][0], HHL, KT, 4, To(OT, times=INV, rows=IC), then=ws[0], lead=Lead([X[:, k, :] for k in range(KT)], gain=0, inv=INV, spill=True, summed=True))
    run(g.project, ws[0][0], HHL, KT, 4, To(R, 0, func=ACT.Silu, times=INV), then=ws[1])
    run(g.project, ws[1][0], HHL, KT, 4, To(R, 4, func=ACT.Sigmoid, times=INV))

    CHAIN, S0 = view(g.Wf, 3 * T, NBLK, P), view(g.Wf, 3 * T + 1024, NB, P)
    E = [g.Wf[:, i * T:(i + 1) * T] for i in range(3)]
    KTS = g.Wf[:, 2048 + 3 * T:2048 + 3 * T + P]
    KTK, VBD = view(COS[:, :], 0, NBLK, P), view(SIN[:, :], 0, NB, P)
    SUMS, SCORES = [OT[:, 4, :], OT[:, 5, :]], [OT[:, 6, :], OT[:, 7, :]]
    DB = OT[:, 3, :]
    HALF = P // 2

    def right_halves(v, lv):
        return v.rearrange("p (b t) -> p b t", t=2 ** lv)[:, :, 2 ** lv // 2:]

    def left_halves(v, lv):
        return v.rearrange("p (b t) -> p b t", t=2 ** lv)[:, :, 0:2 ** lv // 2]

    def tokens(lv):
        return T if 2 ** lv <= NS else SEQ

    def hgrn(h):
        intra, inter = h < HEADS, h > 0
        q, k, B, A = R[:, h % HEADS, :], R[:, 4 + h % HEADS, :], SUMS[h % 2], SCORES[h % 2]
        M = OT[:, 2, :] if h < 3 else R[:, 0, :]
        logged, forgot, keyed, summed = (count("hg_" + n) for n in ("logged", "forgot", "keyed", "summed"))
        offset, decayed, paired, scored, masked, added = (count("hg_" + n) for n in ("offset", "decayed", "paired", "scored", "masked", "added"))
        lo, bound = COL[:, 16 + h % HEADS:17 + h % HEADS], COL[:, 20 + h % HEADS:21 + h % HEADS]

        def compact(lv):
            at = (lv % 2) * 544
            return M[:, at:at + 512], M[0:S, at + 512:at + 544]

        i = h - 1
        q1, k1, B1, A1 = R[:, i % HEADS, :], R[:, 4 + i % HEADS, :], SUMS[i % 2], SCORES[i % 2]
        v1 = IC[:, :, i % HEADS * P:(i % HEADS + 1) * P]
        start, bexp, dexp, qkd, turned, turned_out, kv, chained, o_ready, o_sample, o_taken, vspread, s_in = (count("hgi_" + n) for n in (
            "start", "exp_b", "exp_rest", "decayed", "turned", "turned_taken", "kv", "chained", "out", "sample_out", "sample_out_taken", "spread", "updated"))
        with nc.Block() as block:
            @block.vector
            def _(dve):
                def forget():
                    dve.tensor_scalar(k, k, lo, bound, ALU.mult, ALU.add).then_inc(dve_own.sem, 1)
                    dve.wait_ge(dve_own.sem, dve_own.next())
                    dve.tensor_scalar(A, k, 2.0 ** -64, None, ALU.max).then_inc(forgot.sem, 1)
                    dve.tensor_scalar(k, k, -1.0, 1.0, ALU.mult, ALU.add).then_inc(keyed.sem, 1)

                def sum_logs():
                    dve.wait_ge(logged.sem, logged.at(1))
                    dve.tensor_tensor_scan(B, RESET, A, 0.0, ALU.mult, ALU.add).then_inc(summed.sem, 1)
                    dve.wait_ge(summed.sem, summed.at(1))
                    dve.wait_ge(keyed.sem, keyed.at(1))

                def mask_diagonal():
                    dve.wait_ge(scored.sem, scored.at(1))
                    dve.tensor_tensor(A[:, 0:SEQ].rearrange("p (j n) -> p j n", n=P), PSf[:, 0:SEQ].rearrange("p (j n) -> p j n", n=P),
                                      DIAGONAL.unsqueeze(1).to_broadcast([P, NBLK, P]), ALU.mult)
                    dve.tensor_tensor(A[0:S, SEQ:T], PS[0:S, 2, 0:S], DIAGONAL[0:S, 0:S], ALU.mult).then_inc(masked.sem, 1)

                def pair(lv):
                    dve.wait_ge(decayed.sem, decayed.at(lv))
                    n, e = tokens(lv), E[lv % 3]
                    dve.tensor_tensor(left_halves(e[:, 0:n], lv), left_halves(e[:, 0:n], lv), left_halves(k[:, 0:n], lv), ALU.mult)
                    dve.tensor_tensor(right_halves(e[:, 0:n], lv), right_halves(e[:, 0:n], lv), right_halves(q[:, 0:n], lv), ALU.mult).then_inc(paired.sem, 1)

                def mask(lv):
                    dve.wait_ge(scored.sem, scored.at(lv + 1))
                    if lv > 2:
                        dve.wait_ge(added.sem, added.at(lv - 2))
                    m, m_s = compact(lv)
                    last = dve.tensor_tensor(m.rearrange("p (j n) -> p j n", n=HALF), PS[:, lv % 2, :].rearrange("p (j n) -> p j n", n=HALF),
                                             LMASK[:, lv - 1, :].unsqueeze(1).to_broadcast([P, NBLK, HALF]), ALU.mult)
                    if tokens(lv) == T:
                        last = dve.tensor_tensor(m_s, PS[0:S, 2 + lv % 2, 0:S // 2], LMASK[0:S, lv - 1, 0:S // 2], ALU.mult)
                    last.then_inc(masked.sem, 1)

                def rests():
                    b3, d3 = (x[:, 0:SEQ].rearrange("p (j n) -> p j n", n=P) for x in (B1, DB))
                    dve.tensor_tensor(d3, b3, b3[:, :, P - 1:P].to_broadcast([P, NBLK, P]), ALU.subtract)
                    b3, d3 = (x[:, SEQ:T].rearrange("p (j n) -> p j n", n=NS) for x in (B1, DB))
                    dve.tensor_tensor(d3, b3, b3[:, :, NS - 1:NS].to_broadcast([P, NB, NS]), ALU.subtract).then_inc(start.sem, 1)
                    dve.tensor_tensor(VBD[0:S], v1[0:S, 8, :].unsqueeze(1).to_broadcast([S, NB, P]),
                                      ONE_HOT[0:S].unsqueeze(2).to_broadcast([S, NB, P]), ALU.mult).then_inc(vspread.sem, 1)

                def decay_operands():
                    dve.wait_ge(bexp.sem, bexp.at(1))
                    dve.tensor_tensor(q1, q1, B1, ALU.mult)
                    dve.wait_ge(dexp.sem, dexp.at(1))
                    dve.tensor_tensor(k1, k1, DB, ALU.mult).then_inc(qkd.sem, 1)

                def chain_states():
                    dve.wait_ge(kv.sem, kv.at(1))
                    for j in range(NBLK):
                        ps = PSf[:, 4 * 512 + j * P:4 * 512 + (j + 1) * P]
                        if j == 0:
                            last = dve.tensor_copy(CHAIN[:, 0, :], ps)
                        else:
                            last = dve.scalar_tensor_tensor(CHAIN[:, j, :], CHAIN[:, j - 1, :], B1[:, (j + 1) * P - 1:(j + 1) * P], ps, ALU.mult, ALU.add)
                        last.then_inc(chained.sem, 1)
                        dve.wait_ge(chained.sem, chained.at(j + 1))

                def sample_states():
                    ends = B1[:, SEQ:T].rearrange("p (b t) -> p b t", t=NS)[:, :, NS - 1:NS].to_broadcast([P, NB, P])
                    dve.wait_ge(o_sample.sem, o_sample.at(1))
                    dve.tensor_tensor(S0, S0, ends, ALU.mult).then_inc(dve_own.sem, 1)
                    dve.wait_ge(dve_own.sem, dve_own.next())
                    dve.wait_ge(kv.sem, kv.at(2))
                    for c in range(2):
                        s = S0[:, 4 * c:4 * c + 4, :]
                        dve.tensor_tensor(s, s, PS[:, 6 + c, :].rearrange("p (b v) -> p b v", v=P), ALU.add).then_inc(s_in.sem, 1)
                if intra:
                    forget()
                    sum_logs()
                if inter:
                    rests()
                if intra:
                    mask_diagonal()
                    pair(1)
                if inter:
                    decay_operands()
                if intra:
                    pair(2)
                    mask(1)
                    pair(3)
                    mask(2)
                if inter:
                    chain_states()
                if intra:
                    pair(4)
                    mask(3)
                    pair(5)
                    mask(4)
                if inter:
                    sample_states()
                if intra:
                    pair(6)
                    mask(5)
                    pair(7)
                    mask(6)
                    mask(7)

            @block.scalar
            def _(act):
                def decay(lv):
                    act.wait_ge(offset.sem, offset.at(lv))
                    e = E[lv % 3][:, 0:tokens(lv)]
                    act.activation(e, e, ACT.Exp).then_inc(decayed.sem, 1)

                def exps():
                    act.wait_ge(start.sem, start.at(1))
                    act.activation(B1, B1, ACT.Exp).then_inc(bexp.sem, 1)
                    act.activation(DB, DB, ACT.Exp, scale=-1.0).then_inc(dexp.sem, 1)

                def take_keys():
                    act.wait_ge(turned.sem, turned.at(1))
                    act.activation(KTK, PSf[:, 4 * 512:4 * 512 + SEQ].rearrange("p (j n) -> p j n", n=P), ACT.Copy)
                    act.activation(KTS[0:S, :], PS[0:S, 6, 0:P], ACT.Copy).then_inc(turned_out.sem, 1)

                def take_sample_output():
                    act.wait_ge(o_sample.sem, o_sample.at(1))
                    act.activation(OT[:, i, SEQ:T], PS[:, 7, 0:S], ACT.Copy).then_inc(o_taken.sem, 1)

                def take_output():
                    act.wait_ge(o_ready.sem, o_ready.at(1))
                    act.activation(OT[:, i, 0:SEQ], PSf[:, 4 * 512:4 * 512 + SEQ], ACT.Copy)
                if intra:
                    act.wait_ge(forgot.sem, forgot.at(1))
                    act.activation(A, A, ACT.Ln).then_inc(logged.sem, 1)
                if intra:
                    decay(1)
                if inter:
                    exps()
                if intra:
                    decay(2)
                    decay(3)
                if inter:
                    take_keys()
                if intra:
                    decay(4)
                if inter:
                    take_sample_output()
                if intra:
                    decay(5)
                if inter:
                    take_output()
                if intra:
                    decay(6)
                    decay(7)

            if intra:
                @block.gpsimd
                def _(pool):
                    def offsets(lv):
                        if lv > 3:
                            pool.wait_ge(scored.sem, scored.at(lv - 2))
                        n, e = tokens(lv), E[lv % 3]
                        w = 2 ** lv
                        mid = B[:, 0:n].rearrange("p (b t) -> p b t", t=w)[:, :, w // 2 - 1:w // 2].to_broadcast([P, n // w, w // 2])
                        nc.gpsimd.tensor_tensor(left_halves(e[:, 0:n], lv), mid, left_halves(B[:, 0:n], lv), ALU.subtract)
                        nc.gpsimd.tensor_tensor(right_halves(e[:, 0:n], lv), right_halves(B[:, 0:n], lv), mid, ALU.subtract).then_inc(offset.sem, 1)

                    def add(lv):
                        pool.wait_ge(masked.sem, masked.at(lv + 1))
                        if lv > 1:
                            pool.wait_ge(added.sem, added.at(lv - 1))
                        m, m_s = compact(lv)
                        w = 2 ** lv
                        a = right_halves(A[:, 0:SEQ], lv)
                        last = nc.gpsimd.tensor_tensor(a, a, m.rearrange("p (b t) -> p b t", t=w // 2), ALU.add)
                        if tokens(lv) == T:
                            a = right_halves(A[0:S, SEQ:T], lv)
                            last = nc.gpsimd.tensor_tensor(a, a, m_s.rearrange("p (b t) -> p b t", t=w // 2), ALU.add)
                        last.then_inc(added.sem, 1)
                    pool.wait_ge(summed.sem, summed.at(1))
                    for lv in range(1, 4):
                        offsets(lv)
                    for lv in range(1, LEVELS + 1):
                        if lv + 3 <= LEVELS:
                            offsets(lv + 3)
                        add(lv)

            @block.tensor
            def _(pe):
                def score_diagonal():
                    pe.wait_ge(keyed.sem, keyed.at(1))
                    for j, (a, m) in enumerate(TOK):
                        last = pe.matmul(PSf[0:m, j * P:j * P + m], k[:, a:a + m], q[:, a:a + m], start=True, stop=True)
                    last.then_inc(scored.sem, 1)

                def score(lv):
                    pe.wait_ge(paired.sem, paired.at(lv))
                    pe.wait_ge(masked.sem, masked.at(max(1, lv - 1)))
                    x, w = E[lv % 3], 2 ** lv
                    for j, (a, m) in enumerate(TOK if tokens(lv) == T else TOK[:-1]):
                        ps = PS[:, lv % 2, j * HALF:(j + 1) * HALF] if j < NBLK else PS[0:S, 2 + lv % 2, 0:S // 2]
                        last = pe.matmul(ps.rearrange("p (b t) -> p b t", t=w // 2), x[:, a:a + m], right_halves(x[:, a:a + m], lv), start=True, stop=True)
                    last.then_inc(scored.sem, 1)

                def turn_keys():
                    pe.wait_ge(qkd.sem, qkd.at(1))
                    for j, (a, m) in enumerate(TOK):
                        last = pe.transpose(PSf[0:m, 4 * 512 + j * P:4 * 512 + (j + 1) * P], k1[:, a:a + m], IDENT[:, :])
                    last.then_inc(turned.sem, 1)

                def keys_values():
                    pe.wait_ge(turned_out.sem, turned_out.at(1))
                    for j in range(NBLK):
                        last = pe.matmul(PSf[:, 4 * 512 + j * P:4 * 512 + (j + 1) * P], KTK[:, j, :], v1[:, j, :], start=True, stop=True)
                    last.then_inc(kv.sem, 1)
                    pe.wait_ge(g.loaded.sem, g.loaded.at(16))
                    pe.matmul(PS[:, 7, 0:S], v1[0:S, 8, :], A1[0:S, SEQ:T], start=True, stop=True)
                    for b in range(NB):
                        last = pe.matmul(PS[:, 7, b * NS:(b + 1) * NS], S0[:, b, :], q1[:, SEQ + b * NS:SEQ + (b + 1) * NS],
                                         start=False, stop=True, skip_group_check=True)
                    last.then_inc(o_sample.sem, 1)

                def sample_keys_values():
                    pe.wait_ge(vspread.sem, vspread.at(1))
                    pe.wait_ge(o_taken.sem, o_taken.at(1))
                    for c in range(2):
                        last = pe.matmul(PS[:, 6 + c, :], KTS[0:S, :], VBD[0:S, 4 * c:4 * c + 4, :].rearrange("p a b -> p (a b)"), start=True, stop=True)
                    last.then_inc(kv.sem, 1)

                def outputs():
                    pe.wait_ge(chained.sem, chained.at(NBLK))
                    for j, (a, m) in enumerate(TOK[:-1]):
                        o = PSf[:, 4 * 512 + j * P:4 * 512 + (j + 1) * P]
                        last = pe.matmul(o, v1[:, j, :], A1[:, a:a + m], start=True, stop=(j == 0))
                        if j:
                            last = pe.matmul(o, CHAIN[:, j - 1, :], q1[:, a:a + m], start=False, stop=True)
                    last.then_inc(o_ready.sem, 1)
                if intra:
                    score_diagonal()
                    score(1)
                if inter:
                    turn_keys()
                if intra:
                    score(2)
                if inter:
                    keys_values()
                if intra:
                    score(3)
                if inter:
                    sample_keys_values()
                if intra:
                    score(4)
                if inter:
                    outputs()
                if intra:
                    score(5)
                    score(6)
                    score(7)

            if inter:
                @block.sync
                def _(sp):
                    sp.dma_start(S0, io["state_hgrn"].rearrange("b h k v -> h k b v")[i]).then_inc(g.loaded.sem, 16)
                    if not intra:
                        for c in range(2):
                            sp.dma_start(g.slot(g.WRAW[c], KT), ws[3][0](c, c, 0)[0]).then_inc(g.w_loaded[c].sem, 16)
                        g.prefetched[0] = 2
                    sp.wait_ge(chained.sem, chained.at(NBLK))
                    g.store(sp, io["hgrn_state_prompt"][i], CHAIN[:, NBLK - 1, :])
                    sp.wait_ge(s_in.sem, s_in.at(2))
                    g.store(sp, io["hgrn_state_sample"].rearrange("b h k v -> h k b v")[i], S0)
                    sp.wait_ge(g.stored.sem, g.stored.at(g.stores[0]))
        if intra:
            for c, n in ((logged, 1), (forgot, 1), (keyed, 1), (summed, 1), (offset, LEVELS), (decayed, LEVELS), (paired, LEVELS),
                         (scored, LEVELS + 1), (masked, LEVELS + 1), (added, LEVELS)):
                c.adds(n)
        if inter:
            g.loaded.adds(16)
            for c, n in ((start, 1), (bexp, 1), (dexp, 1), (qkd, 1), (turned, 1), (turned_out, 1), (kv, 2), (chained, NBLK),
                         (o_ready, 1), (o_sample, 1), (o_taken, 1), (vspread, 1), (s_in, 2)):
                c.adds(n)
    for h in range(HEADS + 1):
        run(hgrn, h)

    KD, V = R[:, 8, :], R[:, 9, :]
    VD = view(Rf, T, 9, 2, P)
    KC, VC = view(Rf, T + 2304, NB, WIN), view(Rf, T + 3328, NB, 2, P)
    QZ, QC = view(Rf, T + 5376, 2, 4, P), view(Rf, T + 6400, 2, P)
    BAND, SMASK = view(MASK[:, :], 0, MEM), view(MASK[:, :], MEM, 2, 192)
    SINK, SINKR = COL[:, 40:48], COL[:, 48:50]
    halves = [(slice(0, 64), 0, slice(0, 64)), (slice(64, 128), 1, slice(64, 128))]
    qk = [OT[:, 4 + i, :] for i in range(4)] + [KD]
    w_qkv, out = g.columns(w_in[:, 2048:2816], KT, 6), g.columns(io["od_w_out"], KT, 8)
    swa_loads = [(g.ROT[:, :], io["swa_rot"]), (COS[:, :], io["swa_cos"]), (SIN[:, :], io["swa_sin"]), (MASK[:, 0:640], io["swa_masks"]),
                 (COL[:, 36:37], io["swa_qnorm_g"]), (COL[:, 37:38], io["swa_knorm_g"]), (SINK, io["swa_sinks"].partition_broadcast(P)),
                 (SINKR, io["swa_sinks_rows"]), (KC, io["cache_swa_kT"].rearrange("b d w -> d b w")),
                 (VC[:, :, 0, 0:64], io["cache_swa_v"][:, :, 0:64].rearrange("b w d -> w b d")),
                 (VC[:, :, 1, 64:128], io["cache_swa_v"][:, :, 64:128].rearrange("b w d -> w b d"))]
    run(g.project, ws[3][0], HHL, KT, 4, To(OT, 4, func=ACT.Silu, times=INV, into=[OT[:, h, :] for h in range(4)], heads=[OT[:, h, :] for h in range(4)],
        norm=(g.ONES128[:, :], [COL[:, 12 + h:13 + h] for h in range(4)], 4, R[:, 10, :], R[:, 11, :])), then=w_qkv, loads=swa_loads,
        zero=(VC[:, :, 0, 64:128], VC[:, :, 1, 0:64], VD[:, :, 0, 64:128], VD[:, :, 1, 0:64], QZ))

    run(g.project, w_qkv[0], HHL, KT, 6, To(tiles=qk + [V], times=INV,
        norm=(g.ONES64, [COL[:, 36:37]] * 4 + [COL[:, 37:38]], 5, R[:, 10, :], R[:, 11, :])), then=out)
    run(g.turn_rows, [([V[:, a:a + m] for a, m in toks], [(VD[0:toks[0][1], j:j + len(toks), 0, 0:64], slice(0, 64)), (VD[0:toks[0][1], j:j + len(toks), 1, 64:128], slice(64, 128))])
                      for toks, j in ((TOK[0:4], 0), (TOK[4:8], 4), (TOK[8:9], 8))])
    run(g.rotate, qk, [H[:, 6, :], H[:, 7, :]])

    def spread_queries():
        with nc.Block() as block:
            @block.vector
            def _(dve):
                dve.tensor_scalar(COL[:, 40:50], COL[:, 40:50], -1.0, None, ALU.mult).then_inc(dve_own.sem, 1)
                dve.wait_ge(dve_own.sem, dve_own.next())
                for bt in range(2):
                    for b in range(4):
                        a = SEQ + (bt * 4 + b) * NS
                        src = OT[:, 4:8, a:a + NS]
                        dve.tensor_copy(QC[:, bt, b * 32:(b + 1) * 32].rearrange("p (i t) -> p i t", t=NS), src)
                        dve.tensor_copy(QZ[:, bt, b, b * 32:(b + 1) * 32].rearrange("p (i t) -> p i t", t=NS), src)
    run(spread_queries)

    def prompt_unit(j, s):
        a = j * P
        first = a if j == 0 else a - P
        W = a + P - first
        r = slice(64 * s, 64 * s + 64)

        def scores(pe, ps):
            for i in range(4):
                last = pe.matmul(ps[:, i, 0:W], OT[r, 4 + i, a:a + P], KD[r, first:first + W], start=True, stop=True)
            return last

        def outputs(pe, pt, bank):
            n = W // P
            for kt in range(n):
                last = pe.matmul(PS[:, bank, :], VD[:, first // P + kt, s, :], pt[:, kt, :, :].rearrange("p a b -> p (a b)"),
                                 start=(s == 0 and kt == 0), stop=(s == 1 and kt == n - 1), skip_group_check=True)
            return last

        def place(act, bank):
            return act.activation(OT[:, 4:8, a:a + P], PS[:, bank, :].rearrange("p (i n) -> p i n", n=P), ACT.Copy)
        mask = BAND[:, MEM - W:MEM].unsqueeze(1).to_broadcast([P, 4, W])
        return Unit(P, 4, W, [(x, P) for x in range(0, W, P)], scores, outputs, place, j % 2, s == 0, s == 1, mask, SINK[:, 4 * s:4 * s + 4])

    def sample_unit(bt, s):
        r = slice(64 * s, 64 * s + 64)

        def scores(pe, ps):
            for b in range(4):
                pe.matmul(ps[:, 0, 0:WIN], QZ[r, bt, b, :], KC[r, bt * 4 + b, :], start=(b == 0), stop=(b == 3))
            return pe.matmul(ps[:, 0, WIN:WIN + S], QC[r, bt, :], KD[r, SEQ:T], start=True, stop=True)

        def outputs(pe, pt, bank):
            pe.matmul(PS[:, bank, 0:P], VD[0:S, 8, s, :], pt[0:S, 1, 0, :], start=(s == 0), stop=True, skip_group_check=True)
            for b in range(4):
                last = pe.matmul(PS[:, bank, b * 32:(b + 1) * 32], VC[:, bt * 4 + b, s, :], pt[:, 0, 0, b * 32:(b + 1) * 32],
                                 start=False, stop=True, skip_group_check=True)
            return last

        def place(act, bank):
            a = SEQ + bt * 32
            return act.activation(OT[:, 4:8, a:a + 32].rearrange("p i (b t) -> p i b t", t=NS),
                                  PS[:, bank, 0:P].rearrange("p (b i t) -> p i b t", i=4, t=NS), ACT.Copy)
        return Unit(P, 1, WIN + S, [(0, WIN), (WIN, S)], scores, outputs, place, bt, s == 0, s == 1,
                    SMASK[:, bt, :].unsqueeze(1), SINKR[:, s:s + 1])
    run(_attend, nc, g, [prompt_unit(j, s) for j in range(NBLK) for s in range(2)] + [sample_unit(bt, s) for bt in range(2) for s in range(2)],
        64 ** -0.5, Hf)

    def keep_window():
        with nc.Block() as block:
            @block.sync
            def _(sp):
                g.store(sp, io["swa_kT_prompt"], KD[:, SEQ - WIN:SEQ])
                g.store(sp, io["swa_kT_sample"][:, :, WIN - NS:WIN], KD[:, SEQ:T].rearrange("p (b t) -> p b t", t=NS))
                g.store(sp, io["swa_kT_sample"][:, :, 0:WIN - NS], KC[:, :, NS:WIN])
                for s in range(2):
                    c = slice(64 * s, 64 * s + 64)
                    g.store(sp, io["swa_v_prompt"][:, c], VD[:, NBLK - 1, s, c])
                    g.store(sp, io["swa_v_sample"][0:WIN - NS, :, c], VC[NS:WIN, :, s, c])
                    g.store(sp, io["swa_v_new"][:, c], VD[0:S, 8, s, c])
                sp.wait_ge(g.stored.sem, g.stored.at(g.stores[0]))
    run(keep_window)
    run(g.project, out[0], HHL, KT, 8, To(residual=True, squares=True), then=g.columns(io["mem_w_kv"][1], KT, 8), lead=Lead([OT[:, t, :] for t in range(KT)], reload=io["yT"]),
        loads=_memory_loads(g, io, 1))


def _rope_tables(heads, dim, rot, theta):
    half = rot // 2
    inv = (np.float32(theta) ** (-np.arange(half, dtype=np.float32) / np.float32(half))).astype(np.float32)
    pos = np.concatenate([np.arange(SEQ), np.tile(2048 + np.arange(NS), NB)]).astype(np.float32)
    ang = inv[:, None] * pos[None, :]
    cos, sin, perm = np.ones((P, T), np.float32), np.zeros((P, T), np.float32), np.zeros((P, P), np.float32)
    for h in range(heads):
        for i in range(half):
            a, b = h * dim + i, h * dim + half + i
            cos[a] = cos[b] = np.cos(ang[i])
            sin[a] = sin[b] = np.sin(ang[i])
            perm[b, a], perm[a, b] = -1.0, 1.0
    return cos, sin, perm


def _retention_tables():
    scale = DK_A ** -0.5
    lg = np.log1p(-np.exp2(-5.0 - np.arange(HEADS)))
    out = np.zeros((P, 1320), np.float32)
    n = np.arange(P)
    rel = n[None, :] - n[:, None]
    for h in range(HEADS):
        out[:, h * P:(h + 1) * P] = np.where(rel >= 0, np.exp(rel * lg[h]), 0) * scale
        same = (n[:S, None] // NS) == (n[None, :S] // NS)
        out[:S, 1024 + h * S:1024 + (h + 1) * S] = np.where(same & (rel[:S, :S] >= 0), np.exp(rel[:S, :S] * lg[h]), 0) * scale
        out[:, 1296 + h] = np.exp((P - 1 - n) * lg[h]) * scale
        out[:, 1300 + h] = np.exp((NS - 1 - n % NS) * lg[h]) * scale
    for pr in range(2):
        for hh in range(2):
            r, h = slice(64 * hh, 64 * hh + 64), 2 * pr + hh
            out[r, 512 + pr * P:512 + (pr + 1) * P] = np.exp((n + 1) * lg[h])
            out[r, 1280 + pr * NS:1280 + (pr + 1) * NS] = np.exp((np.arange(NS) + 1) * lg[h])
            out[r, 768 + hh * P:768 + (hh + 1) * P] = 1
            out[r, 1304 + pr], out[r, 1306 + pr] = np.exp(P * lg[h]), np.exp(NS * lg[h])
    out[:, 1308:1316] = _onehot()
    return out


def _onehot():
    return (np.arange(P)[:, None] // NS == np.arange(NB)[None, :]).astype(np.float32)


def _hgrn_masks():
    n = np.arange(P)
    out = [np.eye(P, dtype=np.float32)]
    for lv in range(1, LEVELS + 1):
        w = 2 ** lv
        same = (n[:, None] // w) == (n[None, :] // w)
        right = np.nonzero(n % w >= w // 2)[0]
        out.append((same & (n[:, None] % w < w // 2))[:, right].astype(np.float32))
    reset = np.ones((P, T), np.float32)
    reset[:, 0:SEQ:P] = 0
    reset[:, SEQ::NS] = 0
    return np.concatenate(out, 1), reset


def _window_masks():
    q, k = np.arange(P)[:, None], np.arange(2 * WIN)[None, :] - WIN
    band = np.where((k <= q) & (q - k < WIN), 0.0, -1e30)
    row = np.arange(P)
    b, t = row // 32, row % NS
    out = [band]
    for bt in range(2):
        key = np.arange(WIN)[None, :] - WIN
        cached = np.where(t[:, None] - key < WIN, 0.0, -1e30)
        s = np.arange(S)[None, :]
        new = np.where((s // NS == bt * 4 + b[:, None]) & (s % NS <= t[:, None]), 0.0, -1e30)
        out += [cached, new]
    return np.concatenate(out, 1).astype(np.float32)


def _columns(v, n):
    return v.reshape(n, P).T


def kernel(**inputs):
    import numpy as _np
    import concourse.bacc as _bacc
    from concourse.bass_utils import run_bass_kernel_spmd as _run

    x = {k: _np.asarray(v) for k, v in inputs.items()}
    cat, c32 = _np.concatenate, _np.ascontiguousarray
    ins = {}
    ins["xT"] = cat([x["x_prompt"][0], x["x_sample"].reshape(S, D)]).T
    ins["ident"] = _np.eye(P, dtype=_np.float32)
    for l in range(2):
        ins[f"gain{l}"] = cat([_columns(x[n][l], KT) for n in ("norm_mix_g", "norm_mem_g", "norm_ffn_g")], 1)
    ins["ret_cos"], ins["ret_sin"], ins["ret_rot"] = _rope_tables(2, 64, 64, 10000.0)
    ins["ret_tables"] = _retention_tables()
    ins["ret_gn_g"] = x["ret_gn_g"][0].T
    ins["ev_w_in"], ins["ev_w_out"] = x["ev_w_in"][0], x["ev_w_out"][0]
    ins["state_ret"] = x["state_ret"][0]
    ins["mlp_wT"] = x["mlp_w_s"][0].transpose(0, 2, 1)
    ins["mlp_wTs"] = _np.tile(x["mlp_w_s"][0].transpose(0, 2, 1)[:, :NS, :NS], (1, NB, NB))
    ins["mlp_b_s"] = x["mlp_b_s"][0]
    ins["mlp_norm_g"] = x["mlp_norm_g"][0].reshape(512)
    n = _np.arange(P)
    ins["tri"] = (n[:, None] <= n[None, :]).astype(_np.float32)
    ins["tri_s"] = ((n[:S, None] <= n[None, :S]) & (n[:S, None] // NS == n[None, :S] // NS)).astype(_np.float32)
    ins["memT"] = x["mem_prompt"][0].T
    for name in ("mem_w_kv", "mem_w_q", "mem_w_o", "ffn_w_gate", "ffn_w_up", "ffn_w_down"):
        ins[name] = x[name]
    ins["mem_knorm_g"], ins["mem_qnorm_g"] = x["mem_knorm_g"][:, :, None], x["mem_qnorm_g"][:, :, None]
    ins["cache_mem_kT"] = x["cache_mem_k"].transpose(0, 1, 3, 4, 2)
    ins["cache_mem_v"] = x["cache_mem_v"].reshape(2, NB, MEM, 512)
    past = x["state_ffn_conv"].reshape(2, NB, 2, FT, P)
    ins["conv_past"] = past.transpose(0, 4, 3, 1, 2).reshape(2, P, FT, NB * 2)
    taps = cat([x["ffn_conv_w"], x["ffn_conv_b"][:, None]], 1).reshape(2, 4, FT, P)
    ins["conv_taps"] = taps.transpose(0, 3, 2, 1)
    order = cat([_np.arange(64) + 64 * h for i in range(4) for h in (i, i + 4)])
    w = x["od_w_in"][0]
    ins["od_w_in"] = cat([w[:, :2048], w[:, 2048:2560][:, order], w[:, 2560:]], 1)
    w = x["od_w_out"][0]
    ins["od_w_out"] = cat([w[:512], w[512:][order]])
    ins["state_hgrn"] = x["state_hgrn"][0]
    ins["hgrn_masks"], ins["hgrn_reset"] = _hgrn_masks()
    ins["hgrn_onorm_g"] = x["hgrn_onorm_g"][0].T
    ins["hgrn_lb_logits"] = cat([_columns(x["hgrn_lb_logits"][l], HEADS) for l in range(2)], 1)
    ins["onehot"] = _onehot()
    ins["swa_cos"], ins["swa_sin"], ins["swa_rot"] = _rope_tables(2, 64, 16, 500000.0)
    ins["swa_masks"] = _window_masks()
    ins["swa_qnorm_g"], ins["swa_knorm_g"] = (_np.tile(x[k][0], 2)[:, None] for k in ("swa_qnorm_g", "swa_knorm_g"))
    ins["swa_sinks"] = x["swa_sinks"][0]
    ins["swa_sinks_rows"] = _np.tile(_np.repeat(x["swa_sinks"][0].reshape(2, 4), NS, 1), (1, 4)).T
    ins["cache_swa_kT"] = x["cache_swa_k"][0].reshape(NB, WIN, P).transpose(0, 2, 1)
    ins["cache_swa_v"] = x["cache_swa_v"][0].reshape(NB, WIN, P)
    outs = {
        "yT": (D, T), "ret_state_prompt": (HEADS, DK_A, P), "hgrn_state_prompt": (HEADS, P, P), "swa_kT_prompt": (P, WIN),
        "swa_v_prompt": (WIN, P), "mem_kT_prompt": (2, HEADS, P, MEM), "mem_v_prompt": (2, MEM, 512), "ffn_conv": (2, P, FT, 18),
        "ret_state_sample": (NB, HEADS, DK_A, P), "chunk_v_sample": (S, 512), "hgrn_state_sample": (NB, HEADS, P, P),
        "swa_kT_sample": (P, NB, WIN), "swa_v_sample": (WIN - NS, NB, P), "swa_v_new": (S, P),
    }
    nc = _bacc.Bacc("TRN2", target_bir_lowering=False, num_devices=1)
    io, arrays = {}, {}
    for name, a in ins.items():
        a = c32(a)
        arrays[f"in_{name}"] = a
        io[name] = nc.dram_tensor(f"in_{name}", a.shape, F32, kind="ExternalInput").ap()
    for name, shape in outs.items():
        io[name] = nc.dram_tensor(f"out_{name}", shape, F32, kind="ExternalOutput").ap()
    build(nc, io)
    r = _run(nc, [arrays], core_ids=[0]).results[0]
    o = {name: r[f"out_{name}"] for name in outs}
    y = o["yT"].T
    conv = o["ffn_conv"].transpose(0, 3, 2, 1).reshape(2, 18, FF)
    swa_v = cat([o["swa_v_sample"].transpose(1, 0, 2), o["swa_v_new"].reshape(NB, NS, P)], 1)
    got = (y[:SEQ][None], y[SEQ:].reshape(NB, NS, D), o["ret_state_prompt"][None, None], o["hgrn_state_prompt"][None, None],
           o["swa_kT_prompt"].T.reshape(1, 1, WIN, 2, 64), o["swa_v_prompt"].reshape(1, 1, WIN, 2, 64),
           o["mem_kT_prompt"].transpose(0, 3, 1, 2)[:, None], o["mem_v_prompt"].reshape(2, 1, MEM, HEADS, P),
           conv[:, 0:2][:, None], o["ret_state_sample"][None], o["chunk_v_sample"].reshape(1, NB, NS, 4, P),
           o["hgrn_state_sample"][None], o["swa_kT_sample"].transpose(1, 2, 0).reshape(1, NB, WIN, 2, 64),
           swa_v.reshape(1, NB, WIN, 2, 64), conv[:, 2:18].reshape(2, NB, 2, FF))
    return tuple(c32(a) for a in got)
```
